# Optimizing a Trainium2 kernel written in Bass

```python
import jax, jax.numpy as jnp
from jax import lax
import numpy as np

D_MODEL = 1024
BATCH = 1
SEQ = 512
DEPTH = 2

N_MEM = 256
XA_HEADS = 4
XA_HD = D_MODEL // XA_HEADS
W_A = D_MODEL
H_A = 8
HD_A = W_A // H_A
CONV_A = 4
C_RG = 8.0
W_B = D_MODEL // 2
POOL_WINDOWS = (2, 4, 8, 16)
G_B = len(POOL_WINDOWS)
HD_B = W_B // G_B
IN_AB = 2 * W_A + W_B
OUT_AB = W_A + W_B
CONV_C = 31
D_FF = 3 * D_MODEL
CONV_F = 3
EPS = 1e-6
N_EVEN = (DEPTH + 1) // 2
N_ODD = DEPTH // 2


def rms_norm(x, g):
    xf = x.astype(jnp.float32)
    y = xf * lax.rsqrt(jnp.mean(xf * xf, axis=-1, keepdims=True) + EPS)
    return (y * g.astype(jnp.float32)).astype(x.dtype)

def layer_norm(x, g, b):
    xf = x.astype(jnp.float32)
    mu = jnp.mean(xf, axis=-1, keepdims=True)
    var = jnp.mean(jnp.square(xf - mu), axis=-1, keepdims=True)
    y = (xf - mu) * lax.rsqrt(var + EPS)
    return (y * g.astype(jnp.float32) + b.astype(jnp.float32)).astype(x.dtype)

def causal_dwconv(x, w, b):
    K, C = w.shape
    y = lax.conv_general_dilated(
        x, w[:, None, :], window_strides=(1,), padding=[(K - 1, 0)],
        dimension_numbers=("NWC", "WIO", "NWC"), feature_group_count=C)
    return y + b

def rg_lru(x, w_gx, b_gx, w_ga, b_ga, lam):
    Bn, S, W = x.shape
    xh = x.reshape(Bn, S, H_A, HD_A)
    gate_x = jax.nn.sigmoid(jnp.einsum('bshi,hij->bshj', xh, w_gx).reshape(Bn, S, W) + b_gx)
    gate_a = jax.nn.sigmoid(jnp.einsum('bshi,hij->bshj', xh, w_ga).reshape(Bn, S, W) + b_ga)
    log_a = -C_RG * gate_a.astype(jnp.float32) * jax.nn.softplus(-lam.astype(jnp.float32))
    a = jnp.exp(log_a)
    mult = jnp.sqrt(-jnp.expm1(2.0 * log_a))
    bx = mult * (gate_x * x).astype(jnp.float32)

    def combine(lhs, rhs):
        a_l, b_l = lhs
        a_r, b_r = rhs
        return a_l * a_r, a_r * b_l + b_r

    _, h = lax.associative_scan(combine, (a, bx), axis=1)
    return h.astype(x.dtype)

def multi_scale_pool(u, w_g, b_g, scale):
    Bn, S, W = u.shape
    uf = u.astype(jnp.float32)
    csum = jnp.cumsum(uf, axis=1)
    t = jnp.arange(1, S + 1, dtype=jnp.float32)[:, None]
    outs = []
    for g, w in enumerate(POOL_WINDOWS):
        sl = slice(g * HD_B, (g + 1) * HD_B)
        cg = csum[..., sl]
        lagged = jnp.pad(cg[:, :S - w], ((0, 0), (w, 0), (0, 0)))
        mean = (cg - lagged) / jnp.minimum(t, float(w))
        outs.append(mean - uf[..., sl])
    p = jnp.stack(outs, axis=2).astype(u.dtype)
    y = jnp.einsum('bsgi,gij->bsgj', p, w_g).reshape(Bn, S, W) + b_g
    return y * scale

def mixer_ab(x, norm, w_in, conv_w, conv_b, w_gx, b_gx, w_ga, b_ga, lam, w_pool, b_pool, pool_scale, w_out):
    z = rms_norm(x, norm) @ w_in
    z_gate = z[..., :W_A]
    z_rec = z[..., W_A:2 * W_A]
    z_pool = z[..., 2 * W_A:]
    xr = causal_dwconv(z_rec, conv_w, conv_b)
    y_a = jax.nn.gelu(z_gate) * rg_lru(xr, w_gx, b_gx, w_ga, b_ga, lam)
    y_b = multi_scale_pool(z_pool, w_pool, b_pool, pool_scale)
    return jnp.concatenate([y_a, y_b], axis=-1) @ w_out

def conformer_conv(x, norm, w1, b1, dw_w, dw_b, ln_g, ln_b, w2, b2):
    h = rms_norm(x, norm) @ w1 + b1
    h = jax.nn.glu(h, axis=-1)
    h = causal_dwconv(h, dw_w, dw_b)
    h = jax.nn.silu(layer_norm(h, ln_g, ln_b))
    return h @ w2 + b2

def cross_attn(x, mem, norm, mem_norm, wq, wk, wv, wo):
    Bn, S, _ = x.shape
    M = mem.shape[1]
    q = (rms_norm(x, norm) @ wq).reshape(Bn, S, XA_HEADS, XA_HD)
    m = rms_norm(mem, mem_norm)
    k = (m @ wk).reshape(Bn, M, XA_HEADS, XA_HD)
    v = (m @ wv).reshape(Bn, M, XA_HEADS, XA_HD)
    s = jnp.einsum('bqhd,bkhd->bhqk', q, k).astype(jnp.float32) * (XA_HD ** -0.5)
    p = jax.nn.softmax(s, axis=-1).astype(x.dtype)
    o = jnp.einsum('bhqk,bkhd->bqhd', p, v).reshape(Bn, S, D_MODEL)
    return o @ wo

def conv_ffn(x, norm, w_up, dw_w, dw_b, w_down):
    h = rms_norm(x, norm) @ w_up
    g = causal_dwconv(h[..., :D_FF], dw_w, dw_b)
    u = h[..., D_FF:]
    return (jax.nn.gelu(g) * u) @ w_down

def first_inputs(seed: int = 0) -> dict:
    key = jax.random.key(seed)
    keys = iter(jax.random.split(key, 48))

    def nrm(shape, scale):
        return jax.random.normal(next(keys), shape, jnp.float32) * scale

    def gain(shape):
        return 1.0 + 0.02 * jax.random.normal(next(keys), shape, jnp.float32)

    L, NE, NO, D = DEPTH, N_EVEN, N_ODD, D_MODEL
    u = jax.random.uniform(next(keys), (NE, W_A), jnp.float32, 0.9, 0.999) ** (1.0 / C_RG)
    lam = jnp.log(u) - jnp.log1p(-u)
    return {
        "x": jax.random.normal(next(keys), (BATCH, SEQ, D), jnp.float32),
        "mem": jax.random.normal(next(keys), (BATCH, N_MEM, D), jnp.float32),
        "ab_norm": gain((NE, D)),
        "ab_w_in": nrm((NE, D, IN_AB), D ** -0.5),
        "a_conv_w": nrm((NE, CONV_A, W_A), CONV_A ** -0.5),
        "a_conv_b": nrm((NE, W_A), 0.01),
        "a_gate_x_w": nrm((NE, H_A, HD_A, HD_A), HD_A ** -0.5),
        "a_gate_x_b": nrm((NE, W_A), 0.01),
        "a_gate_a_w": nrm((NE, H_A, HD_A, HD_A), HD_A ** -0.5),
        "a_gate_a_b": nrm((NE, W_A), 0.01),
        "a_lambda": lam,
        "b_group_w": nrm((NE, G_B, HD_B, HD_B), HD_B ** -0.5),
        "b_group_b": nrm((NE, W_B), 0.01),
        "b_scale": 1.0 + 0.1 * jax.random.normal(next(keys), (NE, W_B), jnp.float32),
        "ab_w_out": nrm((NE, OUT_AB, D), OUT_AB ** -0.5),
        "c_norm": gain((NO, D)),
        "c_w_pw1": nrm((NO, D, 2 * D), D ** -0.5),
        "c_b_pw1": nrm((NO, 2 * D), 0.01),
        "c_dw_w": nrm((NO, CONV_C, D), CONV_C ** -0.5),
        "c_dw_b": nrm((NO, D), 0.01),
        "c_ln_g": gain((NO, D)),
        "c_ln_b": nrm((NO, D), 0.01),
        "c_w_pw2": nrm((NO, D, D), D ** -0.5),
        "c_b_pw2": nrm((NO, D), 0.01),
        "xa_norm": gain((L, D)),
        "xa_mem_norm": gain((L, D)),
        "xa_wq": nrm((L, D, D), D ** -0.5),
        "xa_wk": nrm((L, D, D), D ** -0.5),
        "xa_wv": nrm((L, D, D), D ** -0.5),
        "xa_wo": nrm((L, D, D), D ** -0.5),
        "f_norm": gain((L, D)),
        "f_w_up": nrm((L, D, 2 * D_FF), D ** -0.5),
        "f_dw_w": nrm((L, CONV_F, D_FF), CONV_F ** -0.5),
        "f_dw_b": nrm((L, D_FF), 0.01),
        "f_w_down": nrm((L, D_FF, D), D_FF ** -0.5),
        "final_norm": gain((D,)),
    }

def first_block(x, mem, ab_norm, ab_w_in, a_conv_w, a_conv_b, a_gate_x_w, a_gate_x_b,
              a_gate_a_w, a_gate_a_b, a_lambda, b_group_w, b_group_b, b_scale, ab_w_out,
              c_norm, c_w_pw1, c_b_pw1, c_dw_w, c_dw_b, c_ln_g, c_ln_b, c_w_pw2, c_b_pw2,
              xa_norm, xa_mem_norm, xa_wq, xa_wk, xa_wv, xa_wo,
              f_norm, f_w_up, f_dw_w, f_dw_b, f_w_down, final_norm):
    for layer in range(DEPTH):
        if layer % 2 == 0:
            i = layer // 2
            x = x + mixer_ab(x, ab_norm[i], ab_w_in[i], a_conv_w[i], a_conv_b[i],
                             a_gate_x_w[i], a_gate_x_b[i], a_gate_a_w[i], a_gate_a_b[i],
                             a_lambda[i], b_group_w[i], b_group_b[i], b_scale[i], ab_w_out[i])
        else:
            j = layer // 2
            x = x + conformer_conv(x, c_norm[j], c_w_pw1[j], c_b_pw1[j], c_dw_w[j], c_dw_b[j],
                                   c_ln_g[j], c_ln_b[j], c_w_pw2[j], c_b_pw2[j])
        x = x + cross_attn(x, mem, xa_norm[layer], xa_mem_norm[layer], xa_wq[layer],
                           xa_wk[layer], xa_wv[layer], xa_wo[layer])
        x = x + conv_ffn(x, f_norm[layer], f_w_up[layer], f_dw_w[layer], f_dw_b[layer],
                         f_w_down[layer])
    return rms_norm(x, final_norm)


DEPTH_2 = 1

GRID_W = 64
HEAD_DIM = 64
RWKV_HEADS = 8
RWKV_WIDTH = RWKV_HEADS * HEAD_DIM
DECAY_RANK = 64
ICLR_RANK = 64
GATE_RANK = 128
NA_HEADS = 8
NA_WIDTH = NA_HEADS * HEAD_DIM
NA_MAX_WIN_ROWS = 8
NA_WIN_COLS = 16
N_GROUPS = 4
EXPERTS_PER_GROUP = 8
N_EXPERTS = N_GROUPS * EXPERTS_PER_GROUP
D_EXPERT = 256
TOP_K_IN_GROUP = 2
RMS_EPS = 1e-6
GN_EPS = 64e-5
NEG_INF = -1e30
RWKV_COLS = 3 * RWKV_WIDTH + 2 * DECAY_RANK + 2 * ICLR_RANK + GATE_RANK
NA_COLS = 3 * NA_WIDTH
GATE_COLS = 2 * D_MODEL
IN_COLS = RWKV_COLS + NA_COLS + GATE_COLS
RWKV_SPLITS = (RWKV_WIDTH, 2 * RWKV_WIDTH, 3 * RWKV_WIDTH,
               3 * RWKV_WIDTH + DECAY_RANK, 3 * RWKV_WIDTH + 2 * DECAY_RANK,
               3 * RWKV_WIDTH + 2 * DECAY_RANK + ICLR_RANK,
               3 * RWKV_WIDTH + 2 * DECAY_RANK + 2 * ICLR_RANK)
IN_SPLITS = (RWKV_COLS, RWKV_COLS + NA_WIDTH, RWKV_COLS + 2 * NA_WIDTH, RWKV_COLS + 3 * NA_WIDTH)


def rmsnorm(x, g):
    x32 = x.astype(jnp.float32)
    y = x32 * lax.rsqrt(jnp.mean(x32 * x32, axis=-1, keepdims=True) + RMS_EPS)
    return (y * g).astype(x.dtype)

def centred_token_shift(p, mu_prev, mu_next):
    prev = jnp.pad(p, ((0, 0), (1, 0), (0, 0)))[:, :-1]
    nxt = jnp.pad(p, ((0, 0), (0, 1), (0, 0)))[:, 1:]
    return p + mu_prev * (prev - p) + mu_next * (nxt - p)

def rwkv_log_decay(lora, w0, up):
    w_raw = (w0 + jnp.tanh(lora) @ up).astype(jnp.float32)
    return -jnp.exp(-jax.nn.softplus(-w_raw) - 0.5)

def rwkv_step(S, inp):
    r_t, w_t, k_t, v_t, kk_t, a_t = inp
    sa = jnp.einsum('dbhij,dbhj->dbhi', S, -kk_t)
    S = (S * w_t[..., None, :] + sa[..., :, None] * (kk_t * a_t)[..., None, :]
         + v_t[..., :, None] * k_t[..., None, :])
    y = jnp.einsum('dbhij,dbhj->dbhi', S, r_t)
    return S, y

def rwkv7_bidirectional(p, mu_prev, mu_next, w0_f, w_up_f, w0_b, w_up_b, a0_f, a_up_f,
                        a0_b, a_up_b, g_up, k_k, k_a, r_k, lnx_g, lnx_b):
    B, T, _ = p.shape
    dt = p.dtype
    p = centred_token_shift(p, mu_prev, mu_next)
    r, k, v, wl_f, wl_b, al_f, al_b, gl = jnp.split(p, RWKV_SPLITS, axis=-1)
    lw_f = rwkv_log_decay(wl_f, w0_f, w_up_f)
    lw_b = rwkv_log_decay(wl_b, w0_b, w_up_b)
    a_f = jax.nn.sigmoid(a0_f + al_f @ a_up_f)
    a_b = jax.nn.sigmoid(a0_b + al_b @ a_up_b)
    g = jax.nn.sigmoid(gl) @ g_up

    def heads(t):
        return t.reshape(B, T, RWKV_HEADS, HEAD_DIM).astype(jnp.float32)

    r_h, v_h = heads(r), heads(v)
    kk = heads(k * k_k)
    kk = kk * lax.rsqrt(jnp.sum(kk * kk, axis=-1, keepdims=True) + 1e-12)
    k_f = heads(k * (1.0 + (a_f - 1.0) * k_a))
    k_b = heads(k * (1.0 + (a_b - 1.0) * k_a))
    a_fh, a_bh = heads(a_f), heads(a_b)
    w_fh, w_bh = jnp.exp(heads(lw_f)), jnp.exp(heads(lw_b))

    def both(f, b):
        return jnp.stack([f, jnp.flip(b, axis=1)], axis=0).transpose(2, 0, 1, 3, 4)

    xs = (both(r_h, r_h), both(w_fh, w_bh), both(k_f, k_b), both(v_h, v_h),
          both(kk, kk), both(a_fh, a_bh))
    S0 = jnp.zeros((2, B, RWKV_HEADS, HEAD_DIM, HEAD_DIM), jnp.float32)
    _, ys = lax.scan(rwkv_step, S0, xs)
    y_f = ys[:, 0].transpose(1, 0, 2, 3)
    y_b = jnp.flip(ys[:, 1].transpose(1, 0, 2, 3), axis=1)
    y = y_f + y_b
    mean = jnp.mean(y, axis=-1, keepdims=True)
    var = jnp.mean(jnp.square(y - mean), axis=-1, keepdims=True)
    y = ((y - mean) * lax.rsqrt(var + GN_EPS)).reshape(B, T, RWKV_WIDTH) * lnx_g + lnx_b
    bonus = jnp.sum(r_h * (k_f + k_b) * r_k, axis=-1, keepdims=True) * v_h
    y = (y + bonus.reshape(B, T, RWKV_WIDTH)) * g
    return y.astype(dt)

def neighbourhood_attention_2d(q, k, v, q_gain, k_gain, rpb):
    B, T, _ = q.shape
    dt = q.dtype
    rows = T // GRID_W
    kh = min(NA_MAX_WIN_ROWS, rows)

    def qk_norm(t, g):
        t32 = t.reshape(B, T, NA_HEADS, HEAD_DIM).astype(jnp.float32)
        return t32 * lax.rsqrt(jnp.mean(t32 * t32, axis=-1, keepdims=True) + RMS_EPS) * g

    def grid(t):
        return t.reshape(B, rows, GRID_W, NA_HEADS, HEAD_DIM).transpose(0, 3, 1, 2, 4)

    qg = grid(qk_norm(q, q_gain) * (HEAD_DIM ** -0.5))
    kg = grid(qk_norm(k, k_gain))
    vg = grid(v.reshape(B, T, NA_HEADS, HEAD_DIM).astype(jnp.float32))

    cols = np.arange(GRID_W)
    col_start = np.clip(cols - NA_WIN_COLS // 2, 0, GRID_W - NA_WIN_COLS)
    col_mask = ((cols[None, :] >= col_start[:, None])
                & (cols[None, :] < col_start[:, None] + NA_WIN_COLS))
    col_off = np.clip(cols[None, :] - cols[:, None] + NA_WIN_COLS - 1, 0, 2 * NA_WIN_COLS - 2)

    def row_block(i):
        start = jnp.clip(i - kh // 2, 0, rows - kh)
        k_blk = lax.dynamic_slice_in_dim(kg, start, kh, axis=2)
        v_blk = lax.dynamic_slice_in_dim(vg, start, kh, axis=2)
        q_blk = lax.dynamic_index_in_dim(qg, i, axis=2, keepdims=False)
        s = jnp.einsum('bhqd,bhrkd->bhqrk', q_blk, k_blk)
        row_off = start + jnp.arange(kh) - i + NA_MAX_WIN_ROWS - 1
        bias = rpb.astype(jnp.float32)[:, row_off][:, :, col_off]
        s = s + bias.transpose(0, 2, 1, 3)[None]
        s = jnp.where(col_mask[:, None, :], s, NEG_INF)
        prob = jax.nn.softmax(s, axis=(-2, -1))
        return jnp.einsum('bhqrk,bhrkd->bhqd', prob, v_blk)

    out = lax.map(row_block, jnp.arange(rows))
    out = out.transpose(1, 0, 3, 2, 4).reshape(B, T, NA_WIDTH)
    return out.astype(dt)

def hierarchical_moe(h, w_rg, b_rg, w_re, b_re, w_gate_e, w_up_e, w_down_e):
    B, T, D = h.shape
    ht = h.reshape(B * T, D)
    n_tok = ht.shape[0]
    g_logits = (ht @ w_rg + b_rg).astype(jnp.float32)
    g_sel = jnp.argmax(g_logits, axis=-1)
    p_group = jnp.take_along_axis(jax.nn.softmax(g_logits, axis=-1), g_sel[:, None], axis=-1)
    e_logits = (ht @ w_re + b_re).astype(jnp.float32).reshape(n_tok, N_GROUPS, EXPERTS_PER_GROUP)
    e_in_group = jnp.take_along_axis(e_logits, g_sel[:, None, None], axis=1)[:, 0]
    top_val, top_idx = lax.top_k(e_in_group, TOP_K_IN_GROUP)
    weights = p_group * jax.nn.softmax(top_val, axis=-1)
    expert_id = g_sel[:, None] * EXPERTS_PER_GROUP + top_idx
    combine = jnp.sum(jax.nn.one_hot(expert_id, N_EXPERTS, dtype=jnp.float32) * weights[..., None], axis=1)
    combine = combine.astype(h.dtype)
    y = jnp.zeros_like(ht)
    for e in range(N_EXPERTS):
        he = jax.nn.silu(ht @ w_gate_e[e]) * (ht @ w_up_e[e])
        y = y + combine[:, e:e + 1] * (he @ w_down_e[e])
    return y.reshape(B, T, D)

def second_inputs(seed: int = 0) -> dict:
    key = jax.random.key(seed)
    ks = iter(jax.random.split(key, 40))
    L = DEPTH_2

    def nrm(shape, scale):
        return jax.random.normal(next(ks), shape, jnp.float32) * scale

    def unif(shape, lo, hi):
        return jax.random.uniform(next(ks), shape, jnp.float32, lo, hi)

    return {
        'x': nrm((BATCH, SEQ, D_MODEL), 1.0),
        'norm1_g': 1.0 + nrm((L, D_MODEL), 0.02),
        'w_in': nrm((L, D_MODEL, IN_COLS), D_MODEL ** -0.5),
        'mu_prev': unif((L, RWKV_COLS), 0.0, 0.5),
        'mu_next': unif((L, RWKV_COLS), 0.0, 0.5),
        'w0_f': unif((L, RWKV_WIDTH), -6.0, 1.0),
        'w_up_f': nrm((L, DECAY_RANK, RWKV_WIDTH), DECAY_RANK ** -0.5),
        'w0_b': unif((L, RWKV_WIDTH), -6.0, 1.0),
        'w_up_b': nrm((L, DECAY_RANK, RWKV_WIDTH), DECAY_RANK ** -0.5),
        'a0_f': nrm((L, RWKV_WIDTH), 0.5),
        'a_up_f': nrm((L, ICLR_RANK, RWKV_WIDTH), ICLR_RANK ** -0.5),
        'a0_b': nrm((L, RWKV_WIDTH), 0.5),
        'a_up_b': nrm((L, ICLR_RANK, RWKV_WIDTH), ICLR_RANK ** -0.5),
        'g_up': nrm((L, GATE_RANK, RWKV_WIDTH), GATE_RANK ** -0.5),
        'k_k': 0.85 + nrm((L, RWKV_WIDTH), 0.05),
        'k_a': 1.0 + nrm((L, RWKV_WIDTH), 0.05),
        'r_k': nrm((L, RWKV_HEADS, HEAD_DIM), 0.1),
        'lnx_g': 1.0 + nrm((L, RWKV_WIDTH), 0.02),
        'lnx_b': nrm((L, RWKV_WIDTH), 0.01),
        'q_gain': 1.0 + nrm((L, HEAD_DIM), 0.02),
        'k_gain': 1.0 + nrm((L, HEAD_DIM), 0.02),
        'rpb': nrm((L, NA_HEADS, 2 * NA_MAX_WIN_ROWS - 1, 2 * NA_WIN_COLS - 1), 0.1),
        'b_gate': nrm((L, GATE_COLS), 0.01),
        'w_o_rwkv': nrm((L, RWKV_WIDTH, D_MODEL), RWKV_WIDTH ** -0.5),
        'w_o_na': nrm((L, NA_WIDTH, D_MODEL), NA_WIDTH ** -0.5),
        'w_out': nrm((L, D_MODEL, D_MODEL), D_MODEL ** -0.5),
        'norm2_g': 1.0 + nrm((L, D_MODEL), 0.02),
        'w_router_group': nrm((L, D_MODEL, N_GROUPS), D_MODEL ** -0.5),
        'b_router_group': nrm((L, N_GROUPS), 0.01),
        'w_router_expert': nrm((L, D_MODEL, N_EXPERTS), D_MODEL ** -0.5),
        'b_router_expert': nrm((L, N_EXPERTS), 0.01),
        'w_gate_e': nrm((L, N_EXPERTS, D_MODEL, D_EXPERT), D_MODEL ** -0.5),
        'w_up_e': nrm((L, N_EXPERTS, D_MODEL, D_EXPERT), D_MODEL ** -0.5),
        'w_down_e': nrm((L, N_EXPERTS, D_EXPERT, D_MODEL), D_EXPERT ** -0.5),
    }

def second_block(x, norm1_g, w_in, mu_prev, mu_next, w0_f, w_up_f, w0_b, w_up_b, a0_f, a_up_f,
              a0_b, a_up_b, g_up, k_k, k_a, r_k, lnx_g, lnx_b, q_gain, k_gain, rpb, b_gate,
              w_o_rwkv, w_o_na, w_out, norm2_g, w_router_group, b_router_group,
              w_router_expert, b_router_expert, w_gate_e, w_up_e, w_down_e):
    for l in range(DEPTH_2):
        h = rmsnorm(x, norm1_g[l])
        p = h @ w_in[l]
        p_rwkv, q, k, v, gate_logits = jnp.split(p, IN_SPLITS, axis=-1)
        y_a = rwkv7_bidirectional(p_rwkv, mu_prev[l], mu_next[l], w0_f[l], w_up_f[l], w0_b[l],
                                  w_up_b[l], a0_f[l], a_up_f[l], a0_b[l], a_up_b[l], g_up[l],
                                  k_k[l], k_a[l], r_k[l], lnx_g[l], lnx_b[l]) @ w_o_rwkv[l]
        y_b = neighbourhood_attention_2d(q, k, v, q_gain[l], k_gain[l], rpb[l]) @ w_o_na[l]
        g_a, g_b = jnp.split(jax.nn.sigmoid(gate_logits + b_gate[l]), 2, axis=-1)
        x = x + (g_a * y_a + g_b * y_b) @ w_out[l]
        x = x + hierarchical_moe(rmsnorm(x, norm2_g[l]), w_router_group[l], b_router_group[l],
                                 w_router_expert[l], b_router_expert[l], w_gate_e[l],
                                 w_up_e[l], w_down_e[l])
    return x


def setup_inputs(seed=0):
    out = dict(first_inputs(seed))
    for name, value in second_inputs(seed + 1).items():
        if name != "x":
            out[name + "_2"] = value
    return out


def reference(
    x, mem, ab_norm, ab_w_in, a_conv_w, a_conv_b, a_gate_x_w, a_gate_x_b, a_gate_a_w,
    a_gate_a_b, a_lambda, b_group_w, b_group_b, b_scale, ab_w_out, c_norm, c_w_pw1, c_b_pw1,
    c_dw_w, c_dw_b, c_ln_g, c_ln_b, c_w_pw2, c_b_pw2, xa_norm, xa_mem_norm, xa_wq, xa_wk, xa_wv,
    xa_wo, f_norm, f_w_up, f_dw_w, f_dw_b, f_w_down, final_norm, norm1_g_2, w_in_2, mu_prev_2,
    mu_next_2, w0_f_2, w_up_f_2, w0_b_2, w_up_b_2, a0_f_2, a_up_f_2, a0_b_2, a_up_b_2, g_up_2,
    k_k_2, k_a_2, r_k_2, lnx_g_2, lnx_b_2, q_gain_2, k_gain_2, rpb_2, b_gate_2, w_o_rwkv_2,
    w_o_na_2, w_out_2, norm2_g_2, w_router_group_2, b_router_group_2, w_router_expert_2,
    b_router_expert_2, w_gate_e_2, w_up_e_2, w_down_e_2,
):
    x = first_block(
        x, mem, ab_norm, ab_w_in, a_conv_w, a_conv_b, a_gate_x_w, a_gate_x_b, a_gate_a_w,
        a_gate_a_b, a_lambda, b_group_w, b_group_b, b_scale, ab_w_out, c_norm, c_w_pw1, c_b_pw1,
        c_dw_w, c_dw_b, c_ln_g, c_ln_b, c_w_pw2, c_b_pw2, xa_norm, xa_mem_norm, xa_wq, xa_wk,
        xa_wv, xa_wo, f_norm, f_w_up, f_dw_w, f_dw_b, f_w_down, final_norm,
    )
    return second_block(
        x, norm1_g_2, w_in_2, mu_prev_2, mu_next_2, w0_f_2, w_up_f_2, w0_b_2, w_up_b_2, a0_f_2,
        a_up_f_2, a0_b_2, a_up_b_2, g_up_2, k_k_2, k_a_2, r_k_2, lnx_g_2, lnx_b_2, q_gain_2,
        k_gain_2, rpb_2, b_gate_2, w_o_rwkv_2, w_o_na_2, w_out_2, norm2_g_2, w_router_group_2,
        b_router_group_2, w_router_expert_2, b_router_expert_2, w_gate_e_2, w_up_e_2,
        w_down_e_2,
    )


_drawn_inputs = setup_inputs


def setup_inputs(seed=0):
    import zlib

    import numpy as np

    out = dict(_drawn_inputs(seed))
    spreads = {}
    factors = {'a_gate_x_b': 4.694,
     'a_gate_a_b': 8.0,
     'c_b_pw1': 3.386,
     'c_ln_b': 3.149,
     'xa_norm': 4.07,
     'xa_mem_norm': 2.908,
     'lnx_g_2': 2.937,
     'lnx_b_2': 6.447,
     'q_gain_2': 8.0,
     'k_gain_2': 8.0,
     'rpb_2': 7.654,
     'b_gate_2': 8.0,
     'b_router_group_2': 46.943,
     'b_router_expert_2': 3.135}
    for name, (base, spread) in spreads.items():
        noise = np.random.default_rng([zlib.crc32(name.encode()), seed]).standard_normal(out[name].shape)
        drawn = base * np.exp(spread * noise) if base else spread * noise
        out[name] = __import__('jax').numpy.asarray(drawn.astype(out[name].dtype))
    for name, factor in factors.items():
        out[name] = (out[name] * factor).astype(out[name].dtype)
    return out
```

```python
from contextlib import ExitStack

import numpy as np
import concourse.bass as bass
from concourse import mybir

F32 = mybir.dt.float32
F32R = mybir.dt.float32r
U8 = mybir.dt.uint8
ALU = mybir.AluOpType
ACT = mybir.ActivationFunctionType
AX_X = mybir.AxisListType.X

P = 128
D = 1024
S = 512
KT = D // P
UNIT = 2048
N_MEM = 256
XA_HEADS = 4
XA_HD = D // XA_HEADS
D_FF = 3 * D
DEPTH = 2
CONV_A, CONV_C, CONV_F = 4, 31, 3
POOL_WINDOWS = (2, 4, 8, 16)
EPS = 1e-6
GN_EPS = 64e-5
GRID_W = 64
HEAD = 64
RW = 512
WIN_COLS = 16
N_GROUPS, PER_GROUP = 4, 8
N_EXPERTS = N_GROUPS * PER_GROUP
D_EXPERT = 256
CHUNK = 64
LEVELS = 6
CONV_C_PE = 13



def _vector_names():
    names = [("ab_norm", "ab_norm", 0), ("a_conv_b", "a_conv_b", 0), ("gx_b", "a_gate_x_b", 0),
             ("ga_b", "a_gate_a_b", 0), ("lam", "a_lambda", 0), ("bg_b", "b_group_b", 0),
             ("b_scale", "b_scale", 0), ("c_norm", "c_norm", 0), ("c_b1", "c_b_pw1", 0),
             ("c_dw_b", "c_dw_b", 0), ("c_ln_g", "c_ln_g", 0), ("c_ln_b", "c_ln_b", 0),
             ("c_b2", "c_b_pw2", 0)]
    for l in range(DEPTH):
        names += [(f"xa_norm{l}", "xa_norm", l), (f"xa_mem_norm{l}", "xa_mem_norm", l),
                  (f"f_norm{l}", "f_norm", l), (f"f_dw_b{l}", "f_dw_b", l)]
    names += [("final", "final_norm", None)]
    names += [(n, n + "_2", 0) for n in
              ("norm1_g", "mu_prev", "mu_next", "w0_f", "w0_b", "a0_f", "a0_b", "k_k", "k_a",
               "r_k", "lnx_g", "lnx_b", "b_gate", "norm2_g")]
    return names


_WIDTH = {"bg_b": 512, "b_scale": 512, "c_b1": 2048, "mu_prev": 1920, "mu_next": 1920,
          "w0_f": 512, "w0_b": 512, "a0_f": 512, "a0_b": 512, "k_k": 512, "k_a": 512,
          "r_k": 512, "lnx_g": 512, "lnx_b": 512, "b_gate": 2048, "f_dw_b0": 3072,
          "f_dw_b1": 3072}


def _columns():
    at, n = {}, 0
    for key, _, _ in _vector_names():
        at[key] = n
        n += _WIDTH.get(key, 1024) // P
    for key, taps, width in (("a_conv_w", CONV_A, D), ("c_dw_w", CONV_C, D),
                             ("f_dw_w0", CONV_F, D_FF), ("f_dw_w1", CONV_F, D_FF)):
        at[key] = n
        n += taps * width // P
    for key in ("q_gain", "k_gain"):
        at[key] = n
        n += 1
    return at, n


def _plan():
    plan = [("ab_in", h) for h in range(8)] + [("pool_in", i) for i in range(2)]
    plan += [("ab_out_a", i) for i in range(4)] + [("ab_out_b", i) for i in range(2)]
    for l in range(DEPTH):
        if l == 1:
            plan += [("pw1", i) for i in range(8)] + [("pw2", i) for i in range(4)]
        plan += [(f"wk{l}", i) for i in range(4)] + [(f"wv{l}", i) for i in range(4)]
        plan += [(f"wq{l}", i) for i in range(4)] + [(f"wo{l}", i) for i in range(4)]
        for p in range(3):
            plan += [(f"up{l}", 8 * p + i) for i in range(8)] + [(f"down{l}", 4 * p + i) for i in range(4)]
    plan += [("lora", 0), ("lora", 1)]
    for t in range(4):
        plan += [("rkvg", 2 * t), ("rkvg", 2 * t + 1)]
    plan += [("na_v", i) for i in range(2)] + [("na_qk", i) for i in range(4)]
    for out_w, gate in (("o_rwkv", "gate_a"), ("o_na", "gate_b")):
        for i in range(2):
            plan += [(out_w, i), (gate, 2 * i), (gate, 2 * i + 1)]
    plan += [("w_out2", i) for i in range(4)] + [("router", 0)]
    for b in range(8):
        for e in range(4 * b, 4 * b + 4):
            plan += [("expert", 2 * e), ("expert", 2 * e + 1)]
        plan += [("down_e", 4 * b + i) for i in range(4)]
    return plan


def _consts():
    p = np.arange(P)
    c = {"ident": np.eye(P), "head_ones": (p[:, None] // HEAD == p[None, :] // HEAD)}
    t = np.arange(16)
    for g, w in enumerate(POOL_WINDOWS):
        c[f"pool{g}"] = np.broadcast_to(1.0 / np.minimum(t + 1, w), (P, 16))
    col = np.arange(GRID_W)
    start = np.clip(col - WIN_COLS // 2, 0, GRID_W - WIN_COLS)
    inside = (col[None, :] >= start[:, None]) & (col[None, :] < start[:, None] + WIN_COLS)
    c["na_mask"] = np.where(inside[p % GRID_W], 0.0, -1e30)
    c["eps"] = np.full((P, 1), EPS)
    c["gn_eps"] = np.full((P, 1), GN_EPS)
    c["kk_eps"] = np.full((P, 1), 1e-12)
    c["ones"] = np.ones((P, P))
    c["seg8"] = np.broadcast_to((np.arange(32) % 8 != 0), (P, 32))
    c["seg4"] = np.broadcast_to((np.arange(16) % 4 != 0), (P, 16))
    return {k: np.ascontiguousarray(v, np.float32) for k, v in c.items()}


def _rwkv_consts():
    p = np.arange(P)
    t, s = p[:, None], p[None, :]
    same = t // CHUNK == s // CHUNK
    c = {"ident2": (t % HEAD == np.arange(HEAD)[None, :])}
    c["strict0"], c["incl0"] = same & (t > s), same & (t >= s)
    c["strict1"], c["incl1"] = same & (t < s), same & (t <= s)
    c["reset"] = np.broadcast_to(np.arange(S) % CHUNK != 0, (P, S))
    return {k: np.ascontiguousarray(v, np.float32) for k, v in c.items()}


def _level_masks():
    t, s = np.arange(P)[:, None], np.arange(P)[None, :]
    masks = []
    for l in range(LEVELS):
        half = 1 << l
        block = (t // (2 * half) == s // (2 * half)) & (t // half > s // half)
        masks += [block, block.T]
    return np.ascontiguousarray(np.stack(masks, axis=1).astype(np.float32))


def _places(arrays):
    at, n = {}, 0
    for k, v in arrays.items():
        at[k] = (n, v.shape[1])
        n += v.shape[1]
    return at, n



class Queue:

    def __init__(self, eng, sem):
        self.eng, self.sem, self.count, self.seen = eng, sem, 0, {}

    def wait(self, *tokens):
        for token in tokens:
            if token is None:
                continue
            sem, value = token
            if value > 0 and self.seen.get(sem.name, 0) < value:
                self.eng.wait_ge(sem, value)
                self.seen[sem.name] = value

    def done(self, instruction):
        instruction.then_inc(self.sem, 1)
        self.count += 1
        return (self.sem, self.count)

    def last(self):
        return (self.sem, self.count)


class Loader:

    def __init__(self, queue, sem):
        self.queue, self.sem, self.count = queue, sem, 0

    def load(self, dst, src, *after):
        self.queue.wait(*after)
        self.queue.eng.dma_start(dst, src).then_inc(self.sem, 16)
        self.count += 16
        return (self.sem, self.count)


class Arena:

    def __init__(self, nc, stack):
        self.nc, self.stack = nc, stack

    def sb(self, name, shape, dt=F32):
        return self.stack.enter_context(self.nc.sbuf_tensor(name, shape, dt))


def build(nc, stream, vectors, consts, rconsts, x_in, mem_in, gates_w, group_w, lora_w,
          router_b, bias_na, level_masks, out, x_spill, y_spill):
    with ExitStack() as stack:
        def sb(name, shape, dt=F32):
            return stack.enter_context(nc.sbuf_tensor(name, shape, dt))

        def sem(name):
            return stack.enter_context(nc.semaphore(name))

        pe = Queue(nc.tensor, sem("pe_done"))
        act = Queue(nc.scalar, sem("act_done"))
        dve = Queue(nc.vector, sem("dve_done"))
        pool = Queue(nc.gpsimd, sem("pool_done"))
        sp = Queue(nc.sync, sem("sp_unused"))
        V, A, T, G = dve.eng, act.eng, pe.eng, pool.eng

        x = sb("x", [P, KT, S])
        xg_hi = sb("xg_hi", [P, KT, S], F32R)
        xg_lo = sb("xg_lo", [P, KT, S], F32R)
        RAW, SLOTS = 2, 3
        raw = [sb(f"w_raw{i}", [P, UNIT]) for i in range(RAW)]
        w_hi = [sb(f"w_hi{i}", [P, UNIT], F32R) for i in range(SLOTS)]
        w_lo = [sb(f"w_lo{i}", [P, UNIT], F32R) for i in range(SLOTS)]
        square = sb("square", [P, 2, S])
        rstd = sb("rstd", [P, S])
        root = sb("root", [P, S])
        col, n_vec = _columns()
        vec = sb("vec_sb", [P, n_vec])
        c_at, n_const = _places(_consts())
        cst = sb("const_sb", [P, n_const])
        bank = [stack.enter_context(nc.psum_tensor(f"bank{i}", [P, S], F32)) for i in range(8)]

        def const(name):
            a, n = c_at[name]
            return cst[:, a:a + n]

        def vcol(name, i=0):
            return vec[:, col[name] + i:col[name] + i + 1]

        start = Loader(sp, sem("start_loads"))
        start.load(vec[:, :], vectors)
        start.load(cst[:, :], consts)
        started = start.load(x[:, :, :], x_in)

        plan = _plan()
        raw_load = [Loader(sp, sem(f"w_raw{i}_load")) for i in range(RAW)]
        unit_done = {}
        unit_split = {}
        unit_loaded = {}
        taken = [0]

        def load_unit(n):
            before = unit_split[n - RAW] if n >= RAW else ()
            unit_loaded[n] = raw_load[n % RAW].load(raw[n % RAW][:, :], stream[n], *before)

        def split_unit(n):
            r, hi, lo = raw[n % RAW], w_hi[n % SLOTS], w_lo[n % SLOTS]
            free = unit_done.get(n - SLOTS)
            act.wait(unit_loaded[n], free)
            rounded = act.done(A.activation(hi[:, :], r[:, :], ACT.Copy))
            dve.wait(rounded, free)
            rest = dve.done(V.tensor_tensor(lo[:, :], r[:, :], hi[:, :].bitcast(F32), ALU.subtract))
            unit_split[n] = (rounded, rest)
            if n + RAW < len(plan):
                load_unit(n + RAW)

        def take(name, i=0):
            n = taken[0]
            assert plan[n] == (name, i), (plan[n], name, i)
            taken[0] += 1
            for m in range(n, min(n + SLOTS, len(plan))):
                if m not in unit_split and (m < SLOTS or m - SLOTS in unit_done):
                    split_unit(m)
            return n

        def unit(n, cols):
            return [w[n % SLOTS][:, :].rearrange("p (k c) -> p k c", c=cols) for w in (w_hi, w_lo)]

        for n in range(RAW):
            load_unit(n)

        bank_free = [[None]] * 8
        turn = [0]

        def take_bank():
            b = turn[0]
            turn[0] = (b + 1) % 7
            assert bank_free[b] is not None, "bank still in use"
            pe.wait(*bank_free[b])
            bank_free[b] = None
            return b

        def free_bank(b, *readers):
            bank_free[b] = list(readers)

        def matmul(out_ap, lhsT, rhs, first=True, last=True, **kw):
            return T.matmul(out_ap, lhsT, rhs, start=first, stop=last, skip_group_check=True, **kw)

        def split_matmul(out_ap, l_hi, l_lo, r_hi, r_lo, first, last):
            matmul(out_ap, l_hi, r_hi, first, False)
            matmul(out_ap, l_hi, r_lo, False, False)
            return matmul(out_ap, l_lo, r_hi, False, last)

        class Acts:

            def __init__(self, hi, lo, tiles):
                self.hi, self.lo, self.ready = hi, lo, [()] * tiles

        xg = Acts(xg_hi, xg_lo, KT)

        def project(n, cols, c, acts, tiles, b, width=S, first=True, last=True, k0=0):
            hi, lo = unit(n, cols)
            pe.wait(*unit_split[n])
            for i, k in enumerate(tiles):
                pe.wait(*acts.ready[k])
                mm = split_matmul(bank[b][:, 0:width], hi[:, i, c * P:(c + 1) * P],
                                  lo[:, i, c * P:(c + 1) * P], acts.hi[:, k, :], acts.lo[:, k, :],
                                  first and i == 0, last and i == len(tiles) - 1)
            token = pe.done(mm)
            unit_done[n] = token
            return token

        def split_act(acts, k, value, *after):
            act.wait(*after)
            hi = act.done(A.activation(acts.hi[:, k, :], value, ACT.Copy))
            dve.wait(hi, *after)
            lo = dve.done(V.tensor_tensor(acts.lo[:, k, :], value, acts.hi[:, k, :].bitcast(F32), ALU.subtract))
            acts.ready[k] = (hi, lo)
            return hi, lo

        square_read = [None, None]
        norm_state = {}

        def norm_tile(j, gain, x_ready, mean_only=False):
            xg_free = norm_state["xg_free"]
            act.wait(x_ready, xg_free)
            if gain is not None:
                hi = act.done(A.activation(xg_hi[:, j, :], x[:, j, :], ACT.Identity, scale=vcol(gain, j)))
            act.wait(square_read[j % 2])
            sq = act.done(A.activation(square[:, j % 2, :], x[:, j, :], ACT.Square))
            if gain is not None:
                dve.wait(hi, x_ready, xg_free)
                lo = dve.done(V.scalar_tensor_tensor(out=xg_lo[:, j, :], in0=x[:, j, :], scalar=vcol(gain, j),
                                                     in1=xg_hi[:, j, :].bitcast(F32), op0=ALU.mult,
                                                     op1=ALU.subtract))
                xg.ready[j] = (hi, lo)
            norm_state["todo"].append((j, sq))

        def norm_sums(keep=0):
            while len(norm_state["todo"]) > keep:
                j, sq = norm_state["todo"].pop(0)
                pe.wait(sq, started)
                if j == 0:
                    pe.wait(*bank_free[7])
                square_read[j % 2] = pe.done(matmul(bank[7][:, :], const("ones"), square[:, j % 2, :],
                                                    j == 0, j == KT - 1))

        def norm_begin():
            norm_state["xg_free"] = pe.last()
            norm_state["todo"] = []

        def norm_end():
            norm_sums()
            act.wait(square_read[(KT - 1) % 2], norm_state.get("rstd_read"))
            rooted = act.done(A.activation(root[:, :], bank[7][:, :], ACT.Sqrt, scale=1.0 / D, bias=const("eps")))
            bank_free[7] = [rooted]
            dve.wait(rooted)
            norm_state["rstd"] = dve.done(V.reciprocal(rstd[:, :], root[:, :]))
            norm_state["rstd_read"] = None
            return norm_state["rstd"]

        def add_to_x(j, b, mm, bias=None):
            dve.wait(mm)
            if bias is None:
                token = dve.done(V.tensor_tensor(x[:, j, :], bank[b][:, :], x[:, j, :], ALU.add))
            else:
                token = dve.done(V.scalar_tensor_tensor(out=x[:, j, :], in0=bank[b][:, :], scalar=bias,
                                                        in1=x[:, j, :], op0=ALU.add, op1=ALU.add))
            free_bank(b, token)
            return token

        def phase_wait():
            ends = [pe.last(), act.last(), dve.last()]
            for q in (act, dve, pe, pool):
                q.wait(*ends)
            return ends

        def scaled_by_rstd(dst, b, mm, *after):
            dve.wait(mm, norm_state["rstd"], *after)
            token = dve.done(V.tensor_tensor(dst, bank[b][:, :], rstd[:, :], ALU.mult))
            free_bank(b, token)
            return token

        def stt(out_ap, in0, scalar, in1, op0, op1, *after):
            dve.wait(*after)
            return dve.done(V.scalar_tensor_tensor(out=out_ap, in0=in0, scalar=scalar, in1=in1, op0=op0, op1=op1))

        def tt(out_ap, a, b_ap, op, *after):
            dve.wait(*after)
            return dve.done(V.tensor_tensor(out_ap, a, b_ap, op))

        def ts(out_ap, a, s1, s2, op0, op1, *after):
            dve.wait(*after)
            if s2 is None:
                return dve.done(V.tensor_scalar(out_ap, a, s1, None, op0))
            return dve.done(V.tensor_scalar(out_ap, a, s1, s2, op0, op1))

        def activate(out_ap, a, func, *after, **kw):
            act.wait(*after)
            return act.done(A.activation(out_ap, a, func, **kw))

        def copy(engine, out_ap, a, *after):
            engine.wait(*after)
            if engine is act:
                return act.done(A.activation(out_ap, a, ACT.Copy))
            return engine.done(engine.eng.tensor_copy(out_ap, a))

        def causal_taps(dst, src, weight, taps, ready):
            k_last = taps[0]
            for k in taps[1]:
                s = k_last - k
                ready = stt(dst[:, s:], src[:, 0:S - s], weight(k), dst[:, s:], ALU.mult, ALU.add, ready)
            return ready

        def out_projection(names, acts, tiles_of, hook=None, bias=None):
            for name, n_units, cols in names:
                for i in range(n_units):
                    n = take(name, i)
                    for c in range(cols // P):
                        j = i * cols // P + c
                        b = take_bank()
                        mm = project(n, cols, c, acts, tiles_of[name], b)
                        token = add_to_x(j, b, mm, bias(j) if bias and name == names[-1][0] else None)
                        if hook and name == names[-1][0]:
                            norm_sums(0)
                            hook(j, token)

        def next_norm(gain):
            def hook(j, token):
                if j == 0:
                    norm_begin_late()
                norm_tile(j, gain, token)
            return hook

        def norm_begin_late():
            norm_state["xg_free"] = norm_state["xg_last"]
            norm_state["todo"] = []

        def mixer():
            for q in (act, dve, pe, pool):
                q.wait(started)
            norm_begin()
            for j in range(KT):
                norm_tile(j, "ab_norm", started)
                norm_sums(1)
            norm_end()

            with ExitStack() as ph:
                ar = Arena(nc, ph)
                y_hi, y_lo = ar.sb("ab_y_hi", [P, KT, S], F32R), ar.sb("ab_y_lo", [P, KT, S], F32R)
                xr = ar.sb("ab_xr", [P, 2, S])
                zr = ar.sb("ab_zr", [P, 2, S])
                gated = ar.sb("ab_gated", [P, 4, S])
                ga = ar.sb("ab_ga", [P, 4, S])
                gate = ar.sb("ab_gate", [P, 4, S])
                tmp = [ar.sb(f"ab_tmp{i}", [P, S]) for i in range(3)]
                gw = ar.sb("ab_gate_w", [P, 2, 2, P])
                sp8 = ar.sb("ab_decay", [P, 4 * KT])
                pool_w = ar.sb("ab_group_w", [P, 4, P])
                y = Acts(y_hi, y_lo, KT)
                gw_load = [Loader(sp, sem(f"ab_gate_w{i}")) for i in range(2)]
                group_loaded = Loader(sp, sem("ab_group_w_load")).load(pool_w[:, :, :], group_w)

                lam = vec[:, col["lam"]:col["lam"] + KT]
                e_, n_, s_, q_ = [sp8[:, i * KT:(i + 1) * KT] for i in range(4)]
                t0 = ts(n_, lam, -1.0, None, ALU.mult, None)
                t1 = tt(s_, lam, n_, ALU.max, t0)
                t2 = activate(e_, s_, ACT.Exp, t1, scale=-1.0)
                t3 = ts(s_, e_, 2.0, None, ALU.add, None, t2)
                dve.wait(t3)
                t3 = dve.done(V.reciprocal(q_, s_))
                t3 = tt(s_, e_, q_, ALU.mult, t3)
                t3 = tt(q_, s_, s_, ALU.mult, t3)
                t4 = ts(e_, q_, 1.0 / 17, 1.0 / 15, ALU.mult, ALU.add, t3)
                for k in (13, 11, 9, 7, 5, 3, 1):
                    t4 = tt(e_, e_, q_, ALU.mult, t4)
                    t4 = ts(e_, e_, 1.0 / k, None, ALU.add, None, t4)
                t4 = tt(e_, e_, s_, ALU.mult, t4)
                t5 = ts(n_, n_, 0.0, None, ALU.max, None)
                t4 = stt(e_, e_, 2.0, n_, ALU.mult, ALU.add, t4, t5)
                c_pos = ts(s_, e_, 8.0, None, ALU.mult, None, t4)
                c_neg = ts(q_, e_, -8.0, None, ALU.mult, None, t4)
                decay_pos, decay_neg = s_, q_

                gate_w_read = [None, None]
                gated_free = [None] * 4
                xr_read = [None, None]
                for half in range(2):
                    gate_ready, gated_ready, ga_ready = [None] * 4, [None] * 4, [None] * 4
                    for h4 in range(4):
                        h = 4 * half + h4
                        i = h % 2
                        gw_loaded = gw_load[i].load(gw[:, i, :, :], gates_w[:, h, :, :], gate_w_read[i])
                        n = take("ab_in", h)
                        b_rec = take_bank()
                        mm = project(n, 2 * P, 1, xg, range(KT), b_rec)
                        zr_ready = scaled_by_rstd(zr[:, i, :], b_rec, mm)
                        b_gate = take_bank()
                        mm = project(n, 2 * P, 0, xg, range(KT), b_gate)
                        w = lambda k, h=h: vcol("a_conv_w", CONV_A * h + k)
                        ready = activate(xr[:, i, :], zr[:, i, :], ACT.Identity, zr_ready, xr_read[i],
                                         scale=w(CONV_A - 1), bias=vcol("a_conv_b", h))
                        ready = causal_taps(xr[:, i, :], zr[:, i, :], w, (CONV_A - 1, range(CONV_A - 1)), ready)
                        gate_ready[h4] = scaled_by_rstd(gate[:, h4, :], b_gate, mm, gated_free[h4])
                        pe.wait(gw_loaded, ready)
                        b_gx = take_bank()
                        mm_gx = pe.done(matmul(bank[b_gx][:, :], gw[:, i, 0, :], xr[:, i, :]))
                        b_ga = take_bank()
                        mm_ga = pe.done(matmul(bank[b_ga][:, :], gw[:, i, 1, :], xr[:, i, :]))
                        gate_w_read[i] = mm_ga
                        gx = activate(gated[:, h4, :], bank[b_gx][:, :], ACT.Sigmoid, mm_gx, gated_free[h4],
                                      bias=vcol("gx_b", h))
                        free_bank(b_gx, gx)
                        ga_ready[h4] = activate(ga[:, h4, :], bank[b_ga][:, :], ACT.Sigmoid, mm_ga, bias=vcol("ga_b", h))
                        free_bank(b_ga, ga_ready[h4])
                        gated_ready[h4] = tt(gated[:, h4, :], gated[:, h4, :], xr[:, i, :], ALU.mult, gx, ready)
                        xr_read[i] = gated_ready[h4]
                    for h4 in range(4):
                        h = 4 * half + h4
                        th = activate(tmp[0][:, :], ga[:, h4, :], ACT.Tanh, ga_ready[h4], dve.last(), c_pos, c_neg,
                                      scale=decay_pos[:, h:h + 1])
                        a_ready = activate(ga[:, h4, :], ga[:, h4, :], ACT.Exp, th, scale=decay_neg[:, h:h + 1])
                        m = tt(tmp[1][:, :], ga[:, h4, :], ga[:, h4, :], ALU.mult, a_ready)
                        m = stt(tmp[1][:, :], tmp[1][:, :], 1.0, tmp[0][:, :], ALU.add, ALU.mult, m)
                        r = activate(tmp[2][:, :], tmp[1][:, :], ACT.Sqrt, m)
                        bx = tt(gated[:, h4, :], gated[:, h4, :], tmp[2][:, :], ALU.mult, r, gated_ready[h4])
                        dve.wait(bx)
                        scan = dve.done(V.tensor_tensor_scan(tmp[1][:, :], ga[:, h4, :], gated[:, h4, :], 0.0,
                                                             ALU.mult, ALU.add))
                        ge = activate(gate[:, h4, :], gate[:, h4, :], ACT.Gelu_apprx_tanh, gate_ready[h4])
                        ya = tt(gate[:, h4, :], gate[:, h4, :], tmp[1][:, :], ALU.mult, ge, scan)
                        hi, lo = split_act(y, h, gate[:, h4, :], ya)
                        gated_free[h4] = lo
                y_b = Acts(y_hi, y_lo, KT)
                a_done = None
                pooled = []
                u_sb, s_sb = ga, gated
                for i in range(2):
                    n = take("pool_in", i)
                    for c in range(2):
                        g = 2 * i + c
                        b = take_bank()
                        mm = project(n, 2 * P, c, xg, range(KT), b)
                        norm_state["xg_last"] = mm
                        u = scaled_by_rstd(u_sb[:, g, :], b, mm, act.last())
                        src, ready = u_sb[:, g, :], u
                        scratch = [s_sb[:, g, :], tmp[0][:, :]] if g % 2 else [s_sb[:, g, :], tmp[1][:, :]]
                        steps = g + 1
                        for st in range(steps):
                            dst = scratch[(steps - 1 - st) % 2]
                            sh = 1 << st
                            ready = tt(dst[:, sh:], src[:, sh:], src[:, 0:S - sh], ALU.add, ready)
                            ready = copy(dve, dst[:, 0:sh], src[:, 0:sh], ready)
                            src = dst
                        w_ = POOL_WINDOWS[g]
                        fix = tt(tmp[2][:, 0:16], src[:, 0:16], const(f"pool{g}"), ALU.mult, ready)
                        ready = stt(src, src, 1.0 / w_, u_sb[:, g, :], ALU.mult, ALU.subtract, fix)
                        ready = tt(src[:, 0:16], tmp[2][:, 0:16], u_sb[:, g, 0:16], ALU.subtract, ready)
                        pe.wait(group_loaded, ready)
                        b = take_bank()
                        mm = pe.done(matmul(bank[b][:, :], pool_w[:, g, :], src))
                        ready = ts(u_sb[:, g, :], bank[b][:, :], vcol("bg_b", g), vcol("b_scale", g), ALU.add,
                                   ALU.mult, mm)
                        free_bank(b, ready)
                        pooled.append(ready)
                for i in range(4):
                    n = take("ab_out_a", i)
                    for c in range(2):
                        b = take_bank()
                        mm = project(n, 2 * P, c, y, range(KT), b)
                        add_to_x(2 * i + c, b, mm)
                y_a_read = pe.last()
                for g in range(4):
                    act.wait(y_a_read)
                    dve.wait(y_a_read)
                    split_act(y, g, u_sb[:, g, :], pooled[g])
                out_projection([("ab_out_b", 2, S)], y, {"ab_out_b": range(4)}, next_norm("xa_norm0"))
                norm_end()

        def cross_attention(l):
            phase_wait()
            with ExitStack() as ph:
                ar = Arena(nc, ph)
                o_hi, o_lo = ar.sb(f"xa{l}_o_hi", [P, KT, S], F32R), ar.sb(f"xa{l}_o_lo", [P, KT, S], F32R)
                o = Acts(o_hi, o_lo, KT)
                kT = ar.sb(f"xa{l}_k", [P, KT, N_MEM])
                v = ar.sb(f"xa{l}_v", [P, 2, D])
                with ExitStack() as inner:
                    ar2 = Arena(nc, inner)
                    mem = ar2.sb(f"xa{l}_mem", [P, 2, N_MEM])
                    m_hi = ar2.sb(f"xa{l}_m_hi", [P, KT, N_MEM], F32R)
                    m_lo = ar2.sb(f"xa{l}_m_lo", [P, KT, N_MEM], F32R)
                    m_rstd = ar2.sb(f"xa{l}_m_rstd", [P, N_MEM])
                    m_col = ar2.sb(f"xa{l}_m_rstd_col", [P, 2])
                    m = Acts(m_hi, m_lo, KT)
                    mem_load = [Loader(sp, sem(f"xa{l}_mem_load{i}")) for i in range(2)]
                    b_sum = take_bank()
                    mem_read = [(pe.last(), act.last(), dve.last())] * 2
                    for k in range(KT):
                        i = k % 2
                        loaded = mem_load[i].load(mem[:, i, :], mem_in[:, k, :], *mem_read[i])
                        hi = activate(m_hi[:, k, :], mem[:, i, :], ACT.Identity, loaded,
                                      scale=vcol(f"xa_mem_norm{l}", k))
                        lo = stt(m_lo[:, k, :], mem[:, i, :], vcol(f"xa_mem_norm{l}", k),
                                 m_hi[:, k, :].bitcast(F32), ALU.mult, ALU.subtract, hi)
                        m.ready[k] = (hi, lo)
                        sq = activate(square[:, i, 0:N_MEM], mem[:, i, :], ACT.Square, square_read[i])
                        mem_read[i] = (sq, lo)
                        pe.wait(sq)
                        square_read[i] = pe.done(matmul(bank[b_sum][:, 0:N_MEM], const("ones"),
                                                        square[:, i, 0:N_MEM], k == 0, k == KT - 1))
                    r = activate(m_rstd[:, :], bank[b_sum][:, 0:N_MEM], ACT.Sqrt, square_read[1],
                                 scale=1.0 / D, bias=const("eps"))
                    free_bank(b_sum, r)
                    dve.wait(r)
                    m_ready = dve.done(V.reciprocal(m_rstd[:, :], m_rstd[:, :]))
                    b_col = take_bank()
                    pe.wait(m_ready)
                    for t in range(2):
                        mm = matmul(bank[b_col][:, t:t + 1], m_rstd[0:1, t * P:(t + 1) * P],
                                    const("ident")[0:1, 0:1])
                    mm = pe.done(mm)
                    m_col_ready = copy(dve, m_col[:, :], bank[b_col][:, 0:2], mm)
                    free_bank(b_col, m_col_ready)
                    for i in range(4):
                        n = take(f"wk{l}", i)
                        for c in range(2):
                            j = 2 * i + c
                            b = take_bank()
                            mm = project(n, 2 * P, c, m, range(KT), b, width=N_MEM)
                            k_ready = tt(kT[:, j, :], bank[b][:, 0:N_MEM], m_rstd[:, :], ALU.mult, mm, m_ready)
                            free_bank(b, k_ready)
                    for i in range(4):
                        n = take(f"wv{l}", i)
                        hi, lo = unit(n, 2 * P)
                        pe.wait(*unit_split[n])
                        for t in range(2):
                            b = take_bank()
                            for k in range(KT):
                                rows = slice(t * P, (t + 1) * P)
                                mm = split_matmul(bank[b][:, 0:2 * P], m_hi[:, k, rows], m_lo[:, k, rows],
                                                  hi[:, k, :], lo[:, k, :], k == 0, k == KT - 1)
                            mm = pe.done(mm)
                            unit_done[n] = mm
                            v_ready = ts(v[:, t, i * 2 * P:(i + 1) * 2 * P], bank[b][:, 0:2 * P],
                                         m_col[:, t:t + 1], None, ALU.mult, None, mm, m_col_ready)
                            free_bank(b, v_ready)
                    inner_end = [pe.last(), act.last(), dve.last()]
                q_sb = ar.sb(f"xa{l}_q", [P, 2, 2, S])
                prob = ar.sb(f"xa{l}_p", [P, 2, 2, N_MEM])
                pT = ar.sb(f"xa{l}_pT", [P, 2, S])
                stat = ar.sb(f"xa{l}_stat", [P, 2, 8])
                act.wait(*inner_end)
                dve.wait(*inner_end)
                qh_read = [None, None]
                prob_read = [None, None]
                pT_read = None

                def queries(h):
                    n = take(f"wq{l}", h)
                    for c in range(2):
                        b = take_bank()
                        mm = project(n, 2 * P, c, xg, range(KT), b)
                        ready = scaled_by_rstd(q_sb[:, h % 2, c, :], b, mm, qh_read[h % 2])
                    return ready

                q_ready = queries(0)
                for h in range(XA_HEADS):
                    q_now = q_ready
                    b_s = [take_bank(), take_bank()]
                    pe.wait(q_now, k_ready)
                    scored = [None, None]
                    for pair in range(2):
                        for u in range(2):
                            qt = 2 * pair + u
                            for c in range(2):
                                mm = matmul(bank[b_s[pair]][:, u * N_MEM:(u + 1) * N_MEM],
                                            q_sb[:, h % 2, c, qt * P:(qt + 1) * P], kT[:, 2 * h + c, :],
                                            c == 0, c == 1)
                        scored[pair] = pe.done(mm)
                    qh_read[h % 2] = pe.last()
                    if h + 1 < XA_HEADS:
                        q_ready = queries(h + 1)
                    else:
                        norm_state["xg_last"] = unit_done[taken[0] - 1]
                    b_t = [take_bank(), take_bank()]
                    for pair in range(2):
                        st = stat[:, pair, :]
                        sc = bank[b_s[pair]][:, :].rearrange("p (u m) -> p u m", u=2)
                        dve.wait(scored[pair], prob_read[pair])
                        top = dve.done(V.tensor_reduce(st[:, 0:2], sc, AX_X, ALU.max))
                        top = ts(st[:, 2:4], st[:, 0:2], -XA_HD ** -0.5, None, ALU.mult, None, top)
                        for u in range(2):
                            e = activate(prob[:, pair, u, :], sc[:, u, :], ACT.Exp, top, prob_read[pair],
                                         scale=XA_HD ** -0.5, bias=st[:, 2 + u:3 + u],
                                         accum_out=st[:, 4 + u:5 + u])
                        free_bank(b_s[pair], e)
                        dve.wait(e)
                        r = dve.done(V.reciprocal(st[:, 6:8], st[:, 4:6]))
                        for u in range(2):
                            r2 = ts(prob[:, pair, u, :], prob[:, pair, u, :], st[:, 6 + u:7 + u], None,
                                    ALU.mult, None, r)
                        pe.wait(r2)
                        for u in range(2):
                            for t in range(2):
                                qt = 2 * pair + u
                                mm = T.transpose(bank[b_t[t]][:, qt * P:(qt + 1) * P],
                                                 prob[:, pair, u, t * P:(t + 1) * P], const("ident"))
                        prob_read[pair] = pe.done(mm)
                    for t in range(2):
                        p_ready = copy((act, dve)[t], pT[:, t, :], bank[b_t[t]][:, :], pe.last(), pT_read)
                        free_bank(b_t[t], p_ready)
                        pe.wait(p_ready)
                    for c in range(2):
                        j = 2 * h + c
                        b = take_bank()
                        for t in range(2):
                            pe.wait(v_ready)
                            mm = matmul(bank[b][:, :], v[:, t, j * P:(j + 1) * P], pT[:, t, :], t == 0, t == 1)
                        mm = pe.done(mm)
                        pT_read = mm
                        act.wait(mm)
                        hi = act.done(A.activation(o_hi[:, j, :], bank[b][:, :], ACT.Copy))
                        lo = tt(o_lo[:, j, :], bank[b][:, :], o_hi[:, j, :].bitcast(F32), ALU.subtract, hi)
                        o.ready[j] = (hi, lo)
                        free_bank(b, hi, lo)
                out_projection([(f"wo{l}", 4, 2 * P)], o, {f"wo{l}": range(KT)}, next_norm(f"f_norm{l}"))
                norm_end()

        def conv_ffn(l, next_gain):
            phase_wait()
            with ExitStack() as ph:
                ar = Arena(nc, ph)
                hid = [Acts(ar.sb(f"f{l}_h_hi{i}", [P, KT, S], F32R), ar.sb(f"f{l}_h_lo{i}", [P, KT, S], F32R), KT)
                       for i in range(2)]
                z = ar.sb(f"f{l}_z", [P, 2, S])
                g = ar.sb(f"f{l}_g", [P, 2, S])
                u = ar.sb(f"f{l}_u", [P, 2, S])
                free = [None, None]
                hid_free = [None, None]
                for p in range(3):
                    h = hid[p % 2]
                    for j in range(KT):
                        i = j % 2
                        ch = KT * p + j
                        n = take(f"up{l}", ch)
                        b_g = take_bank()
                        mm_g = project(n, 2 * P, 0, xg, range(KT), b_g)
                        b_u = take_bank()
                        mm_u = project(n, 2 * P, 1, xg, range(KT), b_u)
                        norm_state["xg_last"] = mm_u
                        w = lambda k, ch=ch: vcol(f"f_dw_w{l}", CONV_F * ch + k)
                        ready = scaled_by_rstd(z[:, i, :], b_g, mm_g, free[i])
                        ready = activate(g[:, i, :], z[:, i, :], ACT.Identity, ready, free[i],
                                         scale=w(CONV_F - 1), bias=vcol(f"f_dw_b{l}", ch))
                        ready = causal_taps(g[:, i, :], z[:, i, :], w, (CONV_F - 1, range(CONV_F - 1)), ready)
                        ge = activate(g[:, i, :], g[:, i, :], ACT.Gelu_apprx_tanh, ready)
                        u_ready = scaled_by_rstd(u[:, i, :], b_u, mm_u, free[i])
                        prod = tt(u[:, i, :], u[:, i, :], g[:, i, :], ALU.mult, ge, u_ready)
                        hi, lo = split_act(h, j, u[:, i, :], prod, hid_free[p % 2])
                        free[i] = lo
                    for i in range(4):
                        n = take(f"down{l}", 4 * p + i)
                        for c in range(2):
                            j = 2 * i + c
                            b = take_bank()
                            mm = project(n, 2 * P, c, h, range(KT), b)
                            token = add_to_x(j, b, mm)
                            if p == 2:
                                if j == 0:
                                    norm_begin_late()
                                norm_sums(0)
                                norm_tile(j, next_gain, token)
                    hid_free[p % 2] = pe.last()
                norm_end()

        def conformer():
            phase_wait()
            with ExitStack() as ph:
                ar = Arena(nc, ph)
                h_all = ar.sb("c_h", [P, KT, S])
                s_hi, s_lo = ar.sb("c_s_hi", [P, KT, S], F32R), ar.sb("c_s_lo", [P, KT, S], F32R)
                s = Acts(s_hi, s_lo, KT)
                t1 = ar.sb("c_t1", [P, 2, S])
                t2 = ar.sb("c_t2", [P, 2, S])
                mu = ar.sb("c_mu", [P, S])
                diag = ar.sb("c_diag", [P, 4, P])
                free = [None, None]
                diag_read = [None] * 4
                n_diag = 0
                h_ready = [None] * KT
                for j in range(KT):
                    i = j % 2
                    n = take("pw1", j)
                    b1 = take_bank()
                    mm1 = project(n, 2 * P, 0, xg, range(KT), b1)
                    b2 = take_bank()
                    mm2 = project(n, 2 * P, 1, xg, range(KT), b2)
                    norm_state["xg_last"] = mm2
                    r2 = scaled_by_rstd(t2[:, i, :], b2, mm2, free[i])
                    r2 = activate(t2[:, i, :], t2[:, i, :], ACT.Sigmoid, r2, bias=vcol("c_b1", KT + j))
                    r1 = scaled_by_rstd(t1[:, i, :], b1, mm1, free[i])
                    r1 = stt(t1[:, i, :], t1[:, i, :], vcol("c_b1", j), t2[:, i, :], ALU.add, ALU.mult, r1, r2)
                    w = lambda k, j=j: vcol("c_dw_w", CONV_C * j + k)
                    last = activate(h_all[:, j, :], t1[:, i, :], ACT.Identity, r1,
                                    scale=w(CONV_C - 1), bias=vcol("c_dw_b", j))
                    b = take_bank()
                    order = list(range(CONV_C_PE))[::-1]
                    base = CONV_C - 1 - order[0]
                    for m, k in enumerate(order):
                        d = n_diag % 4
                        n_diag += 1
                        dg = activate(diag[:, d, :], const("ident"), ACT.Copy, diag_read[d], scale=w(k))
                        pe.wait(dg, r1)
                        sh = CONV_C - 1 - k
                        mm = matmul(bank[b][:, sh:], diag[:, d, :], t1[:, i, 0:S - sh], m == 0,
                                    m == len(order) - 1)
                        diag_read[d] = pe.done(mm)
                    ready = causal_taps(h_all[:, j, :], t1[:, i, :], w,
                                        (CONV_C - 1, range(CONV_C_PE, CONV_C - 1)), last)
                    ready = tt(h_all[:, j, base:], bank[b][:, base:], h_all[:, j, base:], ALU.add, diag_read[d],
                               ready)
                    free_bank(b, ready)
                    free[i] = ready
                    h_ready[j] = ready
                b = take_bank()
                for j in range(KT):
                    pe.wait(h_ready[j])
                    mm = matmul(bank[b][:, :], const("ones"), h_all[:, j, :], j == 0, j == KT - 1)
                mm = pe.done(mm)
                mean = activate(mu[:, :], bank[b][:, :], ACT.Copy, mm, scale=1.0 / D)
                free_bank(b, mean)
                b = take_bank()
                for j in range(KT):
                    h_ready[j] = tt(h_all[:, j, :], h_all[:, j, :], mu[:, :], ALU.subtract, mean)
                    sq = activate(square[:, j % 2, :], h_all[:, j, :], ACT.Square, h_ready[j], square_read[j % 2])
                    pe.wait(sq)
                    square_read[j % 2] = pe.done(matmul(bank[b][:, :], const("ones"), square[:, j % 2, :],
                                                        j == 0, j == KT - 1))
                rt = activate(mu[:, :], bank[b][:, :], ACT.Sqrt, pe.last(), dve.last(), scale=1.0 / D,
                              bias=const("eps"))
                free_bank(b, rt)
                dve.wait(rt)
                inv = dve.done(V.reciprocal(t1[:, 0, :], mu[:, :]))
                for j in range(KT):
                    r = stt(h_all[:, j, :], h_all[:, j, :], vcol("c_ln_g", j), t1[:, 0, :], ALU.mult, ALU.mult, inv)
                    r = activate(h_all[:, j, :], h_all[:, j, :], ACT.Silu, r, bias=vcol("c_ln_b", j))
                    split_act(s, j, h_all[:, j, :], r)
                out_projection([("pw2", 4, 2 * P)], s, {"pw2": range(KT)}, next_norm("xa_norm1"),
                               bias=lambda j: vcol("c_b2", j))
                norm_end()

        def final_norm():
            rstd_ready = norm_state["rstd"]
            norm_state["xg_free"] = norm_state["xg_last"]
            norm_state["todo"] = []
            for j in range(KT):
                token = stt(x[:, j, :], x[:, j, :], vcol("final", j), rstd[:, :], ALU.mult, ALU.mult, rstd_ready,
                            act.last())
                norm_tile(j, "norm1_g", token)
                norm_sums(1)
            norm_sums()
            dve.wait(dve.last())
            norm_end()

        def rstd_by_token(dst):
            b = take_bank()
            pe.wait(norm_state["rstd"])
            for t in range(4):
                mm = matmul(bank[b][:, t:t + 1], rstd[0:1, t * P:(t + 1) * P], const("ident")[0:1, 0:1])
            mm = pe.done(mm)
            token = copy(dve, dst, bank[b][:, 0:4], mm)
            free_bank(b, token)
            return token

        def inverse_root(dst, tmp_ap, b, mm, scale, eps, *after):
            r = activate(tmp_ap, bank[b][:, :], ACT.Sqrt, mm, *after, scale=scale, bias=const(eps))
            free_bank(b, r)
            dve.wait(r, *after)
            return dve.done(V.reciprocal(dst, tmp_ap))

        def rwkv():
            ends = phase_wait()
            spill = Loader(sp, sem("x_spill_store"))
            spilled = spill.load(x_spill, x[:, :, :], *ends)
            with ExitStack() as ph:
                ar = Arena(nc, ph)
                rc_at, n_rc = _places(_rwkv_consts())
                rc = ar.sb("rw_constants", [P, n_rc])
                masks = ar.sb("rw_level_masks", [P, 2 * LEVELS, P], U8)
                up_w = ar.sb("rw_lora_w", [P, 3, RW])
                small = ar.sb("rw_small", [P, 24])
                R, A_, B, K = [ar.sb(f"rw_{m}", [P, S]) for m in ("R", "A", "B", "K")]
                Bh, Kh, t3 = [ar.sb(f"rw_{m}", [P, S]) for m in ("Bh", "Kh", "t3")]
                tokV, tokB, tokK = [ar.sb(f"rw_tok_{m}", [P, 4, P]) for m in ("V", "B", "K")]
                GA = ar.sb("rw_lakv_a", [P, 2, 4, P])
                UW = ar.sb("rw_u_w", [P, 2, 4, P])
                LT, X, XT, U, Lrb, Lrk = [ar.sb(f"rw_{m}", [P, 2, 4, P]) for m in
                                          ("LT", "X", "XT", "U", "Lrb", "Lrk")]
                MT, N_ = ar.sb("rw_MT", [P, 8, HEAD]), ar.sb("rw_N", [P, 8, HEAD])
                St = ar.sb("rw_S", [P, 8, HEAD])
                t0, t1, t2 = square[:, 0, :], square[:, 1, :], root[:, :]
                wl, al, gl, r_, k_, v_, kk, ksum = [x[:, i, :] for i in range(8)]

                def rconst(name):
                    a, n = rc_at[name]
                    return rc[:, a:a + n]

                ld = Loader(sp, sem("rw_loads"))
                ld.load(rc[:, :], rconsts, *ends)
                masks_f32 = x[:, 3:6, :].rearrange("p a b -> p (a b)")
                ld.load(masks_f32, level_masks.rearrange("p m c -> p (m c)"), spilled)
                loaded = ld.load(up_w[:, :, :], lora_w)
                for q in (pe, act, dve, pool):
                    q.wait(loaded, spilled)
                masks_ready = copy(dve, masks[:, :, :].rearrange("p m c -> p (m c)"), masks_f32)
                dve.wait(masks_ready)
                omka = small[:, 0:4]
                mu0 = small[:, 4:19]
                c1 = ts(omka, vec[:, col["k_a"]:col["k_a"] + 4], -1.0, 1.0, ALU.mult, ALU.add)
                c2 = tt(mu0, vec[:, col["mu_prev"]:col["mu_prev"] + 15], vec[:, col["mu_next"]:col["mu_next"] + 15],
                        ALU.add)
                c2 = ts(mu0, mu0, -1.0, 1.0, ALU.mult, ALU.add, c2)

                def shifted(dst, n, c, m, *after):
                    b = take_bank()
                    mm = project(n, 2 * P, c, xg, range(KT), b)
                    z = scaled_by_rstd(t3[:, :], b, mm, dve.last(), *after)
                    d = ts(dst, t3[:, :], mu0[:, m:m + 1], None, ALU.mult, None, z, c2, *after)
                    d = stt(dst[:, 1:], t3[:, 0:S - 1], vcol("mu_prev", m), dst[:, 1:], ALU.mult, ALU.add, d)
                    return stt(dst[:, 0:S - 1], t3[:, 1:], vcol("mu_next", m), dst[:, 0:S - 1], ALU.mult,
                               ALU.add, d)

                n = take("lora", 0)
                z = shifted(wl, n, 0, 12)
                wl_ready = activate(wl, wl, ACT.Tanh, z)
                al_ready = shifted(al, n, 1, 13)
                n = take("lora", 1)
                z = shifted(gl, n, 0, 14)
                gl_ready = activate(gl, gl, ACT.Sigmoid, z)

                def transposed(dst_of, src, ready, engine, *after):
                    b = take_bank()
                    pe.wait(ready)
                    for t in range(4):
                        mm = T.transpose(bank[b][:, t * P:(t + 1) * P], src[:, t * P:(t + 1) * P], const("ident"))
                    mm = pe.done(mm)
                    token = copy(engine, dst_of, bank[b][:, :].rearrange("p (t c) -> p t c", t=4), mm, *after)
                    free_bank(b, token)
                    return token

                def four(ap):
                    return ap.unsqueeze(1).to_broadcast([P, 4, P])

                def quad(b):
                    return bank[b][:, :].rearrange("p (t c) -> p t c", t=4)

                store = Loader(sp, sem("ya_store"))
                y_stored = None
                for t in range(4):
                    prev = (pe.last(), act.last())
                    n = take("rkvg", 2 * t)
                    r_ready = shifted(r_, n, 0, t, *prev)
                    k_ready = shifted(k_, n, 1, 4 + t, *prev)
                    n = take("rkvg", 2 * t + 1)
                    v_ready = shifted(v_, n, 0, 8 + t, *prev)
                    norm_state["xg_last"] = pe.last()
                    kr = ts(kk, k_, vcol("k_k", t), None, ALU.mult, None, k_ready)
                    sq = activate(t0, kk, ACT.Square, kr)
                    b = take_bank()
                    pe.wait(sq)
                    mm = pe.done(matmul(bank[b][:, :], const("head_ones"), t0))
                    inv = inverse_root(t1, t2, b, mm, 1.0, "kk_eps")
                    kk_ready = tt(kk, kk, t1, ALU.mult, inv)
                    tokV_ready = transposed(tokV[:, :, :], v_, v_ready, act)
                    pe.wait(*bank_free[7])
                    for d, (w0, a0) in enumerate((("w0_f", "a0_f"), ("w0_b", "a0_b"))):
                        rows = slice(d * HEAD, (d + 1) * HEAD)
                        cols = slice(t * P, (t + 1) * P)
                        prior = pe.last()
                        b = take_bank()
                        pe.wait(wl_ready, al_ready)
                        mm = pe.done(matmul(bank[b][:, :], up_w[rows, 0, cols], wl[rows, :]))
                        lw = activate(t0, bank[b][:, :], ACT.Sigmoid, mm, kk_ready, dve.last(), bias=vcol(w0, t))
                        free_bank(b, lw)
                        b = take_bank()
                        mm = pe.done(matmul(bank[b][:, :], up_w[rows, 1, cols], al[rows, :]))
                        a_ready = activate(t1, bank[b][:, :], ACT.Sigmoid, mm, bias=vcol(a0, t))
                        free_bank(b, a_ready)
                        kd = ts(Kh[:, :], t1, vcol("k_a", t), omka[:, t:t + 1], ALU.mult, ALU.add, a_ready, c1, prior)
                        kd = tt(Kh[:, :], Kh[:, :], k_, ALU.mult, kd)
                        if d == 0:
                            ks = copy(dve, ksum, Kh[:, :], kd, prior)
                        else:
                            ks = tt(ksum, ksum, Kh[:, :], ALU.add, kd)
                        kka = tt(Bh[:, :], kk, t1, ALU.mult, kk_ready)
                        lw = ts(t0, t0, -float(np.exp(-0.5)), None, ALU.mult, None, lw)
                        dve.wait(lw)
                        F = dve.done(V.tensor_tensor_scan(t2, rconst("reset"), t0, 0.0, ALU.mult, ALU.add))
                        E = tt(t3[:, :], t2, t0, ALU.subtract, F)
                        ch = lambda ap: ap.rearrange("p (c t) -> p c t", t=CHUNK)
                        total = ch(t2)[:, :, CHUNK - 1:CHUNK].to_broadcast([P, 8, CHUNK])
                        rest = tt(ch(t0), total, ch(t2), ALU.subtract, E)
                        decay = small[:, 19:19 + 1]
                        if d == 0:
                            dR, dA, dH, ready = t2, t3[:, :], t0, rest
                        else:
                            ready = tt(ch(t1), total, ch(t3[:, :]), ALU.subtract, kka, rest)
                            dR, dA, dH = t1, t0, t3[:, :]
                        DC = dcol
                        dc_ready = activate(DC[:, :], ch(t2)[:, :, CHUNK - 1], ACT.Exp, F, dve.last())
                        e = activate(R[:, :], dR, ACT.Exp, ready, prior)
                        Rr = tt(R[:, :], R[:, :], r_, ALU.mult, e, r_ready)
                        e = activate(A_[:, :], dA, ACT.Exp, prior)
                        Ar = stt(A_[:, :], A_[:, :], -1.0, kk, ALU.mult, ALU.mult, e)
                        e = activate(B[:, :], dR, ACT.Exp, prior, scale=-1.0)
                        Kr = tt(K[:, :], B[:, :], Kh[:, :], ALU.mult, e)
                        Br = tt(B[:, :], B[:, :], Bh[:, :], ALU.mult, Kr)
                        e = activate(dH, dH, ACT.Exp)
                        Khr = tt(Kh[:, :], Kh[:, :], dH, ALU.mult, e)
                        Bhr = tt(Bh[:, :], Bh[:, :], dH, ALU.mult)
                        pool.wait(prior, dve.last(), act.last())
                        x_init = None
                        for m in (X, XT):
                            for par in range(2):
                                x_init = pool.done(G.tensor_copy(m[:, par, :, :], four(const("ident"))))
                        b = take_bank()
                        pe.wait(Ar)
                        for i in range(4):
                            mm = T.transpose(bank[b][:, i * P:(i + 1) * P], A_[:, i * P:(i + 1) * P], const("ident"))
                        mm = pe.done(mm)
                        for par in range(2):
                            ga_ready = copy(act, GA[:, par, :, HEAD:P], quad(b)[:, :, par * HEAD:(par + 1) * HEAD],
                                            mm, prior)
                        free_bank(b, ga_ready)
                        tokB_ready = transposed(tokB[:, :, :], Bh[:, :], Bhr, act, prior)
                        tokK_ready = transposed(tokK[:, :, :], Kh[:, :], Khr, act, prior)
                        pe.wait(Rr, Ar, Br, Kr)

                        def products(lhs, rhs):
                            found = []
                            for par in range(2):
                                b = take_bank()
                                rows = slice(par * HEAD, (par + 1) * HEAD)
                                for i in range(4):
                                    c = slice(i * P, (i + 1) * P)
                                    mm = matmul(bank[b][:, c], lhs[rows, c], rhs[rows, c])
                                found.append((b, pe.done(mm)))
                            return found

                        up, low = (1, 0) if d == 0 else (0, 1)
                        x_ready, xt_ready, lt_ready = [None] * 2, [None] * 2, [None] * 2
                        for par, (b, mm) in enumerate(products(A_, B)):
                            dve.wait(mm, x_init)
                            x_ready[par] = dve.done(V.copy_predicated(
                                X[:, par, :, :], four(masks[:, low, :]), quad(b)))
                            free_bank(b, x_ready[par])
                        for par, (b, mm) in enumerate(products(B, A_)):
                            dve.wait(mm, x_init)
                            xt_ready[par] = dve.done(V.copy_predicated(
                                XT[:, par, :, :], four(masks[:, up, :]), quad(b)))
                            lt_ready[par] = copy(act, LT[:, par, :, :], quad(b), mm, prior, xt_ready[par])
                            free_bank(b, xt_ready[par], lt_ready[par])
                        lak, lrb, lrk = [None] * 2, [None] * 2, [None] * 2
                        for par, (b, mm) in enumerate(products(K, A_)):
                            lak[par] = tt(U[:, par, :, :], quad(b), four(rconst(f"strict{up}")), ALU.mult, mm, prior)
                            free_bank(b, lak[par])
                        for par, (b, mm) in enumerate(products(B, R)):
                            lrb[par] = tt(Lrb[:, par, :, :], quad(b), four(rconst(f"incl{up}")), ALU.mult, mm, prior)
                            free_bank(b, lrb[par])
                        for par, (b, mm) in enumerate(products(K, R)):
                            lrk[par] = tt(Lrk[:, par, :, :], quad(b), four(rconst(f"incl{up}")), ALU.mult, mm, prior)
                            free_bank(b, lrk[par])
                        b = take_bank()
                        for par in range(2):
                            pe.wait(lak[par], tokV_ready)
                            for i in range(4):
                                mm = matmul(bank[b][:, (4 * par + i) * HEAD:(4 * par + i + 1) * HEAD],
                                            U[:, par, i, :], tokV[:, i, par * HEAD:(par + 1) * HEAD])
                        mm = pe.done(mm)
                        lak_read = mm
                        g_ready = copy(act, GA[:, :, :, 0:HEAD],
                                       bank[b][:, :].rearrange("p (a t c) -> p a t c", a=2, t=4), mm, prior)
                        free_bank(b, g_ready)
                        for l in range(1, LEVELS):
                            u_ready = [None] * 2
                            for par in range(2):
                                b = take_bank()
                                pe.wait(lt_ready[par], x_ready[par], xt_ready[par])
                                for i in range(4):
                                    mm = matmul(bank[b][:, i * P:(i + 1) * P], LT[:, par, i, :], X[:, par, i, :])
                                mm = pe.done(mm)
                                u_ready[par] = copy(act, U[:, par, :, :], quad(b), mm, lak_read)
                                free_bank(b, u_ready[par])
                            for par in range(2):
                                pe.wait(u_ready[par])
                                if l < LEVELS - 1:
                                    b = take_bank()
                                    for i in range(4):
                                        mm = matmul(bank[b][:, i * P:(i + 1) * P], XT[:, par, i, :], U[:, par, i, :])
                                    mm = pe.done(mm)
                                    dve.wait(mm)
                                    x_ready[par] = dve.done(V.copy_predicated(
                                        X[:, par, :, :], four(masks[:, 2 * l + low, :]), quad(b)))
                                    free_bank(b, x_ready[par])
                                b = take_bank()
                                for i in range(4):
                                    mm = matmul(bank[b][:, i * P:(i + 1) * P], U[:, par, i, :], XT[:, par, i, :])
                                mm = pe.done(mm)
                                dve.wait(mm)
                                xt_ready[par] = dve.done(V.copy_predicated(
                                    XT[:, par, :, :], four(masks[:, 2 * l + up, :]), quad(b)))
                                free_bank(b, xt_ready[par])
                        uw_ready = [None] * 2
                        for par in range(2):
                            b = take_bank()
                            pe.wait(xt_ready[par], g_ready, ga_ready)
                            for i in range(4):
                                mm = matmul(bank[b][:, i * P:(i + 1) * P], XT[:, par, i, :], GA[:, par, i, :])
                            mm = pe.done(mm)
                            uw_ready[par] = copy(act, UW[:, par, :, :], quad(b), mm, prior)
                            free_bank(b, uw_ready[par])
                        pe.wait(*uw_ready, tokB_ready, tokK_ready)
                        b_eo = [take_bank(), take_bank()]
                        for par in range(2):
                            hc = slice(par * HEAD, (par + 1) * HEAD)
                            for c in range(8):
                                i, rows, b = c // 2, slice((c % 2) * HEAD, (c % 2 + 1) * HEAD), b_eo[c % 2]
                                o = slice(i * HEAD, (i + 1) * HEAD)
                                o2 = slice((4 + i) * HEAD, (5 + i) * HEAD)
                                matmul(bank[b][hc, o], UW[rows, par, i, HEAD:P], tokB[rows, i, hc])
                                matmul(bank[b][hc, o2], tokB[rows, i, hc], UW[rows, par, i, 0:HEAD], True, False)
                                mm = matmul(bank[b][hc, o2], tokK[rows, i, hc], tokV[rows, i, hc], False, True)
                        mm = pe.done(mm)
                        dg = tt(MT[:, :, :], rconst("ident2").unsqueeze(1).to_broadcast([P, 8, HEAD]),
                                DC[:, :].unsqueeze(2).to_broadcast([P, 8, HEAD]), ALU.mult, dc_ready, prior)
                        by2 = lambda ap: ap.rearrange("p (i e) j -> p e i j", e=2)
                        for e_ in range(2):
                            b = b_eo[e_]
                            mn = bank[b][:, :].rearrange("p (m c j) -> p m c j", m=2, c=4)
                            mt_ready = tt(by2(MT[:, :, :])[:, e_], by2(MT[:, :, :])[:, e_], mn[:, 0], ALU.add, mm, dg)
                            n_ready = copy(dve, by2(N_[:, :, :])[:, e_], mn[:, 1], mm)
                            free_bank(b, n_ready)
                        b = take_bank()
                        for par in range(2):
                            pe.wait(lrb[par])
                            for i in range(4):
                                mm = matmul(bank[b][par * HEAD:(par + 1) * HEAD, i * P:(i + 1) * P],
                                            UW[:, par, i, HEAD:P], Lrb[:, par, i, :])
                        mm = pe.done(mm)
                        z_ready = tt(R[:, :], R[:, :], bank[b][:, :], ALU.add, mm)
                        free_bank(b, z_ready)
                        for par in range(2):
                            hc = slice(par * HEAD, (par + 1) * HEAD)
                            pe.wait(lrk[par])
                            for i in range(4):
                                o = slice(i * P, (i + 1) * P)
                                matmul(bank[7][hc, o], UW[:, par, i, 0:HEAD], Lrb[:, par, i, :],
                                       d == 0 and i == 0, False)
                                matmul(bank[7][hc, o], tokV[:, i, hc], Lrk[:, par, i, :], False, False)
                        order = list(range(8)) if d == 0 else list(range(8))[::-1]
                        dve.wait(prior)
                        s_ready = dve.done(V.memset(St[:, order[0], :], 0.0))
                        b = take_bank()
                        for step in range(7):
                            c, c_next = order[step], order[step + 1]
                            pe.wait(s_ready, mt_ready)
                            o = slice(step * HEAD, (step + 1) * HEAD)
                            for par in range(2):
                                hc = slice(par * HEAD, (par + 1) * HEAD)
                                mm = matmul(bank[b][hc, o], MT[hc, c, :], St[hc, c, :])
                            mm = pe.done(mm)
                            s_ready = tt(St[:, c_next, :], bank[b][:, o], N_[:, c, :], ALU.add, mm, n_ready)
                        free_bank(b, s_ready)
                        pe.wait(s_ready, z_ready)
                        for par in range(2):
                            hc = slice(par * HEAD, (par + 1) * HEAD)
                            for c in range(8):
                                o = slice(c * CHUNK, (c + 1) * CHUNK)
                                mm = matmul(bank[7][hc, o], St[hc, c, :], R[hc, o], False, d == 1 and c == 7)
                        y_done = pe.done(mm)
                    yt, yn = A_[:, :], B[:, :]
                    yr = copy(act, yt, bank[7][:, :], y_done, dve.last())
                    bank_free[7] = [yr]
                    b = take_bank()
                    pe.wait(yr)
                    mm = pe.done(matmul(bank[b][:, :], const("head_ones"), yt))
                    yc = stt(yt, bank[b][:, :], -1.0 / HEAD, yt, ALU.mult, ALU.add, mm)
                    free_bank(b, yc)
                    sq = activate(t0, yt, ACT.Square, yc)
                    b = take_bank()
                    pe.wait(sq)
                    mm = pe.done(matmul(bank[b][:, :], const("head_ones"), t0))
                    inv = inverse_root(t1, t2, b, mm, 1.0 / HEAD, "gn_eps", dve.last())
                    yn_r = tt(yt, yt, t1, ALU.mult, inv, y_stored)
                    yn_r = ts(yt, yt, vcol("lnx_g", t), vcol("lnx_b", t), ALU.mult, ALU.add, yn_r)
                    bo = stt(ksum, ksum, vcol("r_k", t), r_, ALU.mult, ALU.mult, ks)
                    b = take_bank()
                    pe.wait(bo)
                    mm = pe.done(matmul(bank[b][:, :], const("head_ones"), ksum))
                    bo = tt(t0, bank[b][:, :], v_, ALU.mult, mm, sq)
                    free_bank(b, bo)
                    yn_r = tt(yt, yt, t0, ALU.add, yn_r, bo)
                    b = take_bank()
                    pe.wait(gl_ready)
                    mm = pe.done(matmul(bank[b][:, :], up_w[:, 2, t * P:(t + 1) * P], gl))
                    yg = tt(yn, yt, bank[b][:, :], ALU.mult, mm, yn_r)
                    free_bank(b, yg)
                    y_stored = store.load(y_spill[0, :, t, :], yn, yg)
                    for q in (dve, act, pool):
                        q.wait(y_stored)
                return y_stored

        def neighbourhood():
            ends = phase_wait()
            with ExitStack() as ph:
                ar = Arena(nc, ph)
                r_col = ar.sb("na_rstd_col", [P, 4])
                v = ar.sb("na_v", [P, 4, RW])
                qk = ar.sb("na_qk", [P, 2, 2, S])
                bias = ar.sb("na_bias", [P, 2, 14, GRID_W])
                score = ar.sb("na_score", [P, 4, S])
                pT = ar.sb("na_pT", [P, 4, S])
                stat = ar.sb("na_stat", [P, 4, 4])
                out_t = ar.sb("na_out", [P, 2, S])
                gain8 = ar.sb("na_gain8", [P, 1])
                g8 = ts(gain8[:, :], vcol("q_gain"), HEAD ** -0.5, None, ALU.mult, None)
                col_ready = rstd_by_token(r_col[:, :])
                for i in range(2):
                    n = take("na_v", i)
                    hi, lo = unit(n, 2 * P)
                    pe.wait(*unit_split[n])
                    for t in range(4):
                        b = take_bank()
                        rows = slice(t * P, (t + 1) * P)
                        for k in range(KT):
                            mm = split_matmul(bank[b][:, 0:2 * P], xg_hi[:, k, rows], xg_lo[:, k, rows],
                                              hi[:, k, :], lo[:, k, :], k == 0, k == KT - 1)
                        mm = pe.done(mm)
                        unit_done[n] = mm
                        v_ready = ts(v[:, t, i * 2 * P:(i + 1) * 2 * P], bank[b][:, 0:2 * P], r_col[:, t:t + 1],
                                     None, ALU.mult, None, mm, col_ready)
                        free_bank(b, v_ready)
                bias_load = [[Loader(sp, sem(f"na_bias{i}{a}")) for a in range(2)] for i in range(2)]
                bias_read = [ends[2], ends[2]]
                store = Loader(sp, sem("yb_store"))
                qk_read = [None, None]
                stored = [None, None]
                score_read = [None] * 4
                pT_read = None
                for t in range(4):
                    i = t % 2
                    n = take("na_qk", t)
                    ready = [None, None]
                    for c in range(2):
                        b = take_bank()
                        mm = project(n, 2 * P, c, xg, range(KT), b)
                        z = scaled_by_rstd(qk[:, i, c, :], b, mm, qk_read[i])
                        sq = activate(square[:, c, :], qk[:, i, c, :], ACT.Square, z, dve.last())
                        b = take_bank()
                        pe.wait(sq)
                        mm = pe.done(matmul(bank[b][:, :], const("head_ones"), square[:, c, :]))
                        inv = inverse_root(square[:, c, :], root[:, :], b, mm, 1.0 / HEAD, "eps", dve.last())
                        ready[c] = stt(qk[:, i, c, :], qk[:, i, c, :], gain8[:, :] if c == 0 else vcol("k_gain"),
                                       square[:, c, :], ALU.mult, ALU.mult, inv, g8)
                    b_o = None
                    for par in range(2):
                        h = 2 * t + par
                        hc = slice(par * HEAD, (par + 1) * HEAD)
                        loaded = []
                        for a in range(2):
                            loaded.append(bias_load[par][a].load(
                                bias[a * HEAD:(a + 1) * HEAD, par, :, :],
                                bias_na[h, 1 - a:15 - a, :, :].rearrange("m q k -> q m k"), *ends, bias_read[par]))
                        pool.wait(*loaded, bias_read[par])
                        bias_ready = pool.done(G.tensor_tensor(
                            bias[:, par, :, :], bias[:, par, :, :],
                            const("na_mask").unsqueeze(1).to_broadcast([P, 14, GRID_W]), ALU.add))
                        pe.wait(*ready)
                        done_q = []
                        for qt in range(4):
                            b = take_bank()
                            mm = pe.done(matmul(bank[b][:, :], qk[hc, i, 0, qt * P:(qt + 1) * P], qk[hc, i, 1, :]))
                            st = stat[:, qt, :]
                            rows = bias[:, par, 6 - 2 * qt:14 - 2 * qt, :].rearrange("p m k -> p (m k)")
                            dve.wait(mm, bias_ready, score_read[qt])
                            s1 = dve.done(V.tensor_tensor(score[:, qt, :], bank[b][:, :], rows, ALU.add))
                            free_bank(b, s1)
                            dve.wait(s1)
                            top = dve.done(V.tensor_reduce(st[:, 0:1], score[:, qt, :], AX_X, ALU.max, negate=True))
                            e = activate(score[:, qt, :], score[:, qt, :], ACT.Exp, top, bias=st[:, 0:1],
                                         accum_out=st[:, 1:2])
                            done_q.append(e)
                        bias_read[par] = s1
                        qk_read[i] = pe.last()
                        b_t = [take_bank() for _ in range(4)]
                        for qt in range(4):
                            st = stat[:, qt, :]
                            dve.wait(done_q[qt])
                            r = dve.done(V.reciprocal(st[:, 2:3], st[:, 1:2]))
                            r = ts(score[:, qt, :], score[:, qt, :], st[:, 2:3], None, ALU.mult, None, r)
                            pe.wait(r)
                            for k in range(4):
                                mm = T.transpose(bank[b_t[k]][:, qt * P:(qt + 1) * P],
                                                 score[:, qt, k * P:(k + 1) * P], const("ident"))
                            score_read[qt] = pe.done(mm)
                        p_ready = []
                        for k in range(4):
                            p_ready.append(copy((act, dve)[k % 2], pT[:, k, :], bank[b_t[k]][:, :], pe.last(), pT_read))
                            free_bank(b_t[k], p_ready[k])
                        if par == 0:
                            pe.wait(*bank_free[7])
                        for k in range(4):
                            pe.wait(p_ready[k], v_ready)
                            mm = matmul(bank[7][hc, :], v[:, k, h * HEAD:(h + 1) * HEAD], pT[:, k, :], k == 0, k == 3)
                        pT_read = pe.done(mm)
                    o = copy(act, out_t[:, i, :], bank[7][:, :], pT_read, stored[i])
                    bank_free[7] = [o]
                    stored[i] = store.load(y_spill[1, :, t, :], out_t[:, i, :], o)
                norm_state["xg_last"] = pe.last()
                return stored

        def combine(ya_stored, yb_stored):
            ends = phase_wait()
            with ExitStack() as ph:
                ar = Arena(nc, ph)
                y_sb = ar.sb("mix_y", [P, 2, 4, S])
                y2 = Acts(ar.sb("mix_y_hi", [P, 4, S], F32R), ar.sb("mix_y_lo", [P, 4, S], F32R), 4)
                z_act = Acts(ar.sb("mix_z_hi", [P, KT, S], F32R), ar.sb("mix_z_lo", [P, KT, S], F32R), KT)
                gate = ar.sb("mix_gate", [P, 2, S])
                x_loader = Loader(sp, sem("x_reload"))
                y_loader = [Loader(sp, sem(f"y_reload{i}")) for i in range(2)]
                y_loaded = [y_loader[0].load(y_sb[:, 0, :, :], y_spill[0], *ends, ya_stored),
                            y_loader[1].load(y_sb[:, 1, :, :], y_spill[1], *yb_stored)]
                free = [None, None]
                z_part = [None] * KT
                for side, (w_name, g_name) in enumerate((("o_rwkv", "gate_a"), ("o_na", "gate_b"))):
                    for k in range(4):
                        act.wait(y_loaded[side], pe.last())
                        dve.wait(y_loaded[side], pe.last())
                        split_act(y2, k, y_sb[:, side, k, :])
                    for half in range(2):
                        n = take(w_name, half)
                        banks = []
                        for c in range(4):
                            b = take_bank()
                            banks.append((b, project(n, 4 * P, c, y2, range(4), b)))
                        for u in range(2):
                            n = take(g_name, 2 * half + u)
                            for c in range(2):
                                j = 4 * half + 2 * u + c
                                b = take_bank()
                                mm = project(n, 2 * P, c, xg, range(KT), b)
                                norm_state["xg_last"] = mm
                                b_o, mm_o = banks[2 * u + c]
                                i = j % 2
                                gr = scaled_by_rstd(gate[:, i, :], b, mm, free[i])
                                gr = activate(gate[:, i, :], gate[:, i, :], ACT.Sigmoid, gr,
                                              bias=vcol("b_gate", KT * side + j))
                                if side == 0:
                                    z = tt(x[:, j, :], gate[:, i, :], bank[b_o][:, :], ALU.mult, gr, mm_o)
                                    z_part[j] = z
                                    free[i] = z
                                else:
                                    z = tt(gate[:, i, :], gate[:, i, :], bank[b_o][:, :], ALU.mult, gr, mm_o)
                                    z2 = tt(gate[:, i, :], gate[:, i, :], x[:, j, :], ALU.add, z, z_part[j])
                                    hi, lo = split_act(z_act, j, gate[:, i, :], z2)
                                    free[i] = lo
                                free_bank(b_o, z)
                x_back = x_loader.load(x[:, :, :], x_spill, dve.last())
                dve.wait(x_back)
                act.wait(x_back)
                out_projection([("w_out2", 4, 2 * P)], z_act, {"w_out2": range(KT)}, next_norm("norm2_g"))
                norm_end()

        def experts():
            ends = phase_wait()
            with ExitStack() as ph:
                ar = Arena(nc, ph)
                hid = [Acts(ar.sb(f"e_h_hi{i}", [P, KT, S], F32R), ar.sb(f"e_h_lo{i}", [P, KT, S], F32R), KT)
                       for i in range(2)]
                r_col = ar.sb("e_rstd_col", [P, 4])
                rb = ar.sb("e_router_b", [P, 36])
                combT = ar.sb("e_combine", [N_EXPERTS, S])
                weight = ar.sb("e_weight", [P, 2, S])
                g_sb = ar.sb("e_g", [P, 2, S])
                small = ar.sb("e_routing", [P, 480])
                at = [0]

                def piece(*shape):
                    n = int(np.prod(shape))
                    ap = small[:, at[0]:at[0] + n]
                    at[0] += n
                    return ap.rearrange("p (a b) -> p a b", a=shape[0]) if len(shape) > 1 else ap

                rb_loaded = Loader(sp, sem("router_b_load")).load(rb[:, :], router_b, *ends)
                col_ready = rstd_by_token(r_col[:, :])
                n = take("router", 0)
                hi, lo = unit(n, 2 * P)
                pe.wait(*unit_split[n])
                for k in range(KT):
                    pe.wait(*xg.ready[k])
                logits = piece(4, 36)
                b = take_bank()
                for t in range(4):
                    rows = slice(t * P, (t + 1) * P)
                    for k in range(KT):
                        mm = split_matmul(bank[b][:, t * 36:(t + 1) * 36], xg_hi[:, k, rows], xg_lo[:, k, rows],
                                          hi[:, k, 0:36], lo[:, k, 0:36], k == 0, k == KT - 1)
                mm = pe.done(mm)
                unit_done[n] = mm
                for t in range(4):
                    lg = stt(logits[:, t, :], bank[b][:, t * 36:(t + 1) * 36], r_col[:, t:t + 1], rb[:, :],
                             ALU.mult, ALU.add, mm, col_ready, rb_loaded)
                free_bank(b, lg)
                gl, el = logits[:, :, 0:4], logits[:, :, 4:36]
                wide = lambda ap, n: ap.to_broadcast([P, 4, n])

                def first_of(dst, values, top, n, seg, ready, tmp_ap):
                    r = tt(dst, values, wide(top, n), ALU.is_equal, ready)
                    dve.wait(r)
                    flat = lambda ap: ap.rearrange("p a b -> p (a b)")
                    r = dve.done(V.tensor_tensor_scan(flat(tmp_ap), const(seg), flat(dst), 0.0, ALU.mult, ALU.add))
                    r = ts(tmp_ap, tmp_ap, 1.0, None, ALU.is_equal, None, r)
                    return tt(dst, dst, tmp_ap, ALU.mult, r)

                g_top = piece(4, 1)
                dve.wait(lg)
                r = dve.done(V.tensor_reduce(g_top, gl, AX_X, ALU.max))
                g_one, g_tmp = piece(4, 4), piece(4, 4)
                one_r = first_of(g_one, gl, g_top, 4, "seg4", r, g_tmp)
                r = tt(g_tmp, gl, wide(g_top, 4), ALU.subtract, one_r)
                r = activate(g_tmp, g_tmp, ACT.Exp, r)
                p_group = piece(4, 1)
                dve.wait(r)
                r = dve.done(V.tensor_reduce(p_group, g_tmp, AX_X, ALU.add))
                dve.wait(r)
                pg_r = dve.done(V.reciprocal(p_group, p_group))
                e8, e_tmp = piece(4, 8), piece(4, 8)
                r = None
                for g in range(N_GROUPS):
                    dst = e8 if g == 0 else e_tmp
                    r = tt(dst, el[:, :, 8 * g:8 * g + 8], wide(g_one[:, :, g:g + 1], 8), ALU.mult, r)
                    if g:
                        r = tt(e8, e8, e_tmp, ALU.add, r)
                v1, v2, one1, one2 = piece(4, 1), piece(4, 1), piece(4, 8), piece(4, 8)
                dve.wait(r)
                r = dve.done(V.tensor_reduce(v1, e8, AX_X, ALU.max))
                r = first_of(one1, e8, v1, 8, "seg8", r, e_tmp)
                r = stt(e8, one1, -3e38, e8, ALU.mult, ALU.add, r)
                dve.wait(r)
                r = dve.done(V.tensor_reduce(v2, e8, AX_X, ALU.max))
                r = first_of(one2, e8, v2, 8, "seg8", r, e_tmp)
                w1, w2 = piece(4, 1), piece(4, 1)
                r = tt(w2, v2, v1, ALU.subtract, r)
                r = activate(w2, w2, ACT.Exp, r)
                r = ts(w1, w2, 1.0, None, ALU.add, None, r)
                dve.wait(r)
                r = dve.done(V.reciprocal(w1, w1))
                r = tt(w1, w1, p_group, ALU.mult, r, pg_r)
                r = tt(w2, w2, w1, ALU.mult, r)
                r = tt(one1, one1, wide(w1, 8), ALU.mult, r)
                r = tt(one2, one2, wide(w2, 8), ALU.mult, r)
                r = tt(one1, one1, one2, ALU.add, r)
                comb = piece(4, 32)
                for g in range(N_GROUPS):
                    comb_r = tt(comb[:, :, 8 * g:8 * g + 8], one1, wide(g_one[:, :, g:g + 1], 8), ALU.mult, r)
                b = take_bank()
                pe.wait(comb_r)
                for t in range(4):
                    mm = T.transpose(bank[b][0:N_EXPERTS, t * P:(t + 1) * P], comb[:, t, :], const("ident"))
                mm = pe.done(mm)
                comb_ready = copy(dve, combT[:, :], bank[b][0:N_EXPERTS, :], mm)
                free_bank(b, comb_ready)

                free = [None, None]
                weight_read = [None, None]
                hid_free = [None, None]
                stores = [Loader(sp, sem(f"out_store{j}")) for j in range(KT)]
                for bt in range(8):
                    h = hid[bt % 2]
                    for q in range(4):
                        e = 4 * bt + q
                        b = take_bank()
                        pe.wait(comb_ready)
                        mm = pe.done(matmul(bank[b][:, :], const("ident")[0:N_EXPERTS, e:e + 1].to_broadcast(
                            [N_EXPERTS, P]), combT[:, :]))
                        w_ready = scaled_by_rstd(weight[:, e % 2, :], b, mm)
                        for c in range(2):
                            n = take("expert", 2 * e + c)
                            b_g = take_bank()
                            mm_g = project(n, 2 * P, 0, xg, range(KT), b_g)
                            b_u = take_bank()
                            mm_u = project(n, 2 * P, 1, xg, range(KT), b_u)
                            r = scaled_by_rstd(g_sb[:, c, :], b_g, mm_g, free[c])
                            sil = activate(g_sb[:, c, :], g_sb[:, c, :], ACT.Silu, r)
                            r = tt(g_sb[:, c, :], g_sb[:, c, :], bank[b_u][:, :], ALU.mult, sil, mm_u)
                            free_bank(b_u, r)
                            r = tt(g_sb[:, c, :], g_sb[:, c, :], weight[:, e % 2, :], ALU.mult, r, w_ready)
                            hi_t, lo_t = split_act(h, 2 * q + c, g_sb[:, c, :], r, hid_free[bt % 2])
                            free[c] = lo_t
                    for i in range(4):
                        n = take("down_e", 4 * bt + i)
                        for c in range(2):
                            j = 2 * i + c
                            b = take_bank()
                            mm = project(n, 2 * P, c, h, range(KT), b)
                            token = add_to_x(j, b, mm)
                            if bt == 7:
                                last_stores.append(stores[j].load(out[:, j, :], x[:, j, :], token))
                    hid_free[bt % 2] = pe.last()
            for token in last_stores:
                sp.wait(token)

        last_stores = []
        dcol = sb("chunk_decay", [P, 8])

        mixer()
        cross_attention(0)
        conv_ffn(0, "c_norm")
        conformer()
        cross_attention(1)
        conv_ffn(1, None)
        final_norm()
        ya_stored = rwkv()
        yb_stored = neighbourhood()
        combine(ya_stored, yb_stored)
        experts()


def _unit_arrays(inp):
    def pack(w, cols):
        k, n = w.shape
        return w.reshape(k // P, P, n // cols, cols).transpose(2, 1, 0, 3).reshape(n // cols, P, -1)

    def pairs(a, b):
        k, n = a.shape
        return np.concatenate([a.reshape(k, n // P, P), b.reshape(k, n // P, P)], axis=2).reshape(k, 2 * n)

    w = {}
    w_in = inp["ab_w_in"][0]
    w["ab_in"] = pack(pairs(w_in[:, 0:D], w_in[:, D:2 * D]), 2 * P)
    w["pool_in"] = pack(w_in[:, 2 * D:], 2 * P)
    w["ab_out_a"] = pack(inp["ab_w_out"][0][0:D], 2 * P)
    w["ab_out_b"] = pack(inp["ab_w_out"][0][D:], 4 * P)
    w["pw1"] = pack(pairs(inp["c_w_pw1"][0][:, 0:D], inp["c_w_pw1"][0][:, D:]), 2 * P)
    w["pw2"] = pack(inp["c_w_pw2"][0], 2 * P)
    for l in range(DEPTH):
        for m in "kvqo":
            w[f"w{m}{l}"] = pack(inp[f"xa_w{m}"][l], 2 * P)
        up = inp["f_w_up"][l]
        w[f"up{l}"] = pack(pairs(up[:, 0:D_FF], up[:, D_FF:]), 2 * P)
        w[f"down{l}"] = np.concatenate([pack(inp["f_w_down"][l][p * D:(p + 1) * D], 2 * P) for p in range(3)])
    w2 = inp["w_in_2"][0]
    r_, k_, v_ = (w2[:, i * RW:(i + 1) * RW] for i in range(3))
    lora = w2[:, 3 * RW:3 * RW + 384]
    zero = np.zeros((D, P), np.float32)
    w["lora"] = pack(np.concatenate([lora, zero], axis=1), 2 * P)
    w["rkvg"] = pack(np.concatenate([np.concatenate([m[:, t * P:(t + 1) * P] for m in (r_, k_, v_)] + [zero], axis=1)
                                     for t in range(4)], axis=1), 2 * P)
    base = 3 * RW + 384
    q2, k2, v2 = (w2[:, base + i * RW:base + (i + 1) * RW] for i in range(3))
    w["na_v"] = pack(v2, 2 * P)
    w["na_qk"] = pack(pairs(q2, k2), 2 * P)
    gates = w2[:, base + 3 * RW:]
    w["gate_a"], w["gate_b"] = pack(gates[:, 0:D], 2 * P), pack(gates[:, D:], 2 * P)
    w["o_rwkv"], w["o_na"] = pack(inp["w_o_rwkv_2"][0], 4 * P), pack(inp["w_o_na_2"][0], 4 * P)
    w["w_out2"] = pack(inp["w_out_2"][0], 2 * P)
    router = np.concatenate([inp["w_router_group_2"][0], inp["w_router_expert_2"][0],
                             np.zeros((D, 2 * P - 36), np.float32)], axis=1)
    w["router"] = pack(router, 2 * P)
    up_e = np.concatenate([inp["w_gate_e_2"][0].reshape(N_EXPERTS, D, 2, P),
                           inp["w_up_e_2"][0].reshape(N_EXPERTS, D, 2, P)], axis=3)
    w["expert"] = np.concatenate([pack(up_e[e].reshape(D, 4 * P), 2 * P) for e in range(N_EXPERTS)])
    down = inp["w_down_e_2"][0].reshape(8, D, D)
    w["down_e"] = np.concatenate([pack(down[b], 2 * P) for b in range(8)])
    return np.stack([w[name][i] for name, i in _plan()])


def _channel_major(a):
    t, c = a.shape
    return np.ascontiguousarray(a.T.reshape(c // P, P, t).transpose(1, 0, 2))


def kernel(**inputs):
    import concourse.bacc as bacc
    from concourse.bass_utils import run_bass_kernel_spmd

    inp = {k: np.asarray(v) for k, v in inputs.items()}
    cols = []
    for _, name, layer in _vector_names():
        a = inp[name] if layer is None else inp[name][layer]
        cols.append(a.reshape(-1, P).T)
    for name, layer in (("a_conv_w", 0), ("c_dw_w", 0), ("f_dw_w", 0), ("f_dw_w", 1)):
        a = inp[name][layer]
        taps, width = a.shape
        cols.append(a.reshape(taps, width // P, P).transpose(2, 1, 0).reshape(P, -1))
    for name in ("q_gain_2", "k_gain_2"):
        cols.append(np.tile(inp[name][0], 2).reshape(P, 1))
    rpb = np.pad(inp["rpb_2"][0], ((0, 0), (0, 0), (48, 48)))
    bias = np.stack([rpb[:, :, 63 - q:127 - q] for q in range(GRID_W)], axis=2)
    lora = np.stack([np.concatenate([inp["w_up_f_2"][0], inp["w_up_b_2"][0]]),
                     np.concatenate([inp["a_up_f_2"][0], inp["a_up_b_2"][0]]), inp["g_up_2"][0]], axis=1)
    arrays = {
        "stream": _unit_arrays(inp),
        "vectors": np.concatenate(cols, axis=1),
        "consts": np.concatenate(list(_consts().values()), axis=1),
        "rconsts": np.concatenate(list(_rwkv_consts().values()), axis=1),
        "x_in": _channel_major(inp["x"][0]),
        "mem_in": _channel_major(inp["mem"][0]),
        "gates_w": np.stack([inp["a_gate_x_w"][0], inp["a_gate_a_w"][0]], axis=1).transpose(2, 0, 1, 3),
        "group_w": inp["b_group_w"][0].transpose(1, 0, 2),
        "lora_w": lora,
        "router_b": np.broadcast_to(np.concatenate([inp["b_router_group_2"][0], inp["b_router_expert_2"][0]]),
                                    (P, 36)),
        "bias_na": bias,
        "level_masks": _level_masks(),
    }
    arrays = {k: np.ascontiguousarray(v) for k, v in arrays.items()}
    nc = bacc.Bacc("TRN2", target_bir_lowering=False, num_devices=1)
    args = [nc.dram_tensor(k, v.shape, mybir.dt.from_np(v.dtype), kind="ExternalInput").ap()
            for k, v in arrays.items()]
    out = nc.dram_tensor("out", (P, KT, S), F32, kind="ExternalOutput").ap()
    spill = nc.dram_tensor("x_spill", (P, KT, S), F32, kind="Internal").ap()
    y_spill = nc.dram_tensor("y_spill", (2, P, 4, S), F32, kind="Internal").ap()
    build(nc, *args, out, spill, y_spill)
    r = run_bass_kernel_spmd(nc, [arrays], core_ids=[0])
    got = np.asarray(r.results[0]["out"])
    return np.ascontiguousarray(got.transpose(1, 0, 2).reshape(D, S).T)[None]
```

```python
from contextlib import ExitStack

import numpy as np
import concourse.bass as bass
from concourse import mybir

F32 = mybir.dt.float32
F32R = mybir.dt.float32r
U8 = mybir.dt.uint8
U32 = mybir.dt.uint32
ALU = mybir.AluOpType
ACT = mybir.ActivationFunctionType
AX_X = mybir.AxisListType.X

P = 128
D = 1024
S = 512
KT = D // P
UNIT = 2048
N_MEM = 256
XA_HEADS = 4
XA_HD = D // XA_HEADS
D_FF = 3 * D
DEPTH = 2
CONV_A, CONV_C, CONV_F = 4, 31, 3
POOL_WINDOWS = (2, 4, 8, 16)
EPS = 1e-6
GN_EPS = 64e-5
GRID_W = 64
HEAD = 64
RW = 512
WIN_COLS = 16
N_GROUPS, PER_GROUP = 4, 8
N_EXPERTS = N_GROUPS * PER_GROUP
D_EXPERT = 256
CHUNK = 64
BLOCKS = (2 * S + N_EXPERTS * (P - 1)) // P
LEVELS = 6
CONV_C_PE = 13



def _vector_names():
    names = [("ab_norm", "ab_norm", 0), ("a_conv_b", "a_conv_b", 0), ("gx_b", "a_gate_x_b", 0),
             ("ga_b", "a_gate_a_b", 0), ("lam", "a_lambda", 0), ("bg_b", "b_group_b", 0),
             ("b_scale", "b_scale", 0), ("c_norm", "c_norm", 0), ("c_b1", "c_b_pw1", 0),
             ("c_dw_b", "c_dw_b", 0), ("c_ln_g", "c_ln_g", 0), ("c_ln_b", "c_ln_b", 0),
             ("c_b2", "c_b_pw2", 0)]
    for l in range(DEPTH):
        names += [(f"xa_norm{l}", "xa_norm", l), (f"xa_mem_norm{l}", "xa_mem_norm", l),
                  (f"f_norm{l}", "f_norm", l), (f"f_dw_b{l}", "f_dw_b", l)]
    names += [("final", "final_norm", None)]
    names += [(n, n + "_2", 0) for n in
              ("norm1_g", "mu_prev", "mu_next", "w0_f", "w0_b", "a0_f", "a0_b", "k_k", "k_a",
               "r_k", "lnx_g", "lnx_b", "b_gate", "norm2_g")]
    return names


_WIDTH = {"bg_b": 512, "b_scale": 512, "c_b1": 2048, "mu_prev": 1920, "mu_next": 1920,
          "w0_f": 512, "w0_b": 512, "a0_f": 512, "a0_b": 512, "k_k": 512, "k_a": 512,
          "r_k": 512, "lnx_g": 512, "lnx_b": 512, "b_gate": 2048, "f_dw_b0": 3072,
          "f_dw_b1": 3072}


def _columns():
    at, n = {}, 0
    for key, _, _ in _vector_names():
        at[key] = n
        n += _WIDTH.get(key, 1024) // P
    for key, taps, width in (("a_conv_w", CONV_A, D), ("c_dw_w", CONV_C, D),
                             ("f_dw_w0", CONV_F, D_FF), ("f_dw_w1", CONV_F, D_FF)):
        at[key] = n
        n += taps * width // P
    for key in ("q_gain", "k_gain"):
        at[key] = n
        n += 1
    return at, n


def _plan():
    plan = [("ab_in", h) for h in range(8)] + [("pool_in", i) for i in range(2)]
    plan += [("ab_out_a", i) for i in range(4)] + [("ab_out_b", i) for i in range(2)]
    for l in range(DEPTH):
        if l == 1:
            plan += [("pw1", i) for i in range(8)] + [("pw2", i) for i in range(4)]
        plan += [(f"wk{l}", i) for i in range(4)] + [(f"wv{l}", i) for i in range(4)]
        plan += [(f"wq{l}", i) for i in range(4)] + [(f"wo{l}", i) for i in range(4)]
        for p in range(3):
            plan += [(f"up{l}", 8 * p + i) for i in range(8)] + [(f"down{l}", 4 * p + i) for i in range(4)]
    plan += [("lora", 0), ("lora", 1)]
    for t in range(4):
        plan += [("rkvg", 2 * t), ("rkvg", 2 * t + 1)]
    plan += [("na_v", i) for i in range(2)] + [("na_qk", i) for i in range(4)]
    for out_w, gate in (("o_rwkv", "gate_a"), ("o_na", "gate_b")):
        for i in range(2):
            plan += [(out_w, i), (gate, 2 * i), (gate, 2 * i + 1)]
    plan += [("w_out2", i) for i in range(4)] + [("router", 0)]
    return plan


def _consts():
    p = np.arange(P)
    c = {"ident": np.eye(P), "head_ones": (p[:, None] // HEAD == p[None, :] // HEAD)}
    t = np.arange(16)
    for g, w in enumerate(POOL_WINDOWS):
        c[f"pool{g}"] = np.broadcast_to(1.0 / np.minimum(t + 1, w), (P, 16))
    col = np.arange(GRID_W)
    start = np.clip(col - WIN_COLS // 2, 0, GRID_W - WIN_COLS)
    inside = (col[None, :] >= start[:, None]) & (col[None, :] < start[:, None] + WIN_COLS)
    c["na_mask"] = np.where(inside[p % GRID_W], 0.0, -1e30)
    c["eps"] = np.full((P, 1), EPS)
    c["gn_eps"] = np.full((P, 1), GN_EPS)
    c["kk_eps"] = np.full((P, 1), 1e-12)
    c["ones"] = np.ones((P, P))
    c["seg8"] = np.broadcast_to((np.arange(32) % 8 != 0), (P, 32))
    c["seg4"] = np.broadcast_to((np.arange(16) % 4 != 0), (P, 16))
    return {k: np.ascontiguousarray(v, np.float32) for k, v in c.items()}


def _rwkv_consts():
    p = np.arange(P)
    t, s = p[:, None], p[None, :]
    same = t // CHUNK == s // CHUNK
    c = {"ident2": (t % HEAD == np.arange(HEAD)[None, :])}
    c["strict0"], c["incl0"] = same & (t > s), same & (t >= s)
    c["strict1"], c["incl1"] = same & (t < s), same & (t <= s)
    c["reset"] = np.broadcast_to(np.arange(S) % CHUNK != 0, (P, S))
    return {k: np.ascontiguousarray(v, np.float32) for k, v in c.items()}


def _expert_consts():
    p = np.arange(P)
    c = {"before": p[:, None] < p[None, :], "one32": np.ones((P, 32)),
         "block": np.broadcast_to(np.arange(BLOCKS), (P, BLOCKS)),
         "row": p[:, None] + P * np.arange(3)[None, :],
         "token": p[:, None] + P * np.arange(4)[None, :]}
    return {k: np.ascontiguousarray(v, np.float32) for k, v in c.items()}


def _level_masks():
    t, s = np.arange(P)[:, None], np.arange(P)[None, :]
    masks = []
    for l in range(LEVELS):
        half = 1 << l
        block = (t // (2 * half) == s // (2 * half)) & (t // half > s // half)
        masks += [block, block.T]
    return np.ascontiguousarray(np.stack(masks, axis=1).astype(np.float32))


def _places(arrays):
    at, n = {}, 0
    for k, v in arrays.items():
        at[k] = (n, v.shape[1])
        n += v.shape[1]
    return at, n



class Queue:

    def __init__(self, eng, sem):
        self.eng, self.sem, self.count, self.seen = eng, sem, 0, {}

    def wait(self, *tokens):
        for token in tokens:
            if token is None:
                continue
            sem, value = token
            if value > 0 and self.seen.get(sem.name, 0) < value:
                self.eng.wait_ge(sem, value)
                self.seen[sem.name] = value

    def done(self, instruction):
        instruction.then_inc(self.sem, 1)
        self.count += 1
        return (self.sem, self.count)

    def last(self):
        return (self.sem, self.count)


class Loader:

    def __init__(self, queue, sem):
        self.queue, self.sem, self.count = queue, sem, 0

    def load(self, dst, src, *after):
        self.queue.wait(*after)
        self.queue.eng.dma_start(dst, src).then_inc(self.sem, 16)
        self.count += 16
        return (self.sem, self.count)

    def indirect(self, dst, dst_rows, src, src_rows, *after):
        self.queue.wait(*after)
        offset = lambda rows: None if rows is None else bass.IndirectOffsetOnAxis(ap=rows, axis=0)
        self.queue.eng.indirect_dma_start(dst, offset(dst_rows), src, offset(src_rows)).then_inc(self.sem, 16)
        self.count += 16
        return (self.sem, self.count)


class Arena:

    def __init__(self, nc, stack):
        self.nc, self.stack = nc, stack

    def sb(self, name, shape, dt=F32):
        return self.stack.enter_context(self.nc.sbuf_tensor(name, shape, dt))


def build(nc, stream, vectors, consts, rconsts, x_in, mem_in, gates_w, group_w, lora_w,
          router_b, bias_na, level_masks, expert_rows, econsts, out, x_spill, y_spill, h_rows, y_rows, slot_table):
    with ExitStack() as stack:
        def sb(name, shape, dt=F32):
            return stack.enter_context(nc.sbuf_tensor(name, shape, dt))

        def sem(name):
            return stack.enter_context(nc.semaphore(name))

        pe = Queue(nc.tensor, sem("pe_done"))
        act = Queue(nc.scalar, sem("act_done"))
        dve = Queue(nc.vector, sem("dve_done"))
        pool = Queue(nc.gpsimd, sem("pool_done"))
        sp = Queue(nc.sync, sem("sp_unused"))
        V, A, T, G = dve.eng, act.eng, pe.eng, pool.eng

        x = sb("x", [P, KT, S])
        xg_hi = sb("xg_hi", [P, KT, S], F32R)
        xg_lo = sb("xg_lo", [P, KT, S], F32R)
        RAW, SLOTS = 2, 3
        raw = [sb(f"w_raw{i}", [P, UNIT]) for i in range(RAW)]
        w_hi = [sb(f"w_hi{i}", [P, UNIT], F32R) for i in range(SLOTS)]
        w_lo = [sb(f"w_lo{i}", [P, UNIT], F32R) for i in range(SLOTS)]
        square = sb("square", [P, 2, S])
        rstd = sb("rstd", [P, S])
        root = sb("root", [P, S])
        col, n_vec = _columns()
        vec = sb("vec_sb", [P, n_vec])
        c_at, n_const = _places(_consts())
        cst = sb("const_sb", [P, n_const])
        bank = [stack.enter_context(nc.psum_tensor(f"bank{i}", [P, S], F32)) for i in range(8)]

        def const(name):
            a, n = c_at[name]
            return cst[:, a:a + n]

        def vcol(name, i=0):
            return vec[:, col[name] + i:col[name] + i + 1]

        start = Loader(sp, sem("start_loads"))
        start.load(vec[:, :], vectors)
        start.load(cst[:, :], consts)
        started = start.load(x[:, :, :], x_in)

        plan = _plan()
        raw_load = [Loader(sp, sem(f"w_raw{i}_load")) for i in range(RAW)]
        unit_done = {}
        unit_split = {}
        unit_loaded = {}
        taken = [0]

        def load_unit(n):
            before = unit_split[n - RAW] if n >= RAW else ()
            unit_loaded[n] = raw_load[n % RAW].load(raw[n % RAW][:, :], stream[n], *before)

        def split_unit(n):
            r, hi, lo = raw[n % RAW], w_hi[n % SLOTS], w_lo[n % SLOTS]
            free = unit_done.get(n - SLOTS)
            act.wait(unit_loaded[n], free)
            rounded = act.done(A.activation(hi[:, :], r[:, :], ACT.Copy))
            dve.wait(rounded, free)
            rest = dve.done(V.tensor_tensor(lo[:, :], r[:, :], hi[:, :].bitcast(F32), ALU.subtract))
            unit_split[n] = (rounded, rest)
            if n + RAW < len(plan):
                load_unit(n + RAW)

        def take(name, i=0):
            n = taken[0]
            assert plan[n] == (name, i), (plan[n], name, i)
            taken[0] += 1
            for m in range(n, min(n + SLOTS, len(plan))):
                if m not in unit_split and (m < SLOTS or m - SLOTS in unit_done):
                    split_unit(m)
            return n

        def unit(n, cols):
            return [w[n % SLOTS][:, :].rearrange("p (k c) -> p k c", c=cols) for w in (w_hi, w_lo)]

        for n in range(RAW):
            load_unit(n)

        bank_free = [[None]] * 8
        turn = [0]

        def take_bank():
            b = turn[0]
            turn[0] = (b + 1) % 7
            assert bank_free[b] is not None, "bank still in use"
            pe.wait(*bank_free[b])
            bank_free[b] = None
            return b

        def free_bank(b, *readers):
            bank_free[b] = list(readers)

        def matmul(out_ap, lhsT, rhs, first=True, last=True, **kw):
            return T.matmul(out_ap, lhsT, rhs, start=first, stop=last, skip_group_check=True, **kw)

        def split_matmul(out_ap, l_hi, l_lo, r_hi, r_lo, first, last):
            matmul(out_ap, l_hi, r_hi, first, False)
            matmul(out_ap, l_hi, r_lo, False, False)
            return matmul(out_ap, l_lo, r_hi, False, last)

        class Acts:

            def __init__(self, hi, lo, tiles):
                self.hi, self.lo, self.ready = hi, lo, [()] * tiles

        xg = Acts(xg_hi, xg_lo, KT)

        def project(n, cols, c, acts, tiles, b, width=S, first=True, last=True, k0=0):
            hi, lo = unit(n, cols)
            pe.wait(*unit_split[n])
            for i, k in enumerate(tiles):
                pe.wait(*acts.ready[k])
                mm = split_matmul(bank[b][:, 0:width], hi[:, i, c * P:(c + 1) * P],
                                  lo[:, i, c * P:(c + 1) * P], acts.hi[:, k, :], acts.lo[:, k, :],
                                  first and i == 0, last and i == len(tiles) - 1)
            token = pe.done(mm)
            unit_done[n] = token
            return token

        def split_act(acts, k, value, *after):
            act.wait(*after)
            hi = act.done(A.activation(acts.hi[:, k, :], value, ACT.Copy))
            dve.wait(hi, *after)
            lo = dve.done(V.tensor_tensor(acts.lo[:, k, :], value, acts.hi[:, k, :].bitcast(F32), ALU.subtract))
            acts.ready[k] = (hi, lo)
            return hi, lo

        square_read = [None, None]
        norm_state = {}

        def norm_tile(j, gain, x_ready, mean_only=False):
            xg_free = norm_state["xg_free"]
            act.wait(x_ready, xg_free)
            if gain is not None:
                hi = act.done(A.activation(xg_hi[:, j, :], x[:, j, :], ACT.Identity, scale=vcol(gain, j)))
            act.wait(square_read[j % 2])
            sq = act.done(A.activation(square[:, j % 2, :], x[:, j, :], ACT.Square))
            if gain is not None:
                dve.wait(hi, x_ready, xg_free)
                lo = dve.done(V.scalar_tensor_tensor(out=xg_lo[:, j, :], in0=x[:, j, :], scalar=vcol(gain, j),
                                                     in1=xg_hi[:, j, :].bitcast(F32), op0=ALU.mult,
                                                     op1=ALU.subtract))
                xg.ready[j] = (hi, lo)
            norm_state["todo"].append((j, sq))

        def norm_sums(keep=0):
            while len(norm_state["todo"]) > keep:
                j, sq = norm_state["todo"].pop(0)
                pe.wait(sq, started)
                if j == 0:
                    pe.wait(*bank_free[7])
                square_read[j % 2] = pe.done(matmul(bank[7][:, :], const("ones"), square[:, j % 2, :],
                                                    j == 0, j == KT - 1))

        def norm_begin():
            norm_state["xg_free"] = pe.last()
            norm_state["todo"] = []

        def norm_end():
            norm_sums()
            act.wait(square_read[(KT - 1) % 2], norm_state.get("rstd_read"))
            rooted = act.done(A.activation(root[:, :], bank[7][:, :], ACT.Sqrt, scale=1.0 / D, bias=const("eps")))
            bank_free[7] = [rooted]
            dve.wait(rooted)
            norm_state["rstd"] = dve.done(V.reciprocal(rstd[:, :], root[:, :]))
            norm_state["rstd_read"] = None
            return norm_state["rstd"]

        def add_to_x(j, b, mm, bias=None):
            dve.wait(mm)
            if bias is None:
                token = dve.done(V.tensor_tensor(x[:, j, :], bank[b][:, :], x[:, j, :], ALU.add))
            else:
                token = dve.done(V.scalar_tensor_tensor(out=x[:, j, :], in0=bank[b][:, :], scalar=bias,
                                                        in1=x[:, j, :], op0=ALU.add, op1=ALU.add))
            free_bank(b, token)
            return token

        def phase_wait():
            ends = [pe.last(), act.last(), dve.last()]
            for q in (act, dve, pe, pool):
                q.wait(*ends)
            return ends

        def scaled_by_rstd(dst, b, mm, *after):
            dve.wait(mm, norm_state["rstd"], *after)
            token = dve.done(V.tensor_tensor(dst, bank[b][:, :], rstd[:, :], ALU.mult))
            free_bank(b, token)
            return token

        def stt(out_ap, in0, scalar, in1, op0, op1, *after):
            dve.wait(*after)
            return dve.done(V.scalar_tensor_tensor(out=out_ap, in0=in0, scalar=scalar, in1=in1, op0=op0, op1=op1))

        def tt(out_ap, a, b_ap, op, *after):
            dve.wait(*after)
            return dve.done(V.tensor_tensor(out_ap, a, b_ap, op))

        def ts(out_ap, a, s1, s2, op0, op1, *after):
            dve.wait(*after)
            if s2 is None:
                return dve.done(V.tensor_scalar(out_ap, a, s1, None, op0))
            return dve.done(V.tensor_scalar(out_ap, a, s1, s2, op0, op1))

        def activate(out_ap, a, func, *after, **kw):
            act.wait(*after)
            return act.done(A.activation(out_ap, a, func, **kw))

        def copy(engine, out_ap, a, *after):
            engine.wait(*after)
            if engine is act:
                return act.done(A.activation(out_ap, a, ACT.Copy))
            return engine.done(engine.eng.tensor_copy(out_ap, a))

        def causal_taps(dst, src, weight, taps, ready):
            k_last = taps[0]
            for k in taps[1]:
                s = k_last - k
                ready = stt(dst[:, s:], src[:, 0:S - s], weight(k), dst[:, s:], ALU.mult, ALU.add, ready)
            return ready

        def out_projection(names, acts, tiles_of, hook=None, bias=None):
            for name, n_units, cols in names:
                for i in range(n_units):
                    n = take(name, i)
                    for c in range(cols // P):
                        j = i * cols // P + c
                        b = take_bank()
                        mm = project(n, cols, c, acts, tiles_of[name], b)
                        token = add_to_x(j, b, mm, bias(j) if bias and name == names[-1][0] else None)
                        if hook and name == names[-1][0]:
                            norm_sums(0)
                            hook(j, token)

        def next_norm(gain):
            def hook(j, token):
                if j == 0:
                    norm_begin_late()
                norm_tile(j, gain, token)
            return hook

        def norm_begin_late():
            norm_state["xg_free"] = norm_state["xg_last"]
            norm_state["todo"] = []

        def mixer():
            for q in (act, dve, pe, pool):
                q.wait(started)
            norm_begin()
            for j in range(KT):
                norm_tile(j, "ab_norm", started)
                norm_sums(1)
            norm_end()

            with ExitStack() as ph:
                ar = Arena(nc, ph)
                y_hi, y_lo = ar.sb("ab_y_hi", [P, KT, S], F32R), ar.sb("ab_y_lo", [P, KT, S], F32R)
                xr = ar.sb("ab_xr", [P, 2, S])
                zr = ar.sb("ab_zr", [P, 2, S])
                gated = ar.sb("ab_gated", [P, 4, S])
                ga = ar.sb("ab_ga", [P, 4, S])
                gate = ar.sb("ab_gate", [P, 4, S])
                tmp = [ar.sb(f"ab_tmp{i}", [P, S]) for i in range(3)]
                gw = ar.sb("ab_gate_w", [P, 2, 2, P])
                sp8 = ar.sb("ab_decay", [P, 4 * KT])
                pool_w = ar.sb("ab_group_w", [P, 4, P])
                y = Acts(y_hi, y_lo, KT)
                gw_load = [Loader(sp, sem(f"ab_gate_w{i}")) for i in range(2)]
                group_loaded = Loader(sp, sem("ab_group_w_load")).load(pool_w[:, :, :], group_w)

                lam = vec[:, col["lam"]:col["lam"] + KT]
                e_, n_, s_, q_ = [sp8[:, i * KT:(i + 1) * KT] for i in range(4)]
                t0 = ts(n_, lam, -1.0, None, ALU.mult, None)
                t1 = tt(s_, lam, n_, ALU.max, t0)
                t2 = activate(e_, s_, ACT.Exp, t1, scale=-1.0)
                t3 = ts(s_, e_, 2.0, None, ALU.add, None, t2)
                dve.wait(t3)
                t3 = dve.done(V.reciprocal(q_, s_))
                t3 = tt(s_, e_, q_, ALU.mult, t3)
                t3 = tt(q_, s_, s_, ALU.mult, t3)
                t4 = ts(e_, q_, 1.0 / 17, 1.0 / 15, ALU.mult, ALU.add, t3)
                for k in (13, 11, 9, 7, 5, 3, 1):
                    t4 = tt(e_, e_, q_, ALU.mult, t4)
                    t4 = ts(e_, e_, 1.0 / k, None, ALU.add, None, t4)
                t4 = tt(e_, e_, s_, ALU.mult, t4)
                t5 = ts(n_, n_, 0.0, None, ALU.max, None)
                t4 = stt(e_, e_, 2.0, n_, ALU.mult, ALU.add, t4, t5)
                c_pos = ts(s_, e_, 8.0, None, ALU.mult, None, t4)
                c_neg = ts(q_, e_, -8.0, None, ALU.mult, None, t4)
                decay_pos, decay_neg = s_, q_

                gate_w_read = [None, None]
                gated_free = [None] * 4
                xr_read = [None, None]
                for half in range(2):
                    gate_ready, gated_ready, ga_ready = [None] * 4, [None] * 4, [None] * 4
                    for h4 in range(4):
                        h = 4 * half + h4
                        i = h % 2
                        gw_loaded = gw_load[i].load(gw[:, i, :, :], gates_w[:, h, :, :], gate_w_read[i])
                        n = take("ab_in", h)
                        b_rec = take_bank()
                        mm = project(n, 2 * P, 1, xg, range(KT), b_rec)
                        zr_ready = scaled_by_rstd(zr[:, i, :], b_rec, mm)
                        b_gate = take_bank()
                        mm = project(n, 2 * P, 0, xg, range(KT), b_gate)
                        w = lambda k, h=h: vcol("a_conv_w", CONV_A * h + k)
                        ready = activate(xr[:, i, :], zr[:, i, :], ACT.Identity, zr_ready, xr_read[i],
                                         scale=w(CONV_A - 1), bias=vcol("a_conv_b", h))
                        ready = causal_taps(xr[:, i, :], zr[:, i, :], w, (CONV_A - 1, range(CONV_A - 1)), ready)
                        gate_ready[h4] = scaled_by_rstd(gate[:, h4, :], b_gate, mm, gated_free[h4])
                        pe.wait(gw_loaded, ready)
                        b_gx = take_bank()
                        mm_gx = pe.done(matmul(bank[b_gx][:, :], gw[:, i, 0, :], xr[:, i, :]))
                        b_ga = take_bank()
                        mm_ga = pe.done(matmul(bank[b_ga][:, :], gw[:, i, 1, :], xr[:, i, :]))
                        gate_w_read[i] = mm_ga
                        gx = activate(gated[:, h4, :], bank[b_gx][:, :], ACT.Sigmoid, mm_gx, gated_free[h4],
                                      bias=vcol("gx_b", h))
                        free_bank(b_gx, gx)
                        ga_ready[h4] = activate(ga[:, h4, :], bank[b_ga][:, :], ACT.Sigmoid, mm_ga, bias=vcol("ga_b", h))
                        free_bank(b_ga, ga_ready[h4])
                        gated_ready[h4] = tt(gated[:, h4, :], gated[:, h4, :], xr[:, i, :], ALU.mult, gx, ready)
                        xr_read[i] = gated_ready[h4]
                    for h4 in range(4):
                        h = 4 * half + h4
                        th = activate(tmp[0][:, :], ga[:, h4, :], ACT.Tanh, ga_ready[h4], dve.last(), c_pos, c_neg,
                                      scale=decay_pos[:, h:h + 1])
                        a_ready = activate(ga[:, h4, :], ga[:, h4, :], ACT.Exp, th, scale=decay_neg[:, h:h + 1])
                        m = tt(tmp[1][:, :], ga[:, h4, :], ga[:, h4, :], ALU.mult, a_ready)
                        m = stt(tmp[1][:, :], tmp[1][:, :], 1.0, tmp[0][:, :], ALU.add, ALU.mult, m)
                        r = activate(tmp[2][:, :], tmp[1][:, :], ACT.Sqrt, m)
                        bx = tt(gated[:, h4, :], gated[:, h4, :], tmp[2][:, :], ALU.mult, r, gated_ready[h4])
                        dve.wait(bx)
                        scan = dve.done(V.tensor_tensor_scan(tmp[1][:, :], ga[:, h4, :], gated[:, h4, :], 0.0,
                                                             ALU.mult, ALU.add))
                        ge = activate(gate[:, h4, :], gate[:, h4, :], ACT.Gelu_apprx_tanh, gate_ready[h4])
                        ya = tt(gate[:, h4, :], gate[:, h4, :], tmp[1][:, :], ALU.mult, ge, scan)
                        hi, lo = split_act(y, h, gate[:, h4, :], ya)
                        gated_free[h4] = lo
                y_b = Acts(y_hi, y_lo, KT)
                a_done = None
                pooled = []
                u_sb, s_sb = ga, gated
                for i in range(2):
                    n = take("pool_in", i)
                    for c in range(2):
                        g = 2 * i + c
                        b = take_bank()
                        mm = project(n, 2 * P, c, xg, range(KT), b)
                        norm_state["xg_last"] = mm
                        u = scaled_by_rstd(u_sb[:, g, :], b, mm, act.last())
                        src, ready = u_sb[:, g, :], u
                        scratch = [s_sb[:, g, :], tmp[0][:, :]] if g % 2 else [s_sb[:, g, :], tmp[1][:, :]]
                        steps = g + 1
                        for st in range(steps):
                            dst = scratch[(steps - 1 - st) % 2]
                            sh = 1 << st
                            ready = tt(dst[:, sh:], src[:, sh:], src[:, 0:S - sh], ALU.add, ready)
                            ready = copy(dve, dst[:, 0:sh], src[:, 0:sh], ready)
                            src = dst
                        w_ = POOL_WINDOWS[g]
                        fix = tt(tmp[2][:, 0:16], src[:, 0:16], const(f"pool{g}"), ALU.mult, ready)
                        ready = stt(src, src, 1.0 / w_, u_sb[:, g, :], ALU.mult, ALU.subtract, fix)
                        ready = tt(src[:, 0:16], tmp[2][:, 0:16], u_sb[:, g, 0:16], ALU.subtract, ready)
                        pe.wait(group_loaded, ready)
                        b = take_bank()
                        mm = pe.done(matmul(bank[b][:, :], pool_w[:, g, :], src))
                        ready = ts(u_sb[:, g, :], bank[b][:, :], vcol("bg_b", g), vcol("b_scale", g), ALU.add,
                                   ALU.mult, mm)
                        free_bank(b, ready)
                        pooled.append(ready)
                for i in range(4):
                    n = take("ab_out_a", i)
                    for c in range(2):
                        b = take_bank()
                        mm = project(n, 2 * P, c, y, range(KT), b)
                        add_to_x(2 * i + c, b, mm)
                y_a_read = pe.last()
                for g in range(4):
                    act.wait(y_a_read)
                    dve.wait(y_a_read)
                    split_act(y, g, u_sb[:, g, :], pooled[g])
                out_projection([("ab_out_b", 2, S)], y, {"ab_out_b": range(4)}, next_norm("xa_norm0"))
                norm_end()

        def cross_attention(l):
            phase_wait()
            with ExitStack() as ph:
                ar = Arena(nc, ph)
                o_hi, o_lo = ar.sb(f"xa{l}_o_hi", [P, KT, S], F32R), ar.sb(f"xa{l}_o_lo", [P, KT, S], F32R)
                o = Acts(o_hi, o_lo, KT)
                kT = ar.sb(f"xa{l}_k", [P, KT, N_MEM])
                v = ar.sb(f"xa{l}_v", [P, 2, D])
                with ExitStack() as inner:
                    ar2 = Arena(nc, inner)
                    mem = ar2.sb(f"xa{l}_mem", [P, 2, N_MEM])
                    m_hi = ar2.sb(f"xa{l}_m_hi", [P, KT, N_MEM], F32R)
                    m_lo = ar2.sb(f"xa{l}_m_lo", [P, KT, N_MEM], F32R)
                    m_rstd = ar2.sb(f"xa{l}_m_rstd", [P, N_MEM])
                    m_col = ar2.sb(f"xa{l}_m_rstd_col", [P, 2])
                    m = Acts(m_hi, m_lo, KT)
                    mem_load = [Loader(sp, sem(f"xa{l}_mem_load{i}")) for i in range(2)]
                    b_sum = take_bank()
                    mem_read = [(pe.last(), act.last(), dve.last())] * 2
                    for k in range(KT):
                        i = k % 2
                        loaded = mem_load[i].load(mem[:, i, :], mem_in[:, k, :], *mem_read[i])
                        hi = activate(m_hi[:, k, :], mem[:, i, :], ACT.Identity, loaded,
                                      scale=vcol(f"xa_mem_norm{l}", k))
                        lo = stt(m_lo[:, k, :], mem[:, i, :], vcol(f"xa_mem_norm{l}", k),
                                 m_hi[:, k, :].bitcast(F32), ALU.mult, ALU.subtract, hi)
                        m.ready[k] = (hi, lo)
                        sq = activate(square[:, i, 0:N_MEM], mem[:, i, :], ACT.Square, square_read[i])
                        mem_read[i] = (sq, lo)
                        pe.wait(sq)
                        square_read[i] = pe.done(matmul(bank[b_sum][:, 0:N_MEM], const("ones"),
                                                        square[:, i, 0:N_MEM], k == 0, k == KT - 1))
                    r = activate(m_rstd[:, :], bank[b_sum][:, 0:N_MEM], ACT.Sqrt, square_read[1],
                                 scale=1.0 / D, bias=const("eps"))
                    free_bank(b_sum, r)
                    dve.wait(r)
                    m_ready = dve.done(V.reciprocal(m_rstd[:, :], m_rstd[:, :]))
                    b_col = take_bank()
                    pe.wait(m_ready)
                    for t in range(2):
                        mm = matmul(bank[b_col][:, t:t + 1], m_rstd[0:1, t * P:(t + 1) * P],
                                    const("ident")[0:1, 0:1])
                    mm = pe.done(mm)
                    m_col_ready = copy(dve, m_col[:, :], bank[b_col][:, 0:2], mm)
                    free_bank(b_col, m_col_ready)
                    for i in range(4):
                        n = take(f"wk{l}", i)
                        for c in range(2):
                            j = 2 * i + c
                            b = take_bank()
                            mm = project(n, 2 * P, c, m, range(KT), b, width=N_MEM)
                            k_ready = tt(kT[:, j, :], bank[b][:, 0:N_MEM], m_rstd[:, :], ALU.mult, mm, m_ready)
                            free_bank(b, k_ready)
                    for i in range(4):
                        n = take(f"wv{l}", i)
                        hi, lo = unit(n, 2 * P)
                        pe.wait(*unit_split[n])
                        for t in range(2):
                            b = take_bank()
                            for k in range(KT):
                                rows = slice(t * P, (t + 1) * P)
                                mm = split_matmul(bank[b][:, 0:2 * P], m_hi[:, k, rows], m_lo[:, k, rows],
                                                  hi[:, k, :], lo[:, k, :], k == 0, k == KT - 1)
                            mm = pe.done(mm)
                            unit_done[n] = mm
                            v_ready = ts(v[:, t, i * 2 * P:(i + 1) * 2 * P], bank[b][:, 0:2 * P],
                                         m_col[:, t:t + 1], None, ALU.mult, None, mm, m_col_ready)
                            free_bank(b, v_ready)
                    inner_end = [pe.last(), act.last(), dve.last()]
                q_sb = ar.sb(f"xa{l}_q", [P, 2, 2, S])
                prob = ar.sb(f"xa{l}_p", [P, 2, 2, N_MEM])
                pT = ar.sb(f"xa{l}_pT", [P, 2, S])
                stat = ar.sb(f"xa{l}_stat", [P, 2, 8])
                act.wait(*inner_end)
                dve.wait(*inner_end)
                qh_read = [None, None]
                prob_read = [None, None]
                pT_read = None

                def queries(h):
                    n = take(f"wq{l}", h)
                    for c in range(2):
                        b = take_bank()
                        mm = project(n, 2 * P, c, xg, range(KT), b)
                        ready = scaled_by_rstd(q_sb[:, h % 2, c, :], b, mm, qh_read[h % 2])
                    return ready

                q_ready = queries(0)
                for h in range(XA_HEADS):
                    q_now = q_ready
                    b_s = [take_bank(), take_bank()]
                    pe.wait(q_now, k_ready)
                    scored = [None, None]
                    for pair in range(2):
                        for u in range(2):
                            qt = 2 * pair + u
                            for c in range(2):
                                mm = matmul(bank[b_s[pair]][:, u * N_MEM:(u + 1) * N_MEM],
                                            q_sb[:, h % 2, c, qt * P:(qt + 1) * P], kT[:, 2 * h + c, :],
                                            c == 0, c == 1)
                        scored[pair] = pe.done(mm)
                    qh_read[h % 2] = pe.last()
                    if h + 1 < XA_HEADS:
                        q_ready = queries(h + 1)
                    else:
                        norm_state["xg_last"] = unit_done[taken[0] - 1]
                    b_t = [take_bank(), take_bank()]
                    for pair in range(2):
                        st = stat[:, pair, :]
                        sc = bank[b_s[pair]][:, :].rearrange("p (u m) -> p u m", u=2)
                        dve.wait(scored[pair], prob_read[pair])
                        top = dve.done(V.tensor_reduce(st[:, 0:2], sc, AX_X, ALU.max))
                        top = ts(st[:, 2:4], st[:, 0:2], -XA_HD ** -0.5, None, ALU.mult, None, top)
                        for u in range(2):
                            e = activate(prob[:, pair, u, :], sc[:, u, :], ACT.Exp, top, prob_read[pair],
                                         scale=XA_HD ** -0.5, bias=st[:, 2 + u:3 + u],
                                         accum_out=st[:, 4 + u:5 + u])
                        free_bank(b_s[pair], e)
                        dve.wait(e)
                        r = dve.done(V.reciprocal(st[:, 6:8], st[:, 4:6]))
                        for u in range(2):
                            r2 = ts(prob[:, pair, u, :], prob[:, pair, u, :], st[:, 6 + u:7 + u], None,
                                    ALU.mult, None, r)
                        pe.wait(r2)
                        for u in range(2):
                            for t in range(2):
                                qt = 2 * pair + u
                                mm = T.transpose(bank[b_t[t]][:, qt * P:(qt + 1) * P],
                                                 prob[:, pair, u, t * P:(t + 1) * P], const("ident"))
                        prob_read[pair] = pe.done(mm)
                    for t in range(2):
                        p_ready = copy((act, dve)[t], pT[:, t, :], bank[b_t[t]][:, :], pe.last(), pT_read)
                        free_bank(b_t[t], p_ready)
                        pe.wait(p_ready)
                    for c in range(2):
                        j = 2 * h + c
                        b = take_bank()
                        for t in range(2):
                            pe.wait(v_ready)
                            mm = matmul(bank[b][:, :], v[:, t, j * P:(j + 1) * P], pT[:, t, :], t == 0, t == 1)
                        mm = pe.done(mm)
                        pT_read = mm
                        act.wait(mm)
                        hi = act.done(A.activation(o_hi[:, j, :], bank[b][:, :], ACT.Copy))
                        lo = tt(o_lo[:, j, :], bank[b][:, :], o_hi[:, j, :].bitcast(F32), ALU.subtract, hi)
                        o.ready[j] = (hi, lo)
                        free_bank(b, hi, lo)
                out_projection([(f"wo{l}", 4, 2 * P)], o, {f"wo{l}": range(KT)}, next_norm(f"f_norm{l}"))
                norm_end()

        def conv_ffn(l, next_gain):
            phase_wait()
            with ExitStack() as ph:
                ar = Arena(nc, ph)
                hid = [Acts(ar.sb(f"f{l}_h_hi{i}", [P, KT, S], F32R), ar.sb(f"f{l}_h_lo{i}", [P, KT, S], F32R), KT)
                       for i in range(2)]
                z = ar.sb(f"f{l}_z", [P, 2, S])
                g = ar.sb(f"f{l}_g", [P, 2, S])
                u = ar.sb(f"f{l}_u", [P, 2, S])
                free = [None, None]
                hid_free = [None, None]
                for p in range(3):
                    h = hid[p % 2]
                    for j in range(KT):
                        i = j % 2
                        ch = KT * p + j
                        n = take(f"up{l}", ch)
                        b_g = take_bank()
                        mm_g = project(n, 2 * P, 0, xg, range(KT), b_g)
                        b_u = take_bank()
                        mm_u = project(n, 2 * P, 1, xg, range(KT), b_u)
                        norm_state["xg_last"] = mm_u
                        w = lambda k, ch=ch: vcol(f"f_dw_w{l}", CONV_F * ch + k)
                        ready = scaled_by_rstd(z[:, i, :], b_g, mm_g, free[i])
                        ready = activate(g[:, i, :], z[:, i, :], ACT.Identity, ready, free[i],
                                         scale=w(CONV_F - 1), bias=vcol(f"f_dw_b{l}", ch))
                        ready = causal_taps(g[:, i, :], z[:, i, :], w, (CONV_F - 1, range(CONV_F - 1)), ready)
                        ge = activate(g[:, i, :], g[:, i, :], ACT.Gelu_apprx_tanh, ready)
                        u_ready = scaled_by_rstd(u[:, i, :], b_u, mm_u, free[i])
                        prod = tt(u[:, i, :], u[:, i, :], g[:, i, :], ALU.mult, ge, u_ready)
                        hi, lo = split_act(h, j, u[:, i, :], prod, hid_free[p % 2])
                        free[i] = lo
                    for i in range(4):
                        n = take(f"down{l}", 4 * p + i)
                        for c in range(2):
                            j = 2 * i + c
                            b = take_bank()
                            mm = project(n, 2 * P, c, h, range(KT), b)
                            token = add_to_x(j, b, mm)
                            if p == 2:
                                if j == 0:
                                    norm_begin_late()
                                norm_sums(0)
                                norm_tile(j, next_gain, token)
                    hid_free[p % 2] = pe.last()
                norm_end()

        def conformer():
            phase_wait()
            with ExitStack() as ph:
                ar = Arena(nc, ph)
                h_all = ar.sb("c_h", [P, KT, S])
                s_hi, s_lo = ar.sb("c_s_hi", [P, KT, S], F32R), ar.sb("c_s_lo", [P, KT, S], F32R)
                s = Acts(s_hi, s_lo, KT)
                t1 = ar.sb("c_t1", [P, 2, S])
                t2 = ar.sb("c_t2", [P, 2, S])
                mu = ar.sb("c_mu", [P, S])
                diag = ar.sb("c_diag", [P, 4, P])
                free = [None, None]
                diag_read = [None] * 4
                n_diag = 0
                h_ready = [None] * KT
                for j in range(KT):
                    i = j % 2
                    n = take("pw1", j)
                    b1 = take_bank()
                    mm1 = project(n, 2 * P, 0, xg, range(KT), b1)
                    b2 = take_bank()
                    mm2 = project(n, 2 * P, 1, xg, range(KT), b2)
                    norm_state["xg_last"] = mm2
                    r2 = scaled_by_rstd(t2[:, i, :], b2, mm2, free[i])
                    r2 = activate(t2[:, i, :], t2[:, i, :], ACT.Sigmoid, r2, bias=vcol("c_b1", KT + j))
                    r1 = scaled_by_rstd(t1[:, i, :], b1, mm1, free[i])
                    r1 = stt(t1[:, i, :], t1[:, i, :], vcol("c_b1", j), t2[:, i, :], ALU.add, ALU.mult, r1, r2)
                    w = lambda k, j=j: vcol("c_dw_w", CONV_C * j + k)
                    last = activate(h_all[:, j, :], t1[:, i, :], ACT.Identity, r1,
                                    scale=w(CONV_C - 1), bias=vcol("c_dw_b", j))
                    b = take_bank()
                    order = list(range(CONV_C_PE))[::-1]
                    base = CONV_C - 1 - order[0]
                    for m, k in enumerate(order):
                        d = n_diag % 4
                        n_diag += 1
                        dg = activate(diag[:, d, :], const("ident"), ACT.Copy, diag_read[d], scale=w(k))
                        pe.wait(dg, r1)
                        sh = CONV_C - 1 - k
                        mm = matmul(bank[b][:, sh:], diag[:, d, :], t1[:, i, 0:S - sh], m == 0,
                                    m == len(order) - 1)
                        diag_read[d] = pe.done(mm)
                    ready = causal_taps(h_all[:, j, :], t1[:, i, :], w,
                                        (CONV_C - 1, range(CONV_C_PE, CONV_C - 1)), last)
                    ready = tt(h_all[:, j, base:], bank[b][:, base:], h_all[:, j, base:], ALU.add, diag_read[d],
                               ready)
                    free_bank(b, ready)
                    free[i] = ready
                    h_ready[j] = ready
                b = take_bank()
                for j in range(KT):
                    pe.wait(h_ready[j])
                    mm = matmul(bank[b][:, :], const("ones"), h_all[:, j, :], j == 0, j == KT - 1)
                mm = pe.done(mm)
                mean = activate(mu[:, :], bank[b][:, :], ACT.Copy, mm, scale=1.0 / D)
                free_bank(b, mean)
                b = take_bank()
                for j in range(KT):
                    h_ready[j] = tt(h_all[:, j, :], h_all[:, j, :], mu[:, :], ALU.subtract, mean)
                    sq = activate(square[:, j % 2, :], h_all[:, j, :], ACT.Square, h_ready[j], square_read[j % 2])
                    pe.wait(sq)
                    square_read[j % 2] = pe.done(matmul(bank[b][:, :], const("ones"), square[:, j % 2, :],
                                                        j == 0, j == KT - 1))
                rt = activate(mu[:, :], bank[b][:, :], ACT.Sqrt, pe.last(), dve.last(), scale=1.0 / D,
                              bias=const("eps"))
                free_bank(b, rt)
                dve.wait(rt)
                inv = dve.done(V.reciprocal(t1[:, 0, :], mu[:, :]))
                for j in range(KT):
                    r = stt(h_all[:, j, :], h_all[:, j, :], vcol("c_ln_g", j), t1[:, 0, :], ALU.mult, ALU.mult, inv)
                    r = activate(h_all[:, j, :], h_all[:, j, :], ACT.Silu, r, bias=vcol("c_ln_b", j))
                    split_act(s, j, h_all[:, j, :], r)
                out_projection([("pw2", 4, 2 * P)], s, {"pw2": range(KT)}, next_norm("xa_norm1"),
                               bias=lambda j: vcol("c_b2", j))
                norm_end()

        def final_norm():
            rstd_ready = norm_state["rstd"]
            norm_state["xg_free"] = norm_state["xg_last"]
            norm_state["todo"] = []
            for j in range(KT):
                token = stt(x[:, j, :], x[:, j, :], vcol("final", j), rstd[:, :], ALU.mult, ALU.mult, rstd_ready,
                            act.last())
                norm_tile(j, "norm1_g", token)
                norm_sums(1)
            norm_sums()
            dve.wait(dve.last())
            norm_end()

        def rstd_by_token(dst):
            b = take_bank()
            pe.wait(norm_state["rstd"])
            for t in range(4):
                mm = matmul(bank[b][:, t:t + 1], rstd[0:1, t * P:(t + 1) * P], const("ident")[0:1, 0:1])
            mm = pe.done(mm)
            token = copy(dve, dst, bank[b][:, 0:4], mm)
            free_bank(b, token)
            return token

        def inverse_root(dst, tmp_ap, b, mm, scale, eps, *after):
            r = activate(tmp_ap, bank[b][:, :], ACT.Sqrt, mm, *after, scale=scale, bias=const(eps))
            free_bank(b, r)
            dve.wait(r, *after)
            return dve.done(V.reciprocal(dst, tmp_ap))

        def rwkv():
            ends = phase_wait()
            spill = Loader(sp, sem("x_spill_store"))
            spilled = spill.load(x_spill, x[:, :, :], *ends)
            with ExitStack() as ph:
                ar = Arena(nc, ph)
                rc_at, n_rc = _places(_rwkv_consts())
                rc = ar.sb("rw_constants", [P, n_rc])
                masks = ar.sb("rw_level_masks", [P, 2 * LEVELS, P], U8)
                up_w = ar.sb("rw_lora_w", [P, 3, RW])
                small = ar.sb("rw_small", [P, 24])
                R, A_, B, K = [ar.sb(f"rw_{m}", [P, S]) for m in ("R", "A", "B", "K")]
                Bh, Kh, t3 = [ar.sb(f"rw_{m}", [P, S]) for m in ("Bh", "Kh", "t3")]
                tokV, tokB, tokK = [ar.sb(f"rw_tok_{m}", [P, 4, P]) for m in ("V", "B", "K")]
                GA = ar.sb("rw_lakv_a", [P, 2, 4, P])
                UW = ar.sb("rw_u_w", [P, 2, 4, P])
                LT, X, XT, U, Lrb, Lrk = [ar.sb(f"rw_{m}", [P, 2, 4, P]) for m in
                                          ("LT", "X", "XT", "U", "Lrb", "Lrk")]
                MT, N_ = ar.sb("rw_MT", [P, 8, HEAD]), ar.sb("rw_N", [P, 8, HEAD])
                St = ar.sb("rw_S", [P, 8, HEAD])
                t0, t1, t2 = square[:, 0, :], square[:, 1, :], root[:, :]
                wl, al, gl, r_, k_, v_, kk, ksum = [x[:, i, :] for i in range(8)]

                def rconst(name):
                    a, n = rc_at[name]
                    return rc[:, a:a + n]

                ld = Loader(sp, sem("rw_loads"))
                ld.load(rc[:, :], rconsts, *ends)
                masks_f32 = x[:, 3:6, :].rearrange("p a b -> p (a b)")
                ld.load(masks_f32, level_masks.rearrange("p m c -> p (m c)"), spilled)
                loaded = ld.load(up_w[:, :, :], lora_w)
                for q in (pe, act, dve, pool):
                    q.wait(loaded, spilled)
                masks_ready = copy(dve, masks[:, :, :].rearrange("p m c -> p (m c)"), masks_f32)
                dve.wait(masks_ready)
                omka = small[:, 0:4]
                mu0 = small[:, 4:19]
                c1 = ts(omka, vec[:, col["k_a"]:col["k_a"] + 4], -1.0, 1.0, ALU.mult, ALU.add)
                c2 = tt(mu0, vec[:, col["mu_prev"]:col["mu_prev"] + 15], vec[:, col["mu_next"]:col["mu_next"] + 15],
                        ALU.add)
                c2 = ts(mu0, mu0, -1.0, 1.0, ALU.mult, ALU.add, c2)

                def shifted(dst, n, c, m, *after):
                    b = take_bank()
                    mm = project(n, 2 * P, c, xg, range(KT), b)
                    z = scaled_by_rstd(t3[:, :], b, mm, dve.last(), *after)
                    d = ts(dst, t3[:, :], mu0[:, m:m + 1], None, ALU.mult, None, z, c2, *after)
                    d = stt(dst[:, 1:], t3[:, 0:S - 1], vcol("mu_prev", m), dst[:, 1:], ALU.mult, ALU.add, d)
                    return stt(dst[:, 0:S - 1], t3[:, 1:], vcol("mu_next", m), dst[:, 0:S - 1], ALU.mult,
                               ALU.add, d)

                n = take("lora", 0)
                z = shifted(wl, n, 0, 12)
                wl_ready = activate(wl, wl, ACT.Tanh, z)
                al_ready = shifted(al, n, 1, 13)
                n = take("lora", 1)
                z = shifted(gl, n, 0, 14)
                gl_ready = activate(gl, gl, ACT.Sigmoid, z)

                def transposed(dst_of, src, ready, engine, *after):
                    b = take_bank()
                    pe.wait(ready)
                    for t in range(4):
                        mm = T.transpose(bank[b][:, t * P:(t + 1) * P], src[:, t * P:(t + 1) * P], const("ident"))
                    mm = pe.done(mm)
                    token = copy(engine, dst_of, bank[b][:, :].rearrange("p (t c) -> p t c", t=4), mm, *after)
                    free_bank(b, token)
                    return token

                def four(ap):
                    return ap.unsqueeze(1).to_broadcast([P, 4, P])

                def quad(b):
                    return bank[b][:, :].rearrange("p (t c) -> p t c", t=4)

                store = Loader(sp, sem("ya_store"))
                y_stored = None
                for t in range(4):
                    prev = (pe.last(), act.last())
                    n = take("rkvg", 2 * t)
                    r_ready = shifted(r_, n, 0, t, *prev)
                    k_ready = shifted(k_, n, 1, 4 + t, *prev)
                    n = take("rkvg", 2 * t + 1)
                    v_ready = shifted(v_, n, 0, 8 + t, *prev)
                    norm_state["xg_last"] = pe.last()
                    kr = ts(kk, k_, vcol("k_k", t), None, ALU.mult, None, k_ready)
                    sq = activate(t0, kk, ACT.Square, kr)
                    b = take_bank()
                    pe.wait(sq)
                    mm = pe.done(matmul(bank[b][:, :], const("head_ones"), t0))
                    inv = inverse_root(t1, t2, b, mm, 1.0, "kk_eps")
                    kk_ready = tt(kk, kk, t1, ALU.mult, inv)
                    tokV_ready = transposed(tokV[:, :, :], v_, v_ready, act)
                    pe.wait(*bank_free[7])
                    for d, (w0, a0) in enumerate((("w0_f", "a0_f"), ("w0_b", "a0_b"))):
                        rows = slice(d * HEAD, (d + 1) * HEAD)
                        cols = slice(t * P, (t + 1) * P)
                        prior = pe.last()
                        b = take_bank()
                        pe.wait(wl_ready, al_ready)
                        mm = pe.done(matmul(bank[b][:, :], up_w[rows, 0, cols], wl[rows, :]))
                        lw = activate(t0, bank[b][:, :], ACT.Sigmoid, mm, kk_ready, dve.last(), bias=vcol(w0, t))
                        free_bank(b, lw)
                        b = take_bank()
                        mm = pe.done(matmul(bank[b][:, :], up_w[rows, 1, cols], al[rows, :]))
                        a_ready = activate(t1, bank[b][:, :], ACT.Sigmoid, mm, bias=vcol(a0, t))
                        free_bank(b, a_ready)
                        kd = ts(Kh[:, :], t1, vcol("k_a", t), omka[:, t:t + 1], ALU.mult, ALU.add, a_ready, c1, prior)
                        kd = tt(Kh[:, :], Kh[:, :], k_, ALU.mult, kd)
                        if d == 0:
                            ks = copy(dve, ksum, Kh[:, :], kd, prior)
                        else:
                            ks = tt(ksum, ksum, Kh[:, :], ALU.add, kd)
                        kka = tt(Bh[:, :], kk, t1, ALU.mult, kk_ready)
                        lw = ts(t0, t0, -float(np.exp(-0.5)), None, ALU.mult, None, lw)
                        dve.wait(lw)
                        F = dve.done(V.tensor_tensor_scan(t2, rconst("reset"), t0, 0.0, ALU.mult, ALU.add))
                        E = tt(t3[:, :], t2, t0, ALU.subtract, F)
                        ch = lambda ap: ap.rearrange("p (c t) -> p c t", t=CHUNK)
                        total = ch(t2)[:, :, CHUNK - 1:CHUNK].to_broadcast([P, 8, CHUNK])
                        rest = tt(ch(t0), total, ch(t2), ALU.subtract, E)
                        decay = small[:, 19:19 + 1]
                        if d == 0:
                            dR, dA, dH, ready = t2, t3[:, :], t0, rest
                        else:
                            ready = tt(ch(t1), total, ch(t3[:, :]), ALU.subtract, kka, rest)
                            dR, dA, dH = t1, t0, t3[:, :]
                        DC = dcol
                        dc_ready = activate(DC[:, :], ch(t2)[:, :, CHUNK - 1], ACT.Exp, F, dve.last())
                        e = activate(R[:, :], dR, ACT.Exp, ready, prior)
                        Rr = tt(R[:, :], R[:, :], r_, ALU.mult, e, r_ready)
                        e = activate(A_[:, :], dA, ACT.Exp, prior)
                        Ar = stt(A_[:, :], A_[:, :], -1.0, kk, ALU.mult, ALU.mult, e)
                        e = activate(B[:, :], dR, ACT.Exp, prior, scale=-1.0)
                        Kr = tt(K[:, :], B[:, :], Kh[:, :], ALU.mult, e)
                        Br = tt(B[:, :], B[:, :], Bh[:, :], ALU.mult, Kr)
                        e = activate(dH, dH, ACT.Exp)
                        Khr = tt(Kh[:, :], Kh[:, :], dH, ALU.mult, e)
                        Bhr = tt(Bh[:, :], Bh[:, :], dH, ALU.mult)
                        pool.wait(prior, dve.last(), act.last())
                        x_init = None
                        for m in (X, XT):
                            for par in range(2):
                                x_init = pool.done(G.tensor_copy(m[:, par, :, :], four(const("ident"))))
                        b = take_bank()
                        pe.wait(Ar)
                        for i in range(4):
                            mm = T.transpose(bank[b][:, i * P:(i + 1) * P], A_[:, i * P:(i + 1) * P], const("ident"))
                        mm = pe.done(mm)
                        for par in range(2):
                            ga_ready = copy(act, GA[:, par, :, HEAD:P], quad(b)[:, :, par * HEAD:(par + 1) * HEAD],
                                            mm, prior)
                        free_bank(b, ga_ready)
                        tokB_ready = transposed(tokB[:, :, :], Bh[:, :], Bhr, act, prior)
                        tokK_ready = transposed(tokK[:, :, :], Kh[:, :], Khr, act, prior)
                        pe.wait(Rr, Ar, Br, Kr)

                        def products(lhs, rhs):
                            found = []
                            for par in range(2):
                                b = take_bank()
                                rows = slice(par * HEAD, (par + 1) * HEAD)
                                for i in range(4):
                                    c = slice(i * P, (i + 1) * P)
                                    mm = matmul(bank[b][:, c], lhs[rows, c], rhs[rows, c])
                                found.append((b, pe.done(mm)))
                            return found

                        up, low = (1, 0) if d == 0 else (0, 1)
                        x_ready, xt_ready, lt_ready = [None] * 2, [None] * 2, [None] * 2
                        for par, (b, mm) in enumerate(products(A_, B)):
                            dve.wait(mm, x_init)
                            x_ready[par] = dve.done(V.copy_predicated(
                                X[:, par, :, :], four(masks[:, low, :]), quad(b)))
                            free_bank(b, x_ready[par])
                        for par, (b, mm) in enumerate(products(B, A_)):
                            dve.wait(mm, x_init)
                            xt_ready[par] = dve.done(V.copy_predicated(
                                XT[:, par, :, :], four(masks[:, up, :]), quad(b)))
                            lt_ready[par] = copy(act, LT[:, par, :, :], quad(b), mm, prior, xt_ready[par])
                            free_bank(b, xt_ready[par], lt_ready[par])
                        lak, lrb, lrk = [None] * 2, [None] * 2, [None] * 2
                        for par, (b, mm) in enumerate(products(K, A_)):
                            lak[par] = tt(U[:, par, :, :], quad(b), four(rconst(f"strict{up}")), ALU.mult, mm, prior)
                            free_bank(b, lak[par])
                        for par, (b, mm) in enumerate(products(B, R)):
                            lrb[par] = tt(Lrb[:, par, :, :], quad(b), four(rconst(f"incl{up}")), ALU.mult, mm, prior)
                            free_bank(b, lrb[par])
                        for par, (b, mm) in enumerate(products(K, R)):
                            lrk[par] = tt(Lrk[:, par, :, :], quad(b), four(rconst(f"incl{up}")), ALU.mult, mm, prior)
                            free_bank(b, lrk[par])
                        b = take_bank()
                        for par in range(2):
                            pe.wait(lak[par], tokV_ready)
                            for i in range(4):
                                mm = matmul(bank[b][:, (4 * par + i) * HEAD:(4 * par + i + 1) * HEAD],
                                            U[:, par, i, :], tokV[:, i, par * HEAD:(par + 1) * HEAD])
                        mm = pe.done(mm)
                        lak_read = mm
                        g_ready = copy(act, GA[:, :, :, 0:HEAD],
                                       bank[b][:, :].rearrange("p (a t c) -> p a t c", a=2, t=4), mm, prior)
                        free_bank(b, g_ready)
                        for l in range(1, LEVELS):
                            u_ready = [None] * 2
                            for par in range(2):
                                b = take_bank()
                                pe.wait(lt_ready[par], x_ready[par], xt_ready[par])
                                for i in range(4):
                                    mm = matmul(bank[b][:, i * P:(i + 1) * P], LT[:, par, i, :], X[:, par, i, :])
                                mm = pe.done(mm)
                                u_ready[par] = copy(act, U[:, par, :, :], quad(b), mm, lak_read)
                                free_bank(b, u_ready[par])
                            for par in range(2):
                                pe.wait(u_ready[par])
                                if l < LEVELS - 1:
                                    b = take_bank()
                                    for i in range(4):
                                        mm = matmul(bank[b][:, i * P:(i + 1) * P], XT[:, par, i, :], U[:, par, i, :])
                                    mm = pe.done(mm)
                                    dve.wait(mm)
                                    x_ready[par] = dve.done(V.copy_predicated(
                                        X[:, par, :, :], four(masks[:, 2 * l + low, :]), quad(b)))
                                    free_bank(b, x_ready[par])
                                b = take_bank()
                                for i in range(4):
                                    mm = matmul(bank[b][:, i * P:(i + 1) * P], U[:, par, i, :], XT[:, par, i, :])
                                mm = pe.done(mm)
                                dve.wait(mm)
                                xt_ready[par] = dve.done(V.copy_predicated(
                                    XT[:, par, :, :], four(masks[:, 2 * l + up, :]), quad(b)))
                                free_bank(b, xt_ready[par])
                        uw_ready = [None] * 2
                        for par in range(2):
                            b = take_bank()
                            pe.wait(xt_ready[par], g_ready, ga_ready)
                            for i in range(4):
                                mm = matmul(bank[b][:, i * P:(i + 1) * P], XT[:, par, i, :], GA[:, par, i, :])
                            mm = pe.done(mm)
                            uw_ready[par] = copy(act, UW[:, par, :, :], quad(b), mm, prior)
                            free_bank(b, uw_ready[par])
                        pe.wait(*uw_ready, tokB_ready, tokK_ready)
                        b_eo = [take_bank(), take_bank()]
                        for par in range(2):
                            hc = slice(par * HEAD, (par + 1) * HEAD)
                            for c in range(8):
                                i, rows, b = c // 2, slice((c % 2) * HEAD, (c % 2 + 1) * HEAD), b_eo[c % 2]
                                o = slice(i * HEAD, (i + 1) * HEAD)
                                o2 = slice((4 + i) * HEAD, (5 + i) * HEAD)
                                matmul(bank[b][hc, o], UW[rows, par, i, HEAD:P], tokB[rows, i, hc])
                                matmul(bank[b][hc, o2], tokB[rows, i, hc], UW[rows, par, i, 0:HEAD], True, False)
                                mm = matmul(bank[b][hc, o2], tokK[rows, i, hc], tokV[rows, i, hc], False, True)
                        mm = pe.done(mm)
                        dg = tt(MT[:, :, :], rconst("ident2").unsqueeze(1).to_broadcast([P, 8, HEAD]),
                                DC[:, :].unsqueeze(2).to_broadcast([P, 8, HEAD]), ALU.mult, dc_ready, prior)
                        by2 = lambda ap: ap.rearrange("p (i e) j -> p e i j", e=2)
                        for e_ in range(2):
                            b = b_eo[e_]
                            mn = bank[b][:, :].rearrange("p (m c j) -> p m c j", m=2, c=4)
                            mt_ready = tt(by2(MT[:, :, :])[:, e_], by2(MT[:, :, :])[:, e_], mn[:, 0], ALU.add, mm, dg)
                            n_ready = copy(dve, by2(N_[:, :, :])[:, e_], mn[:, 1], mm)
                            free_bank(b, n_ready)
                        b = take_bank()
                        for par in range(2):
                            pe.wait(lrb[par])
                            for i in range(4):
                                mm = matmul(bank[b][par * HEAD:(par + 1) * HEAD, i * P:(i + 1) * P],
                                            UW[:, par, i, HEAD:P], Lrb[:, par, i, :])
                        mm = pe.done(mm)
                        z_ready = tt(R[:, :], R[:, :], bank[b][:, :], ALU.add, mm)
                        free_bank(b, z_ready)
                        for par in range(2):
                            hc = slice(par * HEAD, (par + 1) * HEAD)
                            pe.wait(lrk[par])
                            for i in range(4):
                                o = slice(i * P, (i + 1) * P)
                                matmul(bank[7][hc, o], UW[:, par, i, 0:HEAD], Lrb[:, par, i, :],
                                       d == 0 and i == 0, False)
                                matmul(bank[7][hc, o], tokV[:, i, hc], Lrk[:, par, i, :], False, False)
                        order = list(range(8)) if d == 0 else list(range(8))[::-1]
                        dve.wait(prior)
                        s_ready = dve.done(V.memset(St[:, order[0], :], 0.0))
                        b = take_bank()
                        for step in range(7):
                            c, c_next = order[step], order[step + 1]
                            pe.wait(s_ready, mt_ready)
                            o = slice(step * HEAD, (step + 1) * HEAD)
                            for par in range(2):
                                hc = slice(par * HEAD, (par + 1) * HEAD)
                                mm = matmul(bank[b][hc, o], MT[hc, c, :], St[hc, c, :])
                            mm = pe.done(mm)
                            s_ready = tt(St[:, c_next, :], bank[b][:, o], N_[:, c, :], ALU.add, mm, n_ready)
                        free_bank(b, s_ready)
                        pe.wait(s_ready, z_ready)
                        for par in range(2):
                            hc = slice(par * HEAD, (par + 1) * HEAD)
                            for c in range(8):
                                o = slice(c * CHUNK, (c + 1) * CHUNK)
                                mm = matmul(bank[7][hc, o], St[hc, c, :], R[hc, o], False, d == 1 and c == 7)
                        y_done = pe.done(mm)
                    yt, yn = A_[:, :], B[:, :]
                    yr = copy(act, yt, bank[7][:, :], y_done, dve.last())
                    bank_free[7] = [yr]
                    b = take_bank()
                    pe.wait(yr)
                    mm = pe.done(matmul(bank[b][:, :], const("head_ones"), yt))
                    yc = stt(yt, bank[b][:, :], -1.0 / HEAD, yt, ALU.mult, ALU.add, mm)
                    free_bank(b, yc)
                    sq = activate(t0, yt, ACT.Square, yc)
                    b = take_bank()
                    pe.wait(sq)
                    mm = pe.done(matmul(bank[b][:, :], const("head_ones"), t0))
                    inv = inverse_root(t1, t2, b, mm, 1.0 / HEAD, "gn_eps", dve.last())
                    yn_r = tt(yt, yt, t1, ALU.mult, inv, y_stored)
                    yn_r = ts(yt, yt, vcol("lnx_g", t), vcol("lnx_b", t), ALU.mult, ALU.add, yn_r)
                    bo = stt(ksum, ksum, vcol("r_k", t), r_, ALU.mult, ALU.mult, ks)
                    b = take_bank()
                    pe.wait(bo)
                    mm = pe.done(matmul(bank[b][:, :], const("head_ones"), ksum))
                    bo = tt(t0, bank[b][:, :], v_, ALU.mult, mm, sq)
                    free_bank(b, bo)
                    yn_r = tt(yt, yt, t0, ALU.add, yn_r, bo)
                    b = take_bank()
                    pe.wait(gl_ready)
                    mm = pe.done(matmul(bank[b][:, :], up_w[:, 2, t * P:(t + 1) * P], gl))
                    yg = tt(yn, yt, bank[b][:, :], ALU.mult, mm, yn_r)
                    free_bank(b, yg)
                    y_stored = store.load(y_spill[0, :, t, :], yn, yg)
                    for q in (dve, act, pool):
                        q.wait(y_stored)
                return y_stored

        def neighbourhood():
            ends = phase_wait()
            with ExitStack() as ph:
                ar = Arena(nc, ph)
                r_col = ar.sb("na_rstd_col", [P, 4])
                v = ar.sb("na_v", [P, 4, RW])
                qk = ar.sb("na_qk", [P, 2, 2, S])
                bias = ar.sb("na_bias", [P, 2, 14, GRID_W])
                score = ar.sb("na_score", [P, 4, S])
                pT = ar.sb("na_pT", [P, 4, S])
                stat = ar.sb("na_stat", [P, 4, 4])
                out_t = ar.sb("na_out", [P, 2, S])
                gain8 = ar.sb("na_gain8", [P, 1])
                g8 = ts(gain8[:, :], vcol("q_gain"), HEAD ** -0.5, None, ALU.mult, None)
                col_ready = rstd_by_token(r_col[:, :])
                for i in range(2):
                    n = take("na_v", i)
                    hi, lo = unit(n, 2 * P)
                    pe.wait(*unit_split[n])
                    for t in range(4):
                        b = take_bank()
                        rows = slice(t * P, (t + 1) * P)
                        for k in range(KT):
                            mm = split_matmul(bank[b][:, 0:2 * P], xg_hi[:, k, rows], xg_lo[:, k, rows],
                                              hi[:, k, :], lo[:, k, :], k == 0, k == KT - 1)
                        mm = pe.done(mm)
                        unit_done[n] = mm
                        v_ready = ts(v[:, t, i * 2 * P:(i + 1) * 2 * P], bank[b][:, 0:2 * P], r_col[:, t:t + 1],
                                     None, ALU.mult, None, mm, col_ready)
                        free_bank(b, v_ready)
                bias_load = [[Loader(sp, sem(f"na_bias{i}{a}")) for a in range(2)] for i in range(2)]
                bias_read = [ends[2], ends[2]]
                store = Loader(sp, sem("yb_store"))
                qk_read = [None, None]
                stored = [None, None]
                score_read = [None] * 4
                pT_read = None
                for t in range(4):
                    i = t % 2
                    n = take("na_qk", t)
                    ready = [None, None]
                    for c in range(2):
                        b = take_bank()
                        mm = project(n, 2 * P, c, xg, range(KT), b)
                        z = scaled_by_rstd(qk[:, i, c, :], b, mm, qk_read[i])
                        sq = activate(square[:, c, :], qk[:, i, c, :], ACT.Square, z, dve.last())
                        b = take_bank()
                        pe.wait(sq)
                        mm = pe.done(matmul(bank[b][:, :], const("head_ones"), square[:, c, :]))
                        inv = inverse_root(square[:, c, :], root[:, :], b, mm, 1.0 / HEAD, "eps", dve.last())
                        ready[c] = stt(qk[:, i, c, :], qk[:, i, c, :], gain8[:, :] if c == 0 else vcol("k_gain"),
                                       square[:, c, :], ALU.mult, ALU.mult, inv, g8)
                    b_o = None
                    for par in range(2):
                        h = 2 * t + par
                        hc = slice(par * HEAD, (par + 1) * HEAD)
                        loaded = []
                        for a in range(2):
                            loaded.append(bias_load[par][a].load(
                                bias[a * HEAD:(a + 1) * HEAD, par, :, :],
                                bias_na[h, 1 - a:15 - a, :, :].rearrange("m q k -> q m k"), *ends, bias_read[par]))
                        pool.wait(*loaded, bias_read[par])
                        bias_ready = pool.done(G.tensor_tensor(
                            bias[:, par, :, :], bias[:, par, :, :],
                            const("na_mask").unsqueeze(1).to_broadcast([P, 14, GRID_W]), ALU.add))
                        pe.wait(*ready)
                        done_q = []
                        for qt in range(4):
                            b = take_bank()
                            mm = pe.done(matmul(bank[b][:, :], qk[hc, i, 0, qt * P:(qt + 1) * P], qk[hc, i, 1, :]))
                            st = stat[:, qt, :]
                            rows = bias[:, par, 6 - 2 * qt:14 - 2 * qt, :].rearrange("p m k -> p (m k)")
                            dve.wait(mm, bias_ready, score_read[qt])
                            s1 = dve.done(V.tensor_tensor(score[:, qt, :], bank[b][:, :], rows, ALU.add))
                            free_bank(b, s1)
                            dve.wait(s1)
                            top = dve.done(V.tensor_reduce(st[:, 0:1], score[:, qt, :], AX_X, ALU.max, negate=True))
                            e = activate(score[:, qt, :], score[:, qt, :], ACT.Exp, top, bias=st[:, 0:1],
                                         accum_out=st[:, 1:2])
                            done_q.append(e)
                        bias_read[par] = s1
                        qk_read[i] = pe.last()
                        b_t = [take_bank() for _ in range(4)]
                        for qt in range(4):
                            st = stat[:, qt, :]
                            dve.wait(done_q[qt])
                            r = dve.done(V.reciprocal(st[:, 2:3], st[:, 1:2]))
                            r = ts(score[:, qt, :], score[:, qt, :], st[:, 2:3], None, ALU.mult, None, r)
                            pe.wait(r)
                            for k in range(4):
                                mm = T.transpose(bank[b_t[k]][:, qt * P:(qt + 1) * P],
                                                 score[:, qt, k * P:(k + 1) * P], const("ident"))
                            score_read[qt] = pe.done(mm)
                        p_ready = []
                        for k in range(4):
                            p_ready.append(copy((act, dve)[k % 2], pT[:, k, :], bank[b_t[k]][:, :], pe.last(), pT_read))
                            free_bank(b_t[k], p_ready[k])
                        if par == 0:
                            pe.wait(*bank_free[7])
                        for k in range(4):
                            pe.wait(p_ready[k], v_ready)
                            mm = matmul(bank[7][hc, :], v[:, k, h * HEAD:(h + 1) * HEAD], pT[:, k, :], k == 0, k == 3)
                        pT_read = pe.done(mm)
                    o = copy(act, out_t[:, i, :], bank[7][:, :], pT_read, stored[i])
                    bank_free[7] = [o]
                    stored[i] = store.load(y_spill[1, :, t, :], out_t[:, i, :], o)
                norm_state["xg_last"] = pe.last()
                return stored

        def combine(ya_stored, yb_stored):
            ends = phase_wait()
            with ExitStack() as ph:
                ar = Arena(nc, ph)
                y_sb = ar.sb("mix_y", [P, 2, 4, S])
                y2 = Acts(ar.sb("mix_y_hi", [P, 4, S], F32R), ar.sb("mix_y_lo", [P, 4, S], F32R), 4)
                z_act = Acts(ar.sb("mix_z_hi", [P, KT, S], F32R), ar.sb("mix_z_lo", [P, KT, S], F32R), KT)
                gate = ar.sb("mix_gate", [P, 2, S])
                x_loader = Loader(sp, sem("x_reload"))
                y_loader = [Loader(sp, sem(f"y_reload{i}")) for i in range(2)]
                y_loaded = [y_loader[0].load(y_sb[:, 0, :, :], y_spill[0], *ends, ya_stored),
                            y_loader[1].load(y_sb[:, 1, :, :], y_spill[1], *yb_stored)]
                free = [None, None]
                z_part = [None] * KT
                for side, (w_name, g_name) in enumerate((("o_rwkv", "gate_a"), ("o_na", "gate_b"))):
                    for k in range(4):
                        act.wait(y_loaded[side], pe.last())
                        dve.wait(y_loaded[side], pe.last())
                        split_act(y2, k, y_sb[:, side, k, :])
                    for half in range(2):
                        n = take(w_name, half)
                        banks = []
                        for c in range(4):
                            b = take_bank()
                            banks.append((b, project(n, 4 * P, c, y2, range(4), b)))
                        for u in range(2):
                            n = take(g_name, 2 * half + u)
                            for c in range(2):
                                j = 4 * half + 2 * u + c
                                b = take_bank()
                                mm = project(n, 2 * P, c, xg, range(KT), b)
                                norm_state["xg_last"] = mm
                                b_o, mm_o = banks[2 * u + c]
                                i = j % 2
                                gr = scaled_by_rstd(gate[:, i, :], b, mm, free[i])
                                gr = activate(gate[:, i, :], gate[:, i, :], ACT.Sigmoid, gr,
                                              bias=vcol("b_gate", KT * side + j))
                                if side == 0:
                                    z = tt(x[:, j, :], gate[:, i, :], bank[b_o][:, :], ALU.mult, gr, mm_o)
                                    z_part[j] = z
                                    free[i] = z
                                else:
                                    z = tt(gate[:, i, :], gate[:, i, :], bank[b_o][:, :], ALU.mult, gr, mm_o)
                                    z2 = tt(gate[:, i, :], gate[:, i, :], x[:, j, :], ALU.add, z, z_part[j])
                                    hi, lo = split_act(z_act, j, gate[:, i, :], z2)
                                    free[i] = lo
                                free_bank(b_o, z)
                x_back = x_loader.load(x[:, :, :], x_spill, dve.last())
                dve.wait(x_back)
                act.wait(x_back)
                out_projection([("w_out2", 4, 2 * P)], z_act, {"w_out2": range(KT)}, next_norm("norm2_g"))
                norm_end()

        def experts():
            ends = phase_wait()
            with ExitStack() as ph:
                ar = Arena(nc, ph)
                r_col = ar.sb("e_rstd_col", [P, 4])
                rb = ar.sb("e_router_b", [P, 36])
                ec_at, n_ec = _places(_expert_consts())
                ec = ar.sb("e_constants", [P, n_ec])
                wide_raw = ar.sb("e_w_raw", [P, 4, UNIT])
                raws = [raw[0][:, :], raw[1][:, :]] + [wide_raw[:, i, :] for i in range(4)]
                h_row = ar.sb("e_h_row", [P, 2, D])
                h_hi, h_lo = ar.sb("e_h_hi", [P, 2, KT, P], F32R), ar.sb("e_h_lo", [P, 2, KT, P], F32R)
                y_row = ar.sb("e_y_row", [P, 2, D])
                he = ar.sb("e_he", [P, 2, D_EXPERT])
                he_hi, he_lo = ar.sb("e_he_hi", [P, 2, 2, P], F32R), ar.sb("e_he_lo", [P, 2, 2, P], F32R)
                small = ar.sb("e_routing", [P, 1280])
                index_tok = ar.sb("e_tokens", [P, 4], U32)
                index = ar.sb("e_index", [P, 8 + BLOCKS + 3 * BLOCKS], U32)
                at = [0]

                def econst(name):
                    a, n = ec_at[name]
                    return ec[:, a:a + n]

                def piece(*shape):
                    n = int(np.prod(shape))
                    ap = small[:, at[0]:at[0] + n]
                    at[0] += n
                    return ap.rearrange("p (a b) -> p a b", a=shape[0]) if len(shape) > 1 else ap

                ld = Loader(sp, sem("e_loads"))
                ld.load(ec[:, :], econsts, *ends)
                rb_loaded = ld_done = ld.load(rb[:, :], router_b)
                col_ready = rstd_by_token(r_col[:, :])
                n = take("router", 0)
                hi, lo = unit(n, 2 * P)
                pe.wait(*unit_split[n])
                for k in range(KT):
                    pe.wait(*xg.ready[k])
                logits = piece(4, 36)
                b = take_bank()
                for t in range(4):
                    rows = slice(t * P, (t + 1) * P)
                    for k in range(KT):
                        mm = split_matmul(bank[b][:, t * 36:(t + 1) * 36], xg_hi[:, k, rows], xg_lo[:, k, rows],
                                          hi[:, k, 0:36], lo[:, k, 0:36], k == 0, k == KT - 1)
                mm = pe.done(mm)
                unit_done[n] = mm
                for t in range(4):
                    lg = stt(logits[:, t, :], bank[b][:, t * 36:(t + 1) * 36], r_col[:, t:t + 1], rb[:, :],
                             ALU.mult, ALU.add, mm, col_ready, rb_loaded)
                free_bank(b, lg)
                gl, el = logits[:, :, 0:4], logits[:, :, 4:36]
                wide = lambda ap, n: ap.to_broadcast([P, 4, n])

                def first_of(dst, values, top, n, seg, ready, tmp_ap):
                    r = tt(dst, values, wide(top, n), ALU.is_equal, ready)
                    dve.wait(r)
                    flat = lambda ap: ap.rearrange("p a b -> p (a b)")
                    r = dve.done(V.tensor_tensor_scan(flat(tmp_ap), const(seg), flat(dst), 0.0, ALU.mult, ALU.add))
                    r = ts(tmp_ap, tmp_ap, 1.0, None, ALU.is_equal, None, r)
                    return tt(dst, dst, tmp_ap, ALU.mult, r)

                g_top = piece(4, 1)
                dve.wait(lg)
                r = dve.done(V.tensor_reduce(g_top, gl, AX_X, ALU.max))
                g_one, g_tmp = piece(4, 4), piece(4, 4)
                one_r = first_of(g_one, gl, g_top, 4, "seg4", r, g_tmp)
                r = tt(g_tmp, gl, wide(g_top, 4), ALU.subtract, one_r)
                r = activate(g_tmp, g_tmp, ACT.Exp, r)
                p_group = piece(4, 1)
                dve.wait(r)
                r = dve.done(V.tensor_reduce(p_group, g_tmp, AX_X, ALU.add))
                dve.wait(r)
                pg_r = dve.done(V.reciprocal(p_group, p_group))
                e8, e_tmp = piece(4, 8), piece(4, 8)
                r = None
                for g in range(N_GROUPS):
                    dst = e8 if g == 0 else e_tmp
                    r = tt(dst, el[:, :, 8 * g:8 * g + 8], wide(g_one[:, :, g:g + 1], 8), ALU.mult, r)
                    if g:
                        r = tt(e8, e8, e_tmp, ALU.add, r)
                v1, v2, one1, one2 = piece(4, 1), piece(4, 1), piece(4, 8), piece(4, 8)
                dve.wait(r)
                r = dve.done(V.tensor_reduce(v1, e8, AX_X, ALU.max))
                r = first_of(one1, e8, v1, 8, "seg8", r, e_tmp)
                r = stt(e8, one1, -3e38, e8, ALU.mult, ALU.add, r)
                dve.wait(r)
                r = dve.done(V.tensor_reduce(v2, e8, AX_X, ALU.max))
                r = first_of(one2, e8, v2, 8, "seg8", r, e_tmp)
                w1, w2 = piece(4, 1), piece(4, 1)
                r = tt(w2, v2, v1, ALU.subtract, r)
                r = activate(w2, w2, ACT.Exp, r)
                r = ts(w1, w2, 1.0, None, ALU.add, None, r)
                dve.wait(r)
                r = dve.done(V.reciprocal(w1, w1))
                r = tt(w1, w1, p_group, ALU.mult, r, pg_r)
                r = tt(w2, w2, w1, ALU.mult, r)
                weights_ready = r

                rows_of = wide_raw[:, 0:2, :].rearrange("p a (b c) -> p (a b) c", b=2)
                row_parts = []
                tile_read = [None, None]
                for j in range(KT):
                    i = j % 2
                    hn = stt(square[:, i, :], x[:, j, :], vcol("norm2_g", j), rstd[:, :], ALU.mult, ALU.mult,
                             norm_state["rstd"], tile_read[i], act.last())
                    b = take_bank()
                    pe.wait(hn)
                    for t in range(4):
                        mm = T.transpose(bank[b][:, t * P:(t + 1) * P], square[:, i, t * P:(t + 1) * P],
                                         const("ident"))
                    tile_read[i] = pe.done(mm)
                    rc_ = copy(act, rows_of[:, :, j * P:(j + 1) * P],
                               bank[b][:, :].rearrange("p (t c) -> p t c", t=4), tile_read[i])
                    free_bank(b, rc_)
                h_store = Loader(sp, sem("h_rows_store"))
                for t in range(4):
                    h_stored = h_store.load(h_rows[t * P:(t + 1) * P, :], rows_of[:, t, :], rc_)

                choice = [piece(4, 32), piece(4, 32)]
                both = piece(4, 32)
                for c, one in enumerate((one1, one2)):
                    for g in range(N_GROUPS):
                        r = tt(choice[c][:, :, 8 * g:8 * g + 8], one, wide(g_one[:, :, g:g + 1], 8), ALU.mult,
                               weights_ready)
                both_ready = tt(both, choice[0], choice[1], ALU.add, r)
                b = take_bank()
                pe.wait(both_ready, ld_done)
                for t in range(4):
                    o = bank[b][:, t * 32:(t + 1) * 32]
                    for u in range(t):
                        matmul(o, const("ones"), both[:, u, :], u == 0, False)
                    matmul(o, econst("before"), both[:, t, :], t == 0, True)
                for t in range(4):
                    mm = matmul(bank[b][:, P:P + 32], const("ones"), both[:, t, :], t == 0, t == 3)
                mm = pe.done(mm)
                rank, quot, over = piece(4, 32), piece(4, 32), piece(4, 32)
                count, blocks, ended, begun = piece(32), piece(32), piece(32), piece(32)
                c1 = copy(dve, count, bank[b][:, P:P + 32], mm)
                c2 = copy(dve, rank, bank[b][:, 0:P].rearrange("p (t e) -> p t e", t=4), mm)
                free_bank(b, c2)
                r = ts(blocks, count, 1.0, None, ALU.is_ge, None, c1)
                q = ts(quot, rank, float(P), None, ALU.is_ge, None, c2)
                for m in range(1, 4):
                    r = stt(blocks, count, float(m * P + 1), blocks, ALU.is_ge, ALU.add, r)
                    if m > 1:
                        q = stt(quot, rank, float(m * P), quot, ALU.is_ge, ALU.add, q)
                dve.wait(r)
                r = dve.done(V.tensor_tensor_scan(ended, econst("one32"), blocks, 0.0, ALU.mult, ALU.add))
                r = tt(begun, ended, blocks, ALU.subtract, r)
                q = stt(rank, quot, -float(P), rank, ALU.mult, ALU.add, q)
                q = tt(quot, quot, begun.unsqueeze(1).to_broadcast([P, 4, 32]), ALU.add, q, r)
                q = stt(rank, rank, float(BLOCKS), quot, ALU.mult, ALU.add, q)
                slot = index[:, 0:8]
                slot_f = piece(2, 4)
                for c in range(2):
                    o = tt(over, choice[c], rank, ALU.mult, q)
                    dve.wait(o)
                    o = dve.done(V.tensor_reduce(slot_f[:, c, :], over, AX_X, ALU.add))
                    q = o
                slot_ready = copy(dve, slot, slot_f.rearrange("p c t -> p (c t)"), q)
                owner = piece(BLOCKS)
                for a in range(0, BLOCKS, 13):
                    n_b = min(13, BLOCKS - a)
                    sq3 = square[:, 0, 0:n_b * 32].rearrange("p (b e) -> p b e", b=n_b)
                    o = tt(sq3, econst("block")[:, a:a + n_b].unsqueeze(2).to_broadcast([P, n_b, 32]),
                           ended.unsqueeze(1).to_broadcast([P, n_b, 32]), ALU.is_ge, r, tile_read[0], dve.last())
                    dve.wait(o)
                    o = dve.done(V.tensor_reduce(owner[:, a:a + n_b], sq3, AX_X, ALU.add))
                o = ts(owner, owner, float(N_EXPERTS - 1), 3.0 * P, ALU.min, ALU.mult, o)
                w_index = index[:, 8 + BLOCKS:8 + 4 * BLOCKS].rearrange("p (b u) -> p b u", u=3)
                for u in range(3):
                    w_index_ready = tt(w_index[:, :, u], owner,
                                       econst("row")[:, u:u + 1].to_broadcast([P, BLOCKS]), ALU.add, o)
                table = index[:, 8:8 + BLOCKS]
                dve.wait(slot_ready)
                zeroed = dve.done(V.memset(table, 0))
                tab = Loader(sp, sem("table_zero"))
                cleared = tab.load(slot_table.rearrange("(p b) o -> p (b o)", p=P), table, zeroed)
                ids = index_tok[:, :]
                ids_ready = copy(dve, ids, econst("token"), dve.last())
                scatter = Loader(pool, sem("table_scatter"))
                pool.wait(cleared, slot_ready, ids_ready)
                for c in range(2):
                    for t in range(4):
                        scattered = scatter.indirect(slot_table, slot[:, 4 * c + t:4 * c + t + 1], ids[:, t:t + 1], None)
                table_ready = tab.load(table, slot_table.rearrange("(p b) o -> p (b o)", p=P), scattered)

                raw_loads = [Loader(pool, sem(f"e_raw_load{i}")) for i in range(6)]
                row_loads = [Loader(pool, sem(f"e_row_load{i}")) for i in range(2)]
                y_stores = [Loader(sp, sem(f"e_y_store{i}")) for i in range(2)]
                units = []
                for k in range(BLOCKS + 1):
                    if k < BLOCKS:
                        units += [(k, 0), (k, 1)]
                    if k >= 1:
                        units += [(k - 1, 2)]
                base = taken[0]
                e_loaded, e_split, e_done = {}, {}, {}
                pool.wait(table_ready, w_index_ready, h_stored, *ends)
                pool.wait(rc_)

                def load_expert(m):
                    k, u = units[m]
                    free = e_split.get(m - 6, ())
                    e_loaded[m] = raw_loads[m % 6].indirect(raws[m % 6], None, expert_rows,
                                                            w_index[:, k, u:u + 1], *free)

                def split_expert(m):
                    r, hi, lo = raws[m % 6], w_hi[(base + m) % SLOTS], w_lo[(base + m) % SLOTS]
                    free = e_done.get(m - SLOTS)
                    act.wait(e_loaded[m], free)
                    rounded = act.done(A.activation(hi[:, :], r, ACT.Copy))
                    dve.wait(rounded, free)
                    rest = dve.done(V.tensor_tensor(lo[:, :], r, hi[:, :].bitcast(F32), ALU.subtract))
                    e_split[m] = (rounded, rest)

                row_loaded, row_read = {}, {}

                def load_rows(k):
                    row_loaded[k] = row_loads[k % 2].indirect(h_row[:, k % 2, :], None, h_rows,
                                                              table[:, k:k + 1], row_read.get(k - 2))

                load_rows(0)
                for m in range(3):
                    load_expert(m)
                load_rows(1)
                for m in range(3, 6):
                    load_expert(m)
                next_load, next_split, use = 6, 0, 0

                def use_unit():
                    nonlocal next_load, next_split, use
                    while next_split < min(use + SLOTS, len(units)) and (
                            next_split < SLOTS or next_split - SLOTS in e_done):
                        split_expert(next_split)
                        next_split += 1
                        if next_load < len(units):
                            load_expert(next_load)
                            next_load += 1
                    m = use
                    use += 1
                    pe.wait(*e_split[m])
                    s = (base + m) % SLOTS
                    return m, w_hi[s], w_lo[s]

                hb_read, he_read, y_stored = {}, {}, {}
                he_done = {}

                def gate_up(k):
                    i = k % 2
                    pe.wait(row_loaded[k])
                    parts = []
                    for half in range(2):
                        b = take_bank()
                        for c in range(4):
                            kt = 4 * half + c
                            mm = T.transpose(bank[b][:, c * P:(c + 1) * P], h_row[:, i, kt * P:(kt + 1) * P],
                                             const("ident"))
                        mm = pe.done(mm)
                        src = bank[b][:, :].rearrange("p (k c) -> p k c", k=4)
                        dst = slice(4 * half, 4 * half + 4)
                        act.wait(mm, hb_read.get(k - 2))
                        a1 = act.done(A.activation(h_hi[:, i, dst, :], src, ACT.Copy))
                        d1 = tt(h_lo[:, i, dst, :], src, h_hi[:, i, dst, :].bitcast(F32), ALU.subtract, a1,
                                hb_read.get(k - 2))
                        free_bank(b, d1)
                        parts.append((a1, d1))
                    row_read[k] = mm
                    if k + 2 < BLOCKS:
                        load_rows(k + 2)
                    b = take_bank()
                    for half in range(2):
                        m, hi, lo = use_unit()
                        pe.wait(*parts[half])
                        w = [z[:, :].rearrange("p (k c) -> p k c", k=4) for z in (hi, lo)]
                        for c in range(4):
                            kt = 4 * half + c
                            first, last = kt == 0, kt == KT - 1
                            matmul(bank[b][:, :], h_hi[:, i, kt, :], w[0][:, c, :], first, False)
                            matmul(bank[b][:, :], h_hi[:, i, kt, :], w[1][:, c, :], False, False)
                            mm = matmul(bank[b][:, :], h_lo[:, i, kt, :], w[0][:, c, :], False, last)
                        e_done[m] = pe.done(mm)
                    hb_read[k] = e_done[m]
                    sil = activate(he[:, i, :], bank[b][:, 0:D_EXPERT], ACT.Silu, e_done[m], he_read.get(k - 2))
                    r = tt(he[:, i, :], he[:, i, :], bank[b][:, D_EXPERT:], ALU.mult, sil)
                    free_bank(b, r)
                    he_done[k] = r

                def down(k):
                    i = k % 2
                    b = take_bank()
                    pe.wait(he_done[k])
                    for c in range(2):
                        mm = T.transpose(bank[b][:, c * P:(c + 1) * P], he[:, i, c * P:(c + 1) * P], const("ident"))
                    he_read[k] = pe.done(mm)
                    src = bank[b][:, 0:2 * P].rearrange("p (k c) -> p k c", k=2)
                    a1 = activate(he_hi[:, i, :, :], src, ACT.Copy, he_read[k])
                    d1 = tt(he_lo[:, i, :, :], src, he_hi[:, i, :, :].bitcast(F32), ALU.subtract, a1)
                    free_bank(b, d1)
                    m, hi, lo = use_unit()
                    pe.wait(a1, d1)
                    w = [z[:, :].rearrange("p (k c) -> p k c", k=2) for z in (hi, lo)]
                    copied = []
                    for half in range(2):
                        b = take_bank()
                        cols = slice(half * S, (half + 1) * S)
                        for c in range(2):
                            matmul(bank[b][:, :], he_hi[:, i, c, :], w[0][:, c, cols], c == 0, False)
                            matmul(bank[b][:, :], he_hi[:, i, c, :], w[1][:, c, cols], False, False)
                            mm = matmul(bank[b][:, :], he_lo[:, i, c, :], w[0][:, c, cols], False, c == 1)
                        mm = pe.done(mm)
                        q_ = copy((act, dve)[half], y_row[:, i, cols], bank[b][:, :], mm, y_stored.get(k - 2))
                        free_bank(b, q_)
                        copied.append(q_)
                    e_done[m] = mm
                    y_stored[k] = y_stores[i].load(
                        y_rows.rearrange("(p b) d -> p b d", b=BLOCKS)[:, k, :], y_row[:, i, :], *copied)

                for k in range(BLOCKS + 1):
                    if k < BLOCKS:
                        gate_up(k)
                    if k >= 1:
                        down(k - 1)

                pool.wait(y_stored[BLOCKS - 1], y_stored[BLOCKS - 2], *e_split[len(units) - 1])
                pool.wait(*e_split[len(units) - 2])
                gathered = [Loader(pool, sem(f"e_gather{t}")) for t in range(4)]
                got = []
                for t in range(4):
                    for c in range(2):
                        token = gathered[t].indirect(wide_raw[:, t, c * D:(c + 1) * D], None, y_rows,
                                                     slot[:, 4 * c + t:4 * c + t + 1])
                    got.append(token)
                out_load = [Loader(sp, sem(f"out_store{i}")) for i in range(2)]
                stored = [y_stored[BLOCKS - 2], y_stored[BLOCKS - 1]] if BLOCKS % 2 == 0 else \
                    [y_stored[BLOCKS - 1], y_stored[BLOCKS - 2]]
                for t in range(4):
                    i = t % 2
                    for half in range(2):
                        b = take_bank()
                        for c in range(4):
                            mm = T.transpose(bank[b][:, c * P:(c + 1) * P], x[:, 4 * half + c, t * P:(t + 1) * P],
                                             const("ident"))
                        mm = pe.done(mm)
                        cols = slice(half * S, (half + 1) * S)
                        r = stt(y_row[:, i, cols], wide_raw[:, t, cols], w1[:, t, :], bank[b][:, :], ALU.mult,
                                ALU.add, mm, got[t], stored[i], weights_ready)
                        free_bank(b, r)
                        r = stt(y_row[:, i, cols], wide_raw[:, t, D + half * S:D + (half + 1) * S], w2[:, t, :],
                                y_row[:, i, cols], ALU.mult, ALU.add, r)
                    stored[i] = out_load[i].load(out[t * P:(t + 1) * P, :], y_row[:, i, :], r)
                sp.wait(*stored)

        dcol = sb("chunk_decay", [P, 8])

        mixer()
        cross_attention(0)
        conv_ffn(0, "c_norm")
        conformer()
        cross_attention(1)
        conv_ffn(1, None)
        final_norm()
        ya_stored = rwkv()
        yb_stored = neighbourhood()
        combine(ya_stored, yb_stored)
        experts()


def _unit_arrays(inp):
    def pack(w, cols):
        k, n = w.shape
        return w.reshape(k // P, P, n // cols, cols).transpose(2, 1, 0, 3).reshape(n // cols, P, -1)

    def pairs(a, b):
        k, n = a.shape
        return np.concatenate([a.reshape(k, n // P, P), b.reshape(k, n // P, P)], axis=2).reshape(k, 2 * n)

    w = {}
    w_in = inp["ab_w_in"][0]
    w["ab_in"] = pack(pairs(w_in[:, 0:D], w_in[:, D:2 * D]), 2 * P)
    w["pool_in"] = pack(w_in[:, 2 * D:], 2 * P)
    w["ab_out_a"] = pack(inp["ab_w_out"][0][0:D], 2 * P)
    w["ab_out_b"] = pack(inp["ab_w_out"][0][D:], 4 * P)
    w["pw1"] = pack(pairs(inp["c_w_pw1"][0][:, 0:D], inp["c_w_pw1"][0][:, D:]), 2 * P)
    w["pw2"] = pack(inp["c_w_pw2"][0], 2 * P)
    for l in range(DEPTH):
        for m in "kvqo":
            w[f"w{m}{l}"] = pack(inp[f"xa_w{m}"][l], 2 * P)
        up = inp["f_w_up"][l]
        w[f"up{l}"] = pack(pairs(up[:, 0:D_FF], up[:, D_FF:]), 2 * P)
        w[f"down{l}"] = np.concatenate([pack(inp["f_w_down"][l][p * D:(p + 1) * D], 2 * P) for p in range(3)])
    w2 = inp["w_in_2"][0]
    r_, k_, v_ = (w2[:, i * RW:(i + 1) * RW] for i in range(3))
    lora = w2[:, 3 * RW:3 * RW + 384]
    zero = np.zeros((D, P), np.float32)
    w["lora"] = pack(np.concatenate([lora, zero], axis=1), 2 * P)
    w["rkvg"] = pack(np.concatenate([np.concatenate([m[:, t * P:(t + 1) * P] for m in (r_, k_, v_)] + [zero], axis=1)
                                     for t in range(4)], axis=1), 2 * P)
    base = 3 * RW + 384
    q2, k2, v2 = (w2[:, base + i * RW:base + (i + 1) * RW] for i in range(3))
    w["na_v"] = pack(v2, 2 * P)
    w["na_qk"] = pack(pairs(q2, k2), 2 * P)
    gates = w2[:, base + 3 * RW:]
    w["gate_a"], w["gate_b"] = pack(gates[:, 0:D], 2 * P), pack(gates[:, D:], 2 * P)
    w["o_rwkv"], w["o_na"] = pack(inp["w_o_rwkv_2"][0], 4 * P), pack(inp["w_o_na_2"][0], 4 * P)
    w["w_out2"] = pack(inp["w_out_2"][0], 2 * P)
    router = np.concatenate([inp["w_router_group_2"][0], inp["w_router_expert_2"][0],
                             np.zeros((D, 2 * P - 36), np.float32)], axis=1)
    w["router"] = pack(router, 2 * P)
    return np.stack([w[name][i] for name, i in _plan()])


def _expert_rows(inp):
    gate_up = np.concatenate([inp["w_gate_e_2"][0], inp["w_up_e_2"][0]], axis=2)
    gate_up = gate_up.reshape(N_EXPERTS, 2, 4, P, S).transpose(0, 1, 3, 2, 4).reshape(N_EXPERTS, 2, P, UNIT)
    down = inp["w_down_e_2"][0].reshape(N_EXPERTS, 1, 2, P, D).transpose(0, 1, 3, 2, 4).reshape(N_EXPERTS, 1, P, UNIT)
    return np.concatenate([gate_up, down], axis=1).reshape(-1, UNIT)


def _channel_major(a):
    t, c = a.shape
    return np.ascontiguousarray(a.T.reshape(c // P, P, t).transpose(1, 0, 2))


def kernel(**inputs):
    import concourse.bacc as bacc
    from concourse.bass_utils import run_bass_kernel_spmd

    inp = {k: np.asarray(v) for k, v in inputs.items()}
    cols = []
    for _, name, layer in _vector_names():
        a = inp[name] if layer is None else inp[name][layer]
        cols.append(a.reshape(-1, P).T)
    for name, layer in (("a_conv_w", 0), ("c_dw_w", 0), ("f_dw_w", 0), ("f_dw_w", 1)):
        a = inp[name][layer]
        taps, width = a.shape
        cols.append(a.reshape(taps, width // P, P).transpose(2, 1, 0).reshape(P, -1))
    for name in ("q_gain_2", "k_gain_2"):
        cols.append(np.tile(inp[name][0], 2).reshape(P, 1))
    rpb = np.pad(inp["rpb_2"][0], ((0, 0), (0, 0), (48, 48)))
    bias = np.stack([rpb[:, :, 63 - q:127 - q] for q in range(GRID_W)], axis=2)
    lora = np.stack([np.concatenate([inp["w_up_f_2"][0], inp["w_up_b_2"][0]]),
                     np.concatenate([inp["a_up_f_2"][0], inp["a_up_b_2"][0]]), inp["g_up_2"][0]], axis=1)
    arrays = {
        "stream": _unit_arrays(inp),
        "vectors": np.concatenate(cols, axis=1),
        "consts": np.concatenate(list(_consts().values()), axis=1),
        "rconsts": np.concatenate(list(_rwkv_consts().values()), axis=1),
        "x_in": _channel_major(inp["x"][0]),
        "mem_in": _channel_major(inp["mem"][0]),
        "gates_w": np.stack([inp["a_gate_x_w"][0], inp["a_gate_a_w"][0]], axis=1).transpose(2, 0, 1, 3),
        "group_w": inp["b_group_w"][0].transpose(1, 0, 2),
        "lora_w": lora,
        "router_b": np.broadcast_to(np.concatenate([inp["b_router_group_2"][0], inp["b_router_expert_2"][0]]),
                                    (P, 36)),
        "bias_na": bias,
        "level_masks": _level_masks(),
        "expert_rows": _expert_rows(inp),
        "econsts": np.concatenate(list(_expert_consts().values()), axis=1),
    }
    arrays = {k: np.ascontiguousarray(v) for k, v in arrays.items()}
    nc = bacc.Bacc("TRN2", target_bir_lowering=False, num_devices=1)
    args = [nc.dram_tensor(k, v.shape, mybir.dt.from_np(v.dtype), kind="ExternalInput").ap()
            for k, v in arrays.items()]
    out = nc.dram_tensor("out", (S, D), F32, kind="ExternalOutput").ap()
    spill = nc.dram_tensor("x_spill", (P, KT, S), F32, kind="Internal").ap()
    y_spill = nc.dram_tensor("y_spill", (2, P, 4, S), F32, kind="Internal").ap()
    h_rows = nc.dram_tensor("h_rows", (S, D), F32, kind="Internal").ap()
    y_rows = nc.dram_tensor("y_rows", (P * BLOCKS, D), F32, kind="Internal").ap()
    slot_table = nc.dram_tensor("slot_table", (P * BLOCKS, 1), U32, kind="Internal").ap()
    build(nc, *args, out, spill, y_spill, h_rows, y_rows, slot_table)
    r = run_bass_kernel_spmd(nc, [arrays], core_ids=[0])
    return np.asarray(r.results[0]["out"])[None]
```

```python
from contextlib import ExitStack

import numpy as np
import concourse.bass as bass
from concourse import mybir

F32 = mybir.dt.float32
F32R = mybir.dt.float32r
U8 = mybir.dt.uint8
U32 = mybir.dt.uint32
ALU = mybir.AluOpType
ACT = mybir.ActivationFunctionType
AX_X = mybir.AxisListType.X

P = 128
D = 1024
S = 512
KT = D // P
UNIT = 2048
N_MEM = 256
XA_HEADS = 4
XA_HD = D // XA_HEADS
D_FF = 3 * D
DEPTH = 2
CONV_A, CONV_C, CONV_F = 4, 31, 3
POOL_WINDOWS = (2, 4, 8, 16)
EPS = 1e-6
GN_EPS = 64e-5
GRID_W = 64
HEAD = 64
RW = 512
WIN_COLS = 16
N_GROUPS, PER_GROUP = 4, 8
N_EXPERTS = N_GROUPS * PER_GROUP
D_EXPERT = 256
CHUNK = 64
SPARE = 2 * S // P - 1
BLOCKS = N_EXPERTS + SPARE
WIDE, ROWS_AHEAD = 4, 3
LEVELS = 6
CONV_C_PE = 13



def _vector_names():
    names = [("ab_norm", "ab_norm", 0), ("a_conv_b", "a_conv_b", 0), ("gx_b", "a_gate_x_b", 0),
             ("ga_b", "a_gate_a_b", 0), ("lam", "a_lambda", 0), ("bg_b", "b_group_b", 0),
             ("b_scale", "b_scale", 0), ("c_norm", "c_norm", 0), ("c_b1", "c_b_pw1", 0),
             ("c_dw_b", "c_dw_b", 0), ("c_ln_g", "c_ln_g", 0), ("c_ln_b", "c_ln_b", 0),
             ("c_b2", "c_b_pw2", 0)]
    for l in range(DEPTH):
        names += [(f"xa_norm{l}", "xa_norm", l), (f"xa_mem_norm{l}", "xa_mem_norm", l),
                  (f"f_norm{l}", "f_norm", l), (f"f_dw_b{l}", "f_dw_b", l)]
    names += [("final", "final_norm", None)]
    names += [(n, n + "_2", 0) for n in
              ("norm1_g", "mu_prev", "mu_next", "w0_f", "w0_b", "a0_f", "a0_b", "k_k", "k_a",
               "r_k", "lnx_g", "lnx_b", "b_gate", "norm2_g")]
    return names


_WIDTH = {"bg_b": 512, "b_scale": 512, "c_b1": 2048, "mu_prev": 1920, "mu_next": 1920,
          "w0_f": 512, "w0_b": 512, "a0_f": 512, "a0_b": 512, "k_k": 512, "k_a": 512,
          "r_k": 512, "lnx_g": 512, "lnx_b": 512, "b_gate": 2048, "f_dw_b0": 3072,
          "f_dw_b1": 3072}


def _columns():
    at, n = {}, 0
    for key, _, _ in _vector_names():
        at[key] = n
        n += _WIDTH.get(key, 1024) // P
    for key, taps, width in (("a_conv_w", CONV_A, D), ("c_dw_w", CONV_C, D),
                             ("f_dw_w0", CONV_F, D_FF), ("f_dw_w1", CONV_F, D_FF)):
        at[key] = n
        n += taps * width // P
    for key in ("q_gain", "k_gain"):
        at[key] = n
        n += 1
    return at, n


def _plan():
    plan = [("ab_in", h) for h in range(8)] + [("pool_in", i) for i in range(2)]
    plan += [("ab_out_a", i) for i in range(4)] + [("ab_out_b", i) for i in range(2)]
    for l in range(DEPTH):
        if l == 1:
            plan += [("pw1", i) for i in range(8)] + [("pw2", i) for i in range(4)]
        plan += [(f"wk{l}", i) for i in range(4)] + [(f"wv{l}", i) for i in range(4)]
        plan += [(f"wq{l}", i) for i in range(4)] + [(f"wo{l}", i) for i in range(4)]
        for p in range(3):
            plan += [(f"up{l}", 8 * p + i) for i in range(8)] + [(f"down{l}", 4 * p + i) for i in range(4)]
    plan += [("lora", 0), ("lora", 1)]
    plan += [("rkvg", i) for i in range(8)]
    for name, n in (("na_v", 2), ("na_qk", 4), ("gate_a", 4), ("gate_b", 4), ("o_rwkv", 2), ("o_na", 2)):
        plan += [(name, i) for i in range(n)]
    plan += [("w_out2", i) for i in range(4)] + [("router", 0)]
    return plan


def _consts():
    p = np.arange(P)
    c = {"ident": np.eye(P), "head_ones": (p[:, None] // HEAD == p[None, :] // HEAD)}
    t = np.arange(16)
    for g, w in enumerate(POOL_WINDOWS):
        c[f"pool{g}"] = np.broadcast_to(1.0 / np.minimum(t + 1, w), (P, 16))
    col = np.arange(GRID_W)
    start = np.clip(col - WIN_COLS // 2, 0, GRID_W - WIN_COLS)
    inside = (col[None, :] >= start[:, None]) & (col[None, :] < start[:, None] + WIN_COLS)
    c["na_mask"] = np.where(inside[p % GRID_W], 0.0, -1e30)
    c["eps"] = np.full((P, 1), EPS)
    c["gn_eps"] = np.full((P, 1), GN_EPS)
    c["kk_eps"] = np.full((P, 1), 1e-12)
    c["ones"] = np.ones((P, P))
    c["seg8"] = np.broadcast_to((np.arange(32) % 8 != 0), (P, 32))
    c["seg4"] = np.broadcast_to((np.arange(16) % 4 != 0), (P, 16))
    return {k: np.ascontiguousarray(v, np.float32) for k, v in c.items()}


def _rwkv_consts():
    p = np.arange(P)
    t, s = p[:, None], p[None, :]
    same = t // CHUNK == s // CHUNK
    c = {"ident2": (t % HEAD == np.arange(HEAD)[None, :])}
    c["strict0"], c["incl0"] = same & (t > s), same & (t >= s)
    c["strict1"], c["incl1"] = same & (t < s), same & (t <= s)
    c["reset"] = np.broadcast_to(np.arange(S) % CHUNK != 0, (P, S))
    return {k: np.ascontiguousarray(v, np.float32) for k, v in c.items()}


def _expert_consts():
    p = np.arange(P)
    c = {"before": p[:, None] < p[None, :], "one32": np.ones((P, 32)),
         "block": np.broadcast_to(np.arange(SPARE), (P, SPARE)),
         "expert": np.broadcast_to(np.arange(N_EXPERTS), (P, N_EXPERTS)),
         "above": np.broadcast_to(N_EXPERTS - 1.0 - np.arange(N_EXPERTS), (P, N_EXPERTS)),
         "row": p[:, None] + P * np.arange(3)[None, :],
         "token": p[:, None] + P * np.arange(4)[None, :]}
    return {k: np.ascontiguousarray(v, np.float32) for k, v in c.items()}


def _level_masks():
    t, s = np.arange(P)[:, None], np.arange(P)[None, :]
    masks = []
    for l in range(LEVELS):
        half = 1 << l
        block = (t // (2 * half) == s // (2 * half)) & (t // half > s // half)
        masks += [block, block.T]
    return np.ascontiguousarray(np.stack(masks, axis=1).astype(np.float32))


def _places(arrays):
    at, n = {}, 0
    for k, v in arrays.items():
        at[k] = (n, v.shape[1])
        n += v.shape[1]
    return at, n



class Queue:

    def __init__(self, eng, sem):
        self.eng, self.sem, self.count, self.seen = eng, sem, 0, {}

    def wait(self, *tokens):
        for token in tokens:
            if token is None:
                continue
            sem, value = token
            if value > 0 and self.seen.get(sem.name, 0) < value:
                self.eng.wait_ge(sem, value)
                self.seen[sem.name] = value

    def done(self, instruction):
        instruction.then_inc(self.sem, 1)
        self.count += 1
        return (self.sem, self.count)

    def last(self):
        return (self.sem, self.count)


class Loader:

    def __init__(self, queue, sem):
        self.queue, self.sem, self.count = queue, sem, 0

    def load(self, dst, src, *after):
        self.queue.wait(*after)
        self.queue.eng.dma_start(dst, src).then_inc(self.sem, 16)
        self.count += 16
        return (self.sem, self.count)

    def indirect(self, dst, dst_rows, src, src_rows, *after, bound=None):
        self.queue.wait(*after)
        offset = lambda rows: None if rows is None else bass.IndirectOffsetOnAxis(ap=rows, axis=0)
        limit = {} if bound is None else {"bounds_check": bound, "oob_is_err": False}
        self.queue.eng.indirect_dma_start(dst, offset(dst_rows), src, offset(src_rows), **limit).then_inc(self.sem, 16)
        self.count += 16
        return (self.sem, self.count)


class Arena:

    def __init__(self, nc, stack):
        self.nc, self.stack = nc, stack

    def sb(self, name, shape, dt=F32):
        return self.stack.enter_context(self.nc.sbuf_tensor(name, shape, dt))


def build(nc, stream, vectors, consts, rconsts, x_in, mem_in, gates_w, group_w, lora_w,
          router_b, bias_na, level_masks, expert_rows, econsts, out, x_spill, y_spill, p_spill, h_rows, y_rows, slot_table):
    with ExitStack() as stack:
        def sb(name, shape, dt=F32):
            return stack.enter_context(nc.sbuf_tensor(name, shape, dt))

        def sem(name):
            return stack.enter_context(nc.semaphore(name))

        pe = Queue(nc.tensor, sem("pe_done"))
        act = Queue(nc.scalar, sem("act_done"))
        dve = Queue(nc.vector, sem("dve_done"))
        pool = Queue(nc.gpsimd, sem("pool_done"))
        sp = Queue(nc.sync, sem("sp_unused"))
        V, A, T, G = dve.eng, act.eng, pe.eng, pool.eng

        x = sb("x", [P, KT, S])
        RAW, SLOTS = 2, 3
        square = sb("square", [P, 2, S])
        rstd = sb("rstd", [P, S])
        root = sb("root", [P, S])
        col, n_vec = _columns()
        vec = sb("vec_sb", [P, n_vec])
        c_at, n_const = _places(_consts())
        cst = sb("const_sb", [P, n_const])
        bank = [stack.enter_context(nc.psum_tensor(f"bank{i}", [P, S], F32)) for i in range(8)]

        def const(name):
            a, n = c_at[name]
            return cst[:, a:a + n]

        def vcol(name, i=0):
            return vec[:, col[name] + i:col[name] + i + 1]

        ring = {}

        def open_ring(tag, limit):
            ring["stack"] = ExitStack()
            ar = Arena(nc, ring["stack"])
            ring["xg"] = (ar.sb(f"xg_hi{tag}", [P, KT, S], F32R), ar.sb(f"xg_lo{tag}", [P, KT, S], F32R))
            ring["raw"] = [ar.sb(f"w_raw{i}{tag}", [P, UNIT]) for i in range(RAW)]
            ring["hi"] = [ar.sb(f"w_hi{i}{tag}", [P, UNIT], F32R) for i in range(SLOTS)]
            ring["lo"] = [ar.sb(f"w_lo{i}{tag}", [P, UNIT], F32R) for i in range(SLOTS)]
            ring["limit"] = limit

        start = Loader(sp, sem("start_loads"))
        start.load(vec[:, :], vectors)
        start.load(cst[:, :], consts)
        started = start.load(x[:, :, :], x_in)

        plan = _plan()
        raw_load = [Loader(sp, sem(f"w_raw{i}_load")) for i in range(RAW)]
        unit_done = {}
        unit_split = {}
        unit_loaded = {}
        taken = [0]

        def load_unit(n, *after):
            before = unit_split[n - RAW] if n >= RAW else ()
            unit_loaded[n] = raw_load[n % RAW].load(ring["raw"][n % RAW][:, :], stream[n], *before, *after)

        def split_unit(n):
            r, hi, lo = ring["raw"][n % RAW], ring["hi"][n % SLOTS], ring["lo"][n % SLOTS]
            free = unit_done.get(n - SLOTS)
            act.wait(unit_loaded[n], free)
            rounded = act.done(A.activation(hi[:, :], r[:, :], ACT.Copy))
            dve.wait(rounded, free)
            rest = dve.done(V.tensor_tensor(lo[:, :], r[:, :], hi[:, :].bitcast(F32), ALU.subtract))
            unit_split[n] = (rounded, rest)
            if n + RAW < ring["limit"]:
                load_unit(n + RAW)

        def take(name, i=0):
            n = taken[0]
            assert plan[n] == (name, i), (plan[n], name, i)
            taken[0] += 1
            for m in range(n, min(n + SLOTS, ring["limit"])):
                if m not in unit_split and (m < SLOTS or m - SLOTS in unit_done):
                    split_unit(m)
            return n

        def unit(n, cols):
            return [w[n % SLOTS][:, :].rearrange("p (k c) -> p k c", c=cols) for w in (ring["hi"], ring["lo"])]

        mixers_at = plan.index(("o_rwkv", 0))
        open_ring("", mixers_at)
        for n in range(RAW):
            load_unit(n)

        bank_free = [[None]] * 8
        idle_banks = list(range(7))

        def take_bank():
            b = idle_banks.pop(0)
            pe.wait(*bank_free[b])
            return b

        def free_bank(b, *readers):
            bank_free[b] = list(readers)
            idle_banks.append(b)

        def matmul(out_ap, lhsT, rhs, first=True, last=True, **kw):
            return T.matmul(out_ap, lhsT, rhs, start=first, stop=last, skip_group_check=True, **kw)

        def split_matmul(out_ap, l_hi, l_lo, r_hi, r_lo, first, last):
            matmul(out_ap, l_hi, r_hi, first, False)
            matmul(out_ap, l_hi, r_lo, False, False)
            return matmul(out_ap, l_lo, r_hi, False, last)

        class Acts:

            def __init__(self, hi, lo, tiles):
                self.hi, self.lo, self.ready = hi, lo, [()] * tiles

        xg = Acts(*ring["xg"], KT)

        def project(n, cols, c, acts, tiles, b, width=S, first=True, last=True, k0=0):
            hi, lo = unit(n, cols)
            pe.wait(*unit_split[n])
            for i, k in enumerate(tiles):
                pe.wait(*acts.ready[k])
                mm = split_matmul(bank[b][:, 0:width], hi[:, i, c * P:(c + 1) * P],
                                  lo[:, i, c * P:(c + 1) * P], acts.hi[:, k, :], acts.lo[:, k, :],
                                  first and i == 0, last and i == len(tiles) - 1)
            token = pe.done(mm)
            unit_done[n] = token
            return token

        def split_act(acts, k, value, *after):
            act.wait(*after)
            hi = act.done(A.activation(acts.hi[:, k, :], value, ACT.Copy))
            dve.wait(hi, *after)
            lo = dve.done(V.tensor_tensor(acts.lo[:, k, :], value, acts.hi[:, k, :].bitcast(F32), ALU.subtract))
            acts.ready[k] = (hi, lo)
            return hi, lo

        square_read = [None, None]
        norm_state = {}

        def norm_tile(j, gain, x_ready, mean_only=False):
            xg_free = norm_state["xg_free"]
            act.wait(x_ready, xg_free)
            if gain is not None:
                hi = act.done(A.activation(xg.hi[:, j, :], x[:, j, :], ACT.Identity, scale=vcol(gain, j)))
            act.wait(square_read[j % 2])
            sq = act.done(A.activation(square[:, j % 2, :], x[:, j, :], ACT.Square))
            if gain is not None:
                dve.wait(hi, x_ready, xg_free)
                lo = dve.done(V.scalar_tensor_tensor(out=xg.lo[:, j, :], in0=x[:, j, :], scalar=vcol(gain, j),
                                                     in1=xg.hi[:, j, :].bitcast(F32), op0=ALU.mult,
                                                     op1=ALU.subtract))
                xg.ready[j] = (hi, lo)
            norm_state["todo"].append((j, sq))

        def norm_sums(keep=0):
            while len(norm_state["todo"]) > keep:
                j, sq = norm_state["todo"].pop(0)
                pe.wait(sq, started)
                if j == 0:
                    pe.wait(*bank_free[7])
                square_read[j % 2] = pe.done(matmul(bank[7][:, :], const("ones"), square[:, j % 2, :],
                                                    j == 0, j == KT - 1))

        def norm_begin():
            norm_state["xg_free"] = pe.last()
            norm_state["todo"] = []

        def norm_end():
            norm_sums()
            act.wait(square_read[(KT - 1) % 2], norm_state.get("rstd_read"))
            rooted = act.done(A.activation(root[:, :], bank[7][:, :], ACT.Sqrt, scale=1.0 / D, bias=const("eps")))
            bank_free[7] = [rooted]
            dve.wait(rooted)
            norm_state["rstd"] = dve.done(V.reciprocal(rstd[:, :], root[:, :]))
            norm_state["rstd_read"] = None
            return norm_state["rstd"]

        def add_to_x(j, b, mm, bias=None):
            dve.wait(mm)
            if bias is None:
                token = dve.done(V.tensor_tensor(x[:, j, :], bank[b][:, :], x[:, j, :], ALU.add))
            else:
                token = dve.done(V.scalar_tensor_tensor(out=x[:, j, :], in0=bank[b][:, :], scalar=bias,
                                                        in1=x[:, j, :], op0=ALU.add, op1=ALU.add))
            free_bank(b, token)
            return token

        def phase_wait():
            ends = [pe.last(), act.last(), dve.last()]
            for q in (act, dve, pe, pool):
                q.wait(*ends)
            return ends

        def scaled_by_rstd(dst, b, mm, *after):
            dve.wait(mm, norm_state["rstd"], *after)
            token = dve.done(V.tensor_tensor(dst, bank[b][:, :], rstd[:, :], ALU.mult))
            free_bank(b, token)
            return token

        def stt(out_ap, in0, scalar, in1, op0, op1, *after):
            dve.wait(*after)
            return dve.done(V.scalar_tensor_tensor(out=out_ap, in0=in0, scalar=scalar, in1=in1, op0=op0, op1=op1))

        def tt(out_ap, a, b_ap, op, *after):
            dve.wait(*after)
            return dve.done(V.tensor_tensor(out_ap, a, b_ap, op))

        def ts(out_ap, a, s1, s2, op0, op1, *after):
            dve.wait(*after)
            if s2 is None:
                return dve.done(V.tensor_scalar(out_ap, a, s1, None, op0))
            return dve.done(V.tensor_scalar(out_ap, a, s1, s2, op0, op1))

        def activate(out_ap, a, func, *after, **kw):
            act.wait(*after)
            return act.done(A.activation(out_ap, a, func, **kw))

        def copy(engine, out_ap, a, *after):
            engine.wait(*after)
            if engine is act:
                return act.done(A.activation(out_ap, a, ACT.Copy))
            return engine.done(engine.eng.tensor_copy(out_ap, a))

        def causal_taps(dst, src, weight, taps, ready):
            k_last = taps[0]
            for k in taps[1]:
                s = k_last - k
                ready = stt(dst[:, s:], src[:, 0:S - s], weight(k), dst[:, s:], ALU.mult, ALU.add, ready)
            return ready

        def out_projection(names, acts, tiles_of, hook=None, bias=None):
            for name, n_units, cols in names:
                for i in range(n_units):
                    n = take(name, i)
                    for c in range(cols // P):
                        j = i * cols // P + c
                        b = take_bank()
                        mm = project(n, cols, c, acts, tiles_of[name], b)
                        token = add_to_x(j, b, mm, bias(j) if bias and name == names[-1][0] else None)
                        if hook and name == names[-1][0]:
                            norm_sums(0)
                            hook(j, token)

        def next_norm(gain):
            def hook(j, token):
                if j == 0:
                    norm_begin_late()
                norm_tile(j, gain, token)
            return hook

        def norm_begin_late():
            norm_state["xg_free"] = norm_state["xg_last"]
            norm_state["todo"] = []

        def mixer():
            for q in (act, dve, pe, pool):
                q.wait(started)
            norm_begin()
            for j in range(KT):
                norm_tile(j, "ab_norm", started)
                norm_sums(1)
            norm_end()

            with ExitStack() as ph:
                ar = Arena(nc, ph)
                y_hi, y_lo = ar.sb("ab_y_hi", [P, KT, S], F32R), ar.sb("ab_y_lo", [P, KT, S], F32R)
                xr = ar.sb("ab_xr", [P, 2, S])
                zr = ar.sb("ab_zr", [P, 2, S])
                gated = ar.sb("ab_gated", [P, 4, S])
                ga = ar.sb("ab_ga", [P, 4, S])
                gate = ar.sb("ab_gate", [P, 4, S])
                tmp = [ar.sb(f"ab_tmp{i}", [P, S]) for i in range(3)]
                gw = ar.sb("ab_gate_w", [P, 2, 2, P])
                sp8 = ar.sb("ab_decay", [P, 4 * KT])
                pool_w = ar.sb("ab_group_w", [P, 4, P])
                y = Acts(y_hi, y_lo, KT)
                gw_load = [Loader(sp, sem(f"ab_gate_w{i}")) for i in range(2)]
                group_loaded = Loader(sp, sem("ab_group_w_load")).load(pool_w[:, :, :], group_w)

                lam = vec[:, col["lam"]:col["lam"] + KT]
                e_, n_, s_, q_ = [sp8[:, i * KT:(i + 1) * KT] for i in range(4)]
                t0 = ts(n_, lam, -1.0, None, ALU.mult, None)
                t1 = tt(s_, lam, n_, ALU.max, t0)
                t2 = activate(e_, s_, ACT.Exp, t1, scale=-1.0)
                t3 = ts(s_, e_, 2.0, None, ALU.add, None, t2)
                dve.wait(t3)
                t3 = dve.done(V.reciprocal(q_, s_))
                t3 = tt(s_, e_, q_, ALU.mult, t3)
                t3 = tt(q_, s_, s_, ALU.mult, t3)
                t4 = ts(e_, q_, 1.0 / 17, 1.0 / 15, ALU.mult, ALU.add, t3)
                for k in (13, 11, 9, 7, 5, 3, 1):
                    t4 = tt(e_, e_, q_, ALU.mult, t4)
                    t4 = ts(e_, e_, 1.0 / k, None, ALU.add, None, t4)
                t4 = tt(e_, e_, s_, ALU.mult, t4)
                t5 = ts(n_, n_, 0.0, None, ALU.max, None)
                t4 = stt(e_, e_, 2.0, n_, ALU.mult, ALU.add, t4, t5)
                c_pos = ts(s_, e_, 8.0, None, ALU.mult, None, t4)
                c_neg = ts(q_, e_, -8.0, None, ALU.mult, None, t4)
                decay_pos, decay_neg = s_, q_

                gate_w_read = [None, None]
                gated_free = [None] * 4
                xr_read = [None, None]
                heads, pools = {}, {}

                def project_head(h):
                    n = take("ab_in", h)
                    b_rec = take_bank()
                    mm_rec = project(n, 2 * P, 1, xg, range(KT), b_rec)
                    b_gate = take_bank()
                    heads[h] = (b_rec, mm_rec, b_gate, project(n, 2 * P, 0, xg, range(KT), b_gate))

                def project_pool(i):
                    n = take("pool_in", i)
                    for c in range(2):
                        b = take_bank()
                        pools[2 * i + c] = (b, project(n, 2 * P, c, xg, range(KT), b))
                    norm_state["xg_last"] = pe.last()

                for half in range(2):
                    gate_ready, gated_ready, ga_ready = [None] * 4, [None] * 4, [None] * 4
                    for h4 in range(4):
                        h = 4 * half + h4
                        i = h % 2
                        gw_loaded = gw_load[i].load(gw[:, i, :, :], gates_w[:, h, :, :], gate_w_read[i])
                        if h not in heads:
                            project_head(h)
                        b_rec, mm_rec, b_gate, mm = heads[h]
                        zr_ready = scaled_by_rstd(zr[:, i, :], b_rec, mm_rec, dve.last())
                        w = lambda k, h=h: vcol("a_conv_w", CONV_A * h + k)
                        ready = activate(xr[:, i, :], zr[:, i, :], ACT.Identity, zr_ready, xr_read[i],
                                         scale=w(CONV_A - 1), bias=vcol("a_conv_b", h))
                        ready = causal_taps(xr[:, i, :], zr[:, i, :], w, (CONV_A - 1, range(CONV_A - 1)), ready)
                        gate_ready[h4] = scaled_by_rstd(gate[:, h4, :], b_gate, mm, gated_free[h4])
                        pe.wait(gw_loaded, ready)
                        b_gx = take_bank()
                        mm_gx = pe.done(matmul(bank[b_gx][:, :], gw[:, i, 0, :], xr[:, i, :]))
                        b_ga = take_bank()
                        mm_ga = pe.done(matmul(bank[b_ga][:, :], gw[:, i, 1, :], xr[:, i, :]))
                        gate_w_read[i] = mm_ga
                        gx = activate(gated[:, h4, :], bank[b_gx][:, :], ACT.Sigmoid, mm_gx, gated_free[h4],
                                      bias=vcol("gx_b", h))
                        free_bank(b_gx, gx)
                        ga_ready[h4] = activate(ga[:, h4, :], bank[b_ga][:, :], ACT.Sigmoid, mm_ga, bias=vcol("ga_b", h))
                        free_bank(b_ga, ga_ready[h4])
                        gated_ready[h4] = tt(gated[:, h4, :], gated[:, h4, :], xr[:, i, :], ALU.mult, gx, ready)
                        xr_read[i] = gated_ready[h4]
                    xr_last_read = pe.last()
                    for ahead in range(2):
                        if half == 0:
                            project_head(4 + ahead)
                        else:
                            project_pool(ahead)
                    mult = [xr[:, 0, :], xr[:, 1, :], zr[:, 0, :], zr[:, 1, :]]
                    m_ready, root_ready, gelu_ready = [None] * 4, [None] * 4, [None] * 4
                    act.wait(dve.last(), xr_last_read, c_pos, c_neg)
                    for h4 in range(4):
                        h = 4 * half + h4
                        th = activate(mult[h4], ga[:, h4, :], ACT.Tanh, ga_ready[h4],
                                      scale=decay_pos[:, h:h + 1])
                        a_ready = activate(ga[:, h4, :], ga[:, h4, :], ACT.Exp, th, scale=decay_neg[:, h:h + 1])
                        m = tt(tmp[1][:, :], ga[:, h4, :], ga[:, h4, :], ALU.mult, a_ready, dve.last())
                        m_ready[h4] = stt(mult[h4], tmp[1][:, :], 1.0, mult[h4], ALU.add, ALU.mult, m)
                    for h4 in range(4):
                        root_ready[h4] = activate(mult[h4], mult[h4], ACT.Sqrt, m_ready[h4])
                    for h4 in range(4):
                        gelu_ready[h4] = activate(gate[:, h4, :], gate[:, h4, :], ACT.Gelu_apprx_tanh,
                                                  gate_ready[h4])
                    for h4 in range(4):
                        bx = tt(gated[:, h4, :], gated[:, h4, :], mult[h4], ALU.mult, root_ready[h4],
                                gated_ready[h4])
                        dve.wait(bx)
                        scan = dve.done(V.tensor_tensor_scan(mult[h4], ga[:, h4, :], gated[:, h4, :], 0.0,
                                                             ALU.mult, ALU.add))
                        ya = tt(gate[:, h4, :], gate[:, h4, :], mult[h4], ALU.mult, gelu_ready[h4], scan)
                        hi, lo = split_act(y, 4 * half + h4, gate[:, h4, :], ya)
                        gated_free[h4] = lo
                    xr_read = [lo, lo]
                pooled = []
                u_sb, s_sb = ga, gated
                for i in range(2):
                    for c in range(2):
                        g = 2 * i + c
                        b, mm = pools[g]
                        u = scaled_by_rstd(u_sb[:, g, :], b, mm, act.last())
                        src, ready = u_sb[:, g, :], u
                        scratch = [s_sb[:, g, :], tmp[0][:, :]] if g % 2 else [s_sb[:, g, :], tmp[1][:, :]]
                        steps = g + 1
                        for st in range(steps):
                            dst = scratch[(steps - 1 - st) % 2]
                            sh = 1 << st
                            ready = tt(dst[:, sh:], src[:, sh:], src[:, 0:S - sh], ALU.add, ready)
                            ready = copy(dve, dst[:, 0:sh], src[:, 0:sh], ready)
                            src = dst
                        w_ = POOL_WINDOWS[g]
                        fix = tt(tmp[2][:, 0:16], src[:, 0:16], const(f"pool{g}"), ALU.mult, ready)
                        ready = stt(src, src, 1.0 / w_, u_sb[:, g, :], ALU.mult, ALU.subtract, fix)
                        ready = tt(src[:, 0:16], tmp[2][:, 0:16], u_sb[:, g, 0:16], ALU.subtract, ready)
                        pe.wait(group_loaded, ready)
                        b = take_bank()
                        mm = pe.done(matmul(bank[b][:, :], pool_w[:, g, :], src))
                        ready = ts(u_sb[:, g, :], bank[b][:, :], vcol("bg_b", g), vcol("b_scale", g), ALU.add,
                                   ALU.mult, mm)
                        free_bank(b, ready)
                        pooled.append(ready)
                for i in range(4):
                    n = take("ab_out_a", i)
                    for c in range(2):
                        b = take_bank()
                        mm = project(n, 2 * P, c, y, range(KT), b)
                        add_to_x(2 * i + c, b, mm)
                y_a_read = pe.last()
                for g in range(4):
                    act.wait(y_a_read)
                    dve.wait(y_a_read)
                    split_act(y, g, u_sb[:, g, :], pooled[g])
                out_projection([("ab_out_b", 2, S)], y, {"ab_out_b": range(4)}, next_norm("xa_norm0"))
                norm_end()

        def cross_attention(l):
            phase_wait()
            with ExitStack() as ph:
                ar = Arena(nc, ph)
                o_hi, o_lo = ar.sb(f"xa{l}_o_hi", [P, KT, S], F32R), ar.sb(f"xa{l}_o_lo", [P, KT, S], F32R)
                o = Acts(o_hi, o_lo, KT)
                kT = ar.sb(f"xa{l}_k", [P, KT, N_MEM])
                v = ar.sb(f"xa{l}_v", [P, 2, D])
                with ExitStack() as inner:
                    ar2 = Arena(nc, inner)
                    mem = ar2.sb(f"xa{l}_mem", [P, 2, N_MEM])
                    m_hi = ar2.sb(f"xa{l}_m_hi", [P, KT, N_MEM], F32R)
                    m_lo = ar2.sb(f"xa{l}_m_lo", [P, KT, N_MEM], F32R)
                    m_rstd = ar2.sb(f"xa{l}_m_rstd", [P, N_MEM])
                    m_col = ar2.sb(f"xa{l}_m_rstd_col", [P, 2])
                    m = Acts(m_hi, m_lo, KT)
                    mem_load = [Loader(sp, sem(f"xa{l}_mem_load{i}")) for i in range(2)]
                    b_sum = take_bank()
                    mem_read = [(pe.last(), act.last(), dve.last())] * 2
                    for k in range(KT):
                        i = k % 2
                        loaded = mem_load[i].load(mem[:, i, :], mem_in[:, k, :], *mem_read[i])
                        hi = activate(m_hi[:, k, :], mem[:, i, :], ACT.Identity, loaded,
                                      scale=vcol(f"xa_mem_norm{l}", k))
                        lo = stt(m_lo[:, k, :], mem[:, i, :], vcol(f"xa_mem_norm{l}", k),
                                 m_hi[:, k, :].bitcast(F32), ALU.mult, ALU.subtract, hi)
                        m.ready[k] = (hi, lo)
                        sq = activate(square[:, i, 0:N_MEM], mem[:, i, :], ACT.Square, square_read[i])
                        mem_read[i] = (sq, lo)
                        pe.wait(sq)
                        square_read[i] = pe.done(matmul(bank[b_sum][:, 0:N_MEM], const("ones"),
                                                        square[:, i, 0:N_MEM], k == 0, k == KT - 1))
                    r = activate(m_rstd[:, :], bank[b_sum][:, 0:N_MEM], ACT.Sqrt, square_read[1],
                                 scale=1.0 / D, bias=const("eps"))
                    free_bank(b_sum, r)
                    dve.wait(r)
                    m_ready = dve.done(V.reciprocal(m_rstd[:, :], m_rstd[:, :]))
                    b_col = take_bank()
                    pe.wait(m_ready)
                    for t in range(2):
                        mm = matmul(bank[b_col][:, t:t + 1], m_rstd[0:1, t * P:(t + 1) * P],
                                    const("ident")[0:1, 0:1])
                    mm = pe.done(mm)
                    m_col_ready = copy(dve, m_col[:, :], bank[b_col][:, 0:2], mm)
                    free_bank(b_col, m_col_ready)
                    for i in range(4):
                        n = take(f"wk{l}", i)
                        for c in range(2):
                            j = 2 * i + c
                            b = take_bank()
                            mm = project(n, 2 * P, c, m, range(KT), b, width=N_MEM)
                            k_ready = tt(kT[:, j, :], bank[b][:, 0:N_MEM], m_rstd[:, :], ALU.mult, mm, m_ready)
                            free_bank(b, k_ready)
                    for i in range(4):
                        n = take(f"wv{l}", i)
                        hi, lo = unit(n, 2 * P)
                        pe.wait(*unit_split[n])
                        for t in range(2):
                            b = take_bank()
                            for k in range(KT):
                                rows = slice(t * P, (t + 1) * P)
                                mm = split_matmul(bank[b][:, 0:2 * P], m_hi[:, k, rows], m_lo[:, k, rows],
                                                  hi[:, k, :], lo[:, k, :], k == 0, k == KT - 1)
                            mm = pe.done(mm)
                            unit_done[n] = mm
                            v_ready = ts(v[:, t, i * 2 * P:(i + 1) * 2 * P], bank[b][:, 0:2 * P],
                                         m_col[:, t:t + 1], None, ALU.mult, None, mm, m_col_ready)
                            free_bank(b, v_ready)
                    inner_end = [pe.last(), act.last(), dve.last()]
                q_sb = ar.sb(f"xa{l}_q", [P, 2, 2, S])
                prob = ar.sb(f"xa{l}_p", [P, 2, 2, N_MEM])
                pT = ar.sb(f"xa{l}_pT", [P, 2, S])
                stat = ar.sb(f"xa{l}_stat", [P, 2, 8])
                act.wait(*inner_end)
                dve.wait(*inner_end)
                qh_read = [None, None]
                prob_read = [None, None]
                pT_read = None

                def queries(h):
                    n = take(f"wq{l}", h)
                    for c in range(2):
                        b = take_bank()
                        mm = project(n, 2 * P, c, xg, range(KT), b)
                        ready = scaled_by_rstd(q_sb[:, h % 2, c, :], b, mm, qh_read[h % 2])
                    return ready

                q_ready = queries(0)
                for h in range(XA_HEADS):
                    q_now = q_ready
                    b_s = [take_bank(), take_bank()]
                    pe.wait(q_now, k_ready)
                    scored = [None, None]
                    for pair in range(2):
                        for u in range(2):
                            qt = 2 * pair + u
                            for c in range(2):
                                mm = matmul(bank[b_s[pair]][:, u * N_MEM:(u + 1) * N_MEM],
                                            q_sb[:, h % 2, c, qt * P:(qt + 1) * P], kT[:, 2 * h + c, :],
                                            c == 0, c == 1)
                        scored[pair] = pe.done(mm)
                    qh_read[h % 2] = pe.last()
                    if h + 1 < XA_HEADS:
                        q_ready = queries(h + 1)
                    else:
                        norm_state["xg_last"] = unit_done[taken[0] - 1]
                    b_t = [take_bank(), take_bank()]
                    for pair in range(2):
                        st = stat[:, pair, :]
                        sc = bank[b_s[pair]][:, :].rearrange("p (u m) -> p u m", u=2)
                        dve.wait(scored[pair], prob_read[pair])
                        top = dve.done(V.tensor_reduce(st[:, 0:2], sc, AX_X, ALU.max))
                        top = ts(st[:, 2:4], st[:, 0:2], -XA_HD ** -0.5, None, ALU.mult, None, top)
                        for u in range(2):
                            e = activate(prob[:, pair, u, :], sc[:, u, :], ACT.Exp, top, prob_read[pair],
                                         scale=XA_HD ** -0.5, bias=st[:, 2 + u:3 + u],
                                         accum_out=st[:, 4 + u:5 + u])
                        free_bank(b_s[pair], e)
                        dve.wait(e)
                        r = dve.done(V.reciprocal(st[:, 6:8], st[:, 4:6]))
                        for u in range(2):
                            r2 = ts(prob[:, pair, u, :], prob[:, pair, u, :], st[:, 6 + u:7 + u], None,
                                    ALU.mult, None, r)
                        pe.wait(r2)
                        for u in range(2):
                            for t in range(2):
                                qt = 2 * pair + u
                                mm = T.transpose(bank[b_t[t]][:, qt * P:(qt + 1) * P],
                                                 prob[:, pair, u, t * P:(t + 1) * P], const("ident"))
                        prob_read[pair] = pe.done(mm)
                    for t in range(2):
                        p_ready = copy((act, dve)[t], pT[:, t, :], bank[b_t[t]][:, :], pe.last(), pT_read)
                        free_bank(b_t[t], p_ready)
                        pe.wait(p_ready)
                    for c in range(2):
                        j = 2 * h + c
                        b = take_bank()
                        for t in range(2):
                            pe.wait(v_ready)
                            mm = matmul(bank[b][:, :], v[:, t, j * P:(j + 1) * P], pT[:, t, :], t == 0, t == 1)
                        mm = pe.done(mm)
                        pT_read = mm
                        act.wait(mm)
                        hi = act.done(A.activation(o_hi[:, j, :], bank[b][:, :], ACT.Copy))
                        lo = tt(o_lo[:, j, :], bank[b][:, :], o_hi[:, j, :].bitcast(F32), ALU.subtract, hi)
                        o.ready[j] = (hi, lo)
                        free_bank(b, hi, lo)
                out_projection([(f"wo{l}", 4, 2 * P)], o, {f"wo{l}": range(KT)}, next_norm(f"f_norm{l}"))
                norm_end()

        def conv_ffn(l, next_gain):
            phase_wait()
            with ExitStack() as ph:
                ar = Arena(nc, ph)
                hid = [Acts(ar.sb(f"f{l}_h_hi{i}", [P, KT, S], F32R), ar.sb(f"f{l}_h_lo{i}", [P, KT, S], F32R), KT)
                       for i in range(2)]
                z = ar.sb(f"f{l}_z", [P, 2, S])
                g = ar.sb(f"f{l}_g", [P, 2, S])
                u = ar.sb(f"f{l}_u", [P, 2, S])
                free = [None, None]
                hid_free = [None, None]
                for p in range(3):
                    h = hid[p % 2]
                    for j in range(KT):
                        i = j % 2
                        ch = KT * p + j
                        n = take(f"up{l}", ch)
                        b_g = take_bank()
                        mm_g = project(n, 2 * P, 0, xg, range(KT), b_g)
                        b_u = take_bank()
                        mm_u = project(n, 2 * P, 1, xg, range(KT), b_u)
                        norm_state["xg_last"] = mm_u
                        w = lambda k, ch=ch: vcol(f"f_dw_w{l}", CONV_F * ch + k)
                        ready = scaled_by_rstd(z[:, i, :], b_g, mm_g, free[i])
                        ready = activate(g[:, i, :], z[:, i, :], ACT.Identity, ready, free[i],
                                         scale=w(CONV_F - 1), bias=vcol(f"f_dw_b{l}", ch))
                        ready = causal_taps(g[:, i, :], z[:, i, :], w, (CONV_F - 1, range(CONV_F - 1)), ready)
                        ge = activate(g[:, i, :], g[:, i, :], ACT.Gelu_apprx_tanh, ready)
                        u_ready = scaled_by_rstd(u[:, i, :], b_u, mm_u, free[i])
                        prod = tt(u[:, i, :], u[:, i, :], g[:, i, :], ALU.mult, ge, u_ready)
                        hi, lo = split_act(h, j, u[:, i, :], prod, hid_free[p % 2])
                        free[i] = lo
                    for i in range(4):
                        n = take(f"down{l}", 4 * p + i)
                        for c in range(2):
                            j = 2 * i + c
                            b = take_bank()
                            mm = project(n, 2 * P, c, h, range(KT), b)
                            token = add_to_x(j, b, mm)
                            if p == 2:
                                if j == 0:
                                    norm_begin_late()
                                norm_sums(0)
                                norm_tile(j, next_gain, token)
                    hid_free[p % 2] = pe.last()
                norm_end()

        def conformer():
            phase_wait()
            with ExitStack() as ph:
                ar = Arena(nc, ph)
                h_all = ar.sb("c_h", [P, KT, S])
                s_hi, s_lo = ar.sb("c_s_hi", [P, KT, S], F32R), ar.sb("c_s_lo", [P, KT, S], F32R)
                s = Acts(s_hi, s_lo, KT)
                t1 = ar.sb("c_t1", [P, 2, S])
                t2 = ar.sb("c_t2", [P, 2, S])
                mu = ar.sb("c_mu", [P, S])
                diag = ar.sb("c_diag", [P, 4, P])
                free = [None, None]
                diag_read = [None] * 4
                n_diag = 0
                h_ready = [None] * KT
                for j in range(KT):
                    i = j % 2
                    n = take("pw1", j)
                    b1 = take_bank()
                    mm1 = project(n, 2 * P, 0, xg, range(KT), b1)
                    b2 = take_bank()
                    mm2 = project(n, 2 * P, 1, xg, range(KT), b2)
                    norm_state["xg_last"] = mm2
                    r2 = scaled_by_rstd(t2[:, i, :], b2, mm2, free[i])
                    r2 = activate(t2[:, i, :], t2[:, i, :], ACT.Sigmoid, r2, bias=vcol("c_b1", KT + j))
                    r1 = scaled_by_rstd(t1[:, i, :], b1, mm1, free[i])
                    r1 = stt(t1[:, i, :], t1[:, i, :], vcol("c_b1", j), t2[:, i, :], ALU.add, ALU.mult, r1, r2)
                    w = lambda k, j=j: vcol("c_dw_w", CONV_C * j + k)
                    last = activate(h_all[:, j, :], t1[:, i, :], ACT.Identity, r1,
                                    scale=w(CONV_C - 1), bias=vcol("c_dw_b", j))
                    b = take_bank()
                    order = list(range(CONV_C_PE))[::-1]
                    base = CONV_C - 1 - order[0]
                    for m, k in enumerate(order):
                        d = n_diag % 4
                        n_diag += 1
                        dg = activate(diag[:, d, :], const("ident"), ACT.Copy, diag_read[d], scale=w(k))
                        pe.wait(dg, r1)
                        sh = CONV_C - 1 - k
                        mm = matmul(bank[b][:, sh:], diag[:, d, :], t1[:, i, 0:S - sh], m == 0,
                                    m == len(order) - 1)
                        diag_read[d] = pe.done(mm)
                    ready = causal_taps(h_all[:, j, :], t1[:, i, :], w,
                                        (CONV_C - 1, range(CONV_C_PE, CONV_C - 1)), last)
                    ready = tt(h_all[:, j, base:], bank[b][:, base:], h_all[:, j, base:], ALU.add, diag_read[d],
                               ready)
                    free_bank(b, ready)
                    free[i] = ready
                    h_ready[j] = ready
                b = take_bank()
                for j in range(KT):
                    pe.wait(h_ready[j])
                    mm = matmul(bank[b][:, :], const("ones"), h_all[:, j, :], j == 0, j == KT - 1)
                mm = pe.done(mm)
                mean = activate(mu[:, :], bank[b][:, :], ACT.Copy, mm, scale=1.0 / D)
                free_bank(b, mean)
                b = take_bank()
                for j in range(KT):
                    h_ready[j] = tt(h_all[:, j, :], h_all[:, j, :], mu[:, :], ALU.subtract, mean)
                    sq = activate(square[:, j % 2, :], h_all[:, j, :], ACT.Square, h_ready[j], square_read[j % 2])
                    pe.wait(sq)
                    square_read[j % 2] = pe.done(matmul(bank[b][:, :], const("ones"), square[:, j % 2, :],
                                                        j == 0, j == KT - 1))
                rt = activate(mu[:, :], bank[b][:, :], ACT.Sqrt, pe.last(), dve.last(), scale=1.0 / D,
                              bias=const("eps"))
                free_bank(b, rt)
                dve.wait(rt)
                inv = dve.done(V.reciprocal(t1[:, 0, :], mu[:, :]))
                for j in range(KT):
                    r = stt(h_all[:, j, :], h_all[:, j, :], vcol("c_ln_g", j), t1[:, 0, :], ALU.mult, ALU.mult, inv)
                    r = activate(h_all[:, j, :], h_all[:, j, :], ACT.Silu, r, bias=vcol("c_ln_b", j))
                    split_act(s, j, h_all[:, j, :], r)
                out_projection([("pw2", 4, 2 * P)], s, {"pw2": range(KT)}, next_norm("xa_norm1"),
                               bias=lambda j: vcol("c_b2", j))
                norm_end()

        def final_norm():
            rstd_ready = norm_state["rstd"]
            norm_state["xg_free"] = norm_state["xg_last"]
            norm_state["todo"] = []
            for j in range(KT):
                token = stt(x[:, j, :], x[:, j, :], vcol("final", j), rstd[:, :], ALU.mult, ALU.mult, rstd_ready,
                            act.last())
                norm_tile(j, "norm1_g", token)
                norm_sums(1)
            norm_sums()
            dve.wait(dve.last())
            norm_end()

        def rstd_by_token(dst):
            b = take_bank()
            pe.wait(norm_state["rstd"])
            for t in range(4):
                mm = matmul(bank[b][:, t:t + 1], rstd[0:1, t * P:(t + 1) * P], const("ident")[0:1, 0:1])
            mm = pe.done(mm)
            token = copy(dve, dst, bank[b][:, 0:4], mm)
            free_bank(b, token)
            return token

        def inverse_root(dst, tmp_ap, b, mm, scale, eps, *after):
            r = activate(tmp_ap, bank[b][:, :], ACT.Sqrt, mm, *after, scale=scale, bias=const(eps))
            free_bank(b, r)
            dve.wait(r, *after)
            return dve.done(V.reciprocal(dst, tmp_ap))

        def second_projections():
            ends = phase_wait()
            spill = Loader(sp, sem("x_spill_store"))
            spilled = spill.load(x_spill, x[:, :, :], *ends)
            with ExitStack() as ph:
                ar = Arena(nc, ph)
                STAGES = 6
                stage_sb = ar.sb("p_stage", [P, STAGES, S])
                zt = ar.sb("p_shift", [P, 2, S])
                mu0 = ar.sb("p_mu0", [P, 15])
                r_col = ar.sb("p_rstd_col", [P, 4])
                gain8 = ar.sb("p_gain8", [P, 1])
                stores = [Loader(sp, sem(f"p_store{i}")) for i in range(STAGES)]
                stored = [None] * STAGES
                used, shifts = [0], [0]
                c2 = tt(mu0[:, :], vec[:, col["mu_prev"]:col["mu_prev"] + 15],
                        vec[:, col["mu_next"]:col["mu_next"] + 15], ALU.add)
                c2 = ts(mu0[:, :], mu0[:, :], -1.0, 1.0, ALU.mult, ALU.add, c2)
                g8 = ts(gain8[:, :], vcol("q_gain"), HEAD ** -0.5, None, ALU.mult, None)
                dve.wait(c2, g8, spilled)
                act.wait(spilled)

                def next_stage():
                    i = used[0] % STAGES
                    used[0] += 1
                    return i, stage_sb[:, i, :]

                def store(i, row, *ready):
                    stored[i] = stores[i].load(p_spill[row], stage_sb[:, i, :], *ready)

                def shifted(dst, n, c, m, *after):
                    i = shifts[0] % 2
                    shifts[0] += 1
                    b = take_bank()
                    mm = project(n, 2 * P, c, xg, range(KT), b)
                    z = scaled_by_rstd(zt[:, i, :], b, mm, dve.last())
                    d = activate(dst, zt[:, i, :], ACT.Copy, z, *after, scale=mu0[:, m:m + 1])
                    d = stt(dst[:, 1:], zt[:, i, 0:S - 1], vcol("mu_prev", m), dst[:, 1:], ALU.mult, ALU.add, d)
                    return stt(dst[:, 0:S - 1], zt[:, i, 1:], vcol("mu_next", m), dst[:, 0:S - 1], ALU.mult,
                               ALU.add, d)

                n = take("lora", 0)
                z = shifted(x[:, 0, :], n, 0, 12)
                activate(x[:, 0, :], x[:, 0, :], ACT.Tanh, z)
                shifted(x[:, 1, :], n, 1, 13)
                n = take("lora", 1)
                z = shifted(x[:, 2, :], n, 0, 14)
                activate(x[:, 2, :], x[:, 2, :], ACT.Sigmoid, z)
                for t in range(4):
                    n = take("rkvg", 2 * t)
                    for c in range(3):
                        if c == 2:
                            n = take("rkvg", 2 * t + 1)
                        i, dst = next_stage()
                        r = shifted(dst, n, c % 2, 4 * c + t, stored[i])
                        store(i, 4 * c + t, r)
                col_ready = rstd_by_token(r_col[:, :])
                for i in range(2):
                    n = take("na_v", i)
                    hi, lo = unit(n, 2 * P)
                    pe.wait(*unit_split[n])
                    for t in range(4):
                        b = take_bank()
                        rows = slice(t * P, (t + 1) * P)
                        for k in range(KT):
                            mm = split_matmul(bank[b][:, 0:2 * P], xg.hi[:, k, rows], xg.lo[:, k, rows],
                                              hi[:, k, :], lo[:, k, :], k == 0, k == KT - 1)
                        mm = pe.done(mm)
                        unit_done[n] = mm
                        s_i, dst = next_stage()
                        r = ts(dst[:, 0:2 * P], bank[b][:, 0:2 * P], r_col[:, t:t + 1], None, ALU.mult, None, mm,
                               col_ready, stored[s_i])
                        free_bank(b, r)
                        stored[s_i] = stores[s_i].load(p_spill[36 + t, :, i * 2 * P:(i + 1) * 2 * P],
                                                       dst[:, 0:2 * P], r)
                for t in range(4):
                    n = take("na_qk", t)
                    for c in range(2):
                        i, dst = next_stage()
                        b = take_bank()
                        mm = project(n, 2 * P, c, xg, range(KT), b)
                        z = scaled_by_rstd(dst, b, mm, stored[i])
                        sq = activate(square[:, c, :], dst, ACT.Square, z, dve.last())
                        b = take_bank()
                        pe.wait(sq)
                        mm = pe.done(matmul(bank[b][:, :], const("head_ones"), square[:, c, :]))
                        inv = inverse_root(square[:, c, :], root[:, :], b, mm, 1.0 / HEAD, "eps", dve.last())
                        r = stt(dst, dst, gain8[:, :] if c == 0 else vcol("k_gain"), square[:, c, :], ALU.mult,
                                ALU.mult, inv)
                        store(i, 12 + 4 * c + t, r)
                for side, name in enumerate(("gate_a", "gate_b")):
                    for u in range(4):
                        n = take(name, u)
                        for c in range(2):
                            j = 2 * u + c
                            i, dst = next_stage()
                            b = take_bank()
                            mm = project(n, 2 * P, c, xg, range(KT), b)
                            r = scaled_by_rstd(dst, b, mm, stored[i])
                            r = activate(dst, dst, ACT.Sigmoid, r, bias=vcol("b_gate", KT * side + j))
                            store(i, 20 + KT * side + j, r)
                return stored

        def mixers(p_stored):
            ends = list(phase_wait()) + list(p_stored)
            with ExitStack() as ph:
                ar = Arena(nc, ph)
                for q in (pe, act, dve, pool, sp):
                    q.wait(*ends)
                rwkv_of, tail_of = rwkv(ar)
                na = neighbourhood(ar)
                y_tokens = {}

                def advance(active):
                    for g in list(active):
                        try:
                            next(g)
                        except StopIteration:
                            active.remove(g)

                others = [na]
                for t in range(4):
                    dirs = rwkv_of(t)
                    while dirs:
                        advance(dirs)
                        advance(others)
                    others.append(tail_of(t, y_tokens))
                while others:
                    advance(others)
                return y_tokens["rwkv"], y_tokens_na

        def rwkv(ar):
            rc_at, n_rc = _places(_rwkv_consts())
            rc = ar.sb("rw_constants", [P, n_rc])
            masks = ar.sb("rw_level_masks", [P, 2 * LEVELS, P], U8)
            up_w = ar.sb("rw_lora_w", [P, 3, RW])
            omka = ar.sb("rw_omka", [P, 4])
            rkv = ar.sb("rw_rkv", [P, 2, 3, S])
            kkb = ar.sb("rw_kk", [P, S])
            ksums = ar.sb("rw_ksum", [P, 2, S])
            tokV = ar.sb("rw_tok_V", [P, 4, P])
            tail_sb = ar.sb("rw_tail", [P, 2, S])
            wl, al, gl = x[:, 0, :], x[:, 1, :], x[:, 2, :]
            bufs = []
            for d in range(2):
                one = {m: ar.sb(f"rw_{m}{d}", [P, S]) for m in ("R", "A", "B", "K", "Bh", "Kh")}
                one.update({f"tok{m}": ar.sb(f"rw_tok{m}{d}", [P, 4, P]) for m in "BK"})
                one.update({m: ar.sb(f"rw_{m}{d}", [P, 2, 4, P]) for m in
                            ("GA", "UW", "LT", "X", "XT", "U", "Lrb", "Lrk")})
                one.update({m: ar.sb(f"rw_{m}{d}", [P, 8, HEAD]) for m in ("MT", "N", "S")})
                one["DC"] = ar.sb(f"rw_DC{d}", [P, 8])
                bufs.append(one)
            temps = [[x[:, 3, :], x[:, 4, :], x[:, 5, :], x[:, 6, :]],
                     [x[:, 7, :], square[:, 0, :], square[:, 1, :], root[:, :]]]

            def rconst(name):
                a, n = rc_at[name]
                return rc[:, a:a + n]

            ld = Loader(sp, sem("rw_loads"))
            ld.load(rc[:, :], rconsts)
            masks_f32 = x[:, 3:6, :].rearrange("p a b -> p (a b)")
            ld.load(masks_f32, level_masks.rearrange("p m c -> p (m c)"))
            loaded = ld.load(up_w[:, :, :], lora_w)
            for q in (pe, act, dve, pool):
                q.wait(loaded)
            masks_ready = copy(dve, masks[:, :, :].rearrange("p m c -> p (m c)"), masks_f32)
            c1 = ts(omka[:, :], vec[:, col["k_a"]:col["k_a"] + 4], -1.0, 1.0, ALU.mult, ALU.add)
            dve.wait(c1)
            act.wait(masks_ready)
            rkv_loads = [[Loader(sp, sem(f"rw_load{i}{m}")) for m in range(3)] for i in range(2)]
            store = Loader(sp, sem("ya_store"))
            tail_done = [None, None, None, None]
            shared = {"kk": None, "tokV_read": None, "dirs_end": None}

            def four(ap):
                return ap.unsqueeze(1).to_broadcast([P, 4, P])

            def quad(b):
                return bank[b][:, :].rearrange("p (t c) -> p t c", t=4)

            def transposed(dst_of, src, ready, engine, *after):
                b = take_bank()
                pe.wait(ready)
                for t in range(4):
                    mm = T.transpose(bank[b][:, t * P:(t + 1) * P], src[:, t * P:(t + 1) * P], const("ident"))
                mm = pe.done(mm)
                token = copy(engine, dst_of, quad(b), mm, *after)
                free_bank(b, token)
                return token

            def load_rkv(t, *after):
                i = t % 2
                return [rkv_loads[i][m].load(rkv[:, i, m, :], p_spill[4 * m + t], *after) for m in range(3)]

            rkv_loaded = {0: load_rkv(0), 1: load_rkv(1)}

            def rwkv_of(t):
                i2 = t % 2
                r_, k_, v_ = [rkv[:, i2, m, :] for m in range(3)]
                if t >= 1:
                    for q in (act, dve):
                        q.wait(pe.last(), act.last(), dve.last(), pool.last())
                r_in, k_in, v_in = rkv_loaded[t]
                t1, t2 = temps[0][1], temps[0][2]
                kr = ts(kkb[:, :], k_, vcol("k_k", t), None, ALU.mult, None, k_in)
                sq = activate(temps[0][0], kkb[:, :], ACT.Square, kr)
                b = take_bank()
                pe.wait(sq)
                mm = pe.done(matmul(bank[b][:, :], const("head_ones"), temps[0][0]))
                inv = inverse_root(t1, t2, b, mm, 1.0, "kk_eps")
                kk_ready = tt(kkb[:, :], kkb[:, :], t1, ALU.mult, inv)
                tokV_ready = transposed(tokV[:, :, :], v_, v_in, act)
                return [direction(t, d, kk_ready, tokV_ready, (r_in, k_in, v_in)) for d in range(2)]

            y_done = {}

            def direction(t, d, kk_ready, tokV_ready, inputs):
                i2 = t % 2
                r_, k_, v_ = [rkv[:, i2, m, :] for m in range(3)]
                kk, ksum = kkb[:, :], ksums[:, i2, :]
                one = bufs[d]
                R, A_, B, K, Bh, Kh = [one[m][:, :] for m in ("R", "A", "B", "K", "Bh", "Kh")]
                tokB, tokK, GA, UW, LT, X, XT, U, Lrb, Lrk = [
                    one[m] for m in ("tokB", "tokK", "GA", "UW", "LT", "X", "XT", "U", "Lrb", "Lrk")]
                MT, N_, St, DC = [one[m] for m in ("MT", "N", "S", "DC")]
                t0, t1, t2, t3 = temps[d]
                w0, a0 = (("w0_f", "a0_f"), ("w0_b", "a0_b"))[d]
                rows = slice(d * HEAD, (d + 1) * HEAD)
                cols = slice(t * P, (t + 1) * P)
                prior = pe.last()
                b = take_bank()
                mm = pe.done(matmul(bank[b][:, :], up_w[rows, 0, cols], wl[rows, :]))
                lw = activate(t0, bank[b][:, :], ACT.Sigmoid, mm, kk_ready, dve.last(), bias=vcol(w0, t))
                free_bank(b, lw)
                b = take_bank()
                mm = pe.done(matmul(bank[b][:, :], up_w[rows, 1, cols], al[rows, :]))
                a_ready = activate(t1, bank[b][:, :], ACT.Sigmoid, mm, bias=vcol(a0, t))
                free_bank(b, a_ready)
                yield
                dve.wait(*inputs)
                pool.wait(*inputs)
                kd = ts(Kh, t1, vcol("k_a", t), omka[:, t:t + 1], ALU.mult, ALU.add, a_ready, prior)
                kd = tt(Kh, Kh, k_, ALU.mult, kd)
                kka = tt(Bh, kk, t1, ALU.mult, kk_ready)
                lw = ts(t0, t0, -float(np.exp(-0.5)), None, ALU.mult, None, lw)
                dve.wait(lw)
                F = dve.done(V.tensor_tensor_scan(t2, rconst("reset"), t0, 0.0, ALU.mult, ALU.add))
                E = tt(t3, t2, t0, ALU.subtract, F)
                ch = lambda ap: ap.rearrange("p (c t) -> p c t", t=CHUNK)
                total = ch(t2)[:, :, CHUNK - 1:CHUNK].to_broadcast([P, 8, CHUNK])
                rest = tt(ch(t0), total, ch(t2), ALU.subtract, E)
                if d == 0:
                    dR, dA, dH, ready = t2, t3, t0, rest
                else:
                    ready = tt(ch(t1), total, ch(t3), ALU.subtract, kka, rest)
                    dR, dA, dH = t1, t0, t3
                pool.wait(kd, shared.get(("ks", t)), prior, tail_done[t - 2] if t >= 2 else None)
                if ("ks", t) not in shared:
                    ks = pool.done(G.tensor_copy(ksum, Kh))
                else:
                    ks = pool.done(G.tensor_tensor(ksum, ksum, Kh, ALU.add))
                shared[("ks", t)] = ks
                dc_ready = activate(DC[:, :], ch(t2)[:, :, CHUNK - 1], ACT.Exp, F, dve.last())
                e = activate(R, dR, ACT.Exp, ready, prior)
                Rr = tt(R, R, r_, ALU.mult, e)
                e = activate(A_, dA, ACT.Exp, prior)
                Ar = stt(A_, A_, -1.0, kk, ALU.mult, ALU.mult, e)
                e = activate(B, dR, ACT.Exp, prior, scale=-1.0)
                Kr = tt(K, B, Kh, ALU.mult, e)
                Br = tt(B, B, Bh, ALU.mult, Kr)
                e = activate(dH, dH, ACT.Exp, dve.last())
                pool.wait(e, Kr, Br, ks)
                Khr = pool.done(G.tensor_tensor(Kh, Kh, dH, ALU.mult))
                Bhr = pool.done(G.tensor_tensor(Bh, Bh, dH, ALU.mult))
                pool.wait(prior)
                for m in (X, XT):
                    for par in range(2):
                        x_init = pool.done(G.tensor_copy(m[:, par, :, :], four(const("ident"))))
                pool.wait(dc_ready)
                dg = pool.done(G.tensor_tensor(
                    MT[:, :, :], rconst("ident2").unsqueeze(1).to_broadcast([P, 8, HEAD]),
                    DC[:, :].unsqueeze(2).to_broadcast([P, 8, HEAD]), ALU.mult))
                yield
                b = take_bank()
                pe.wait(Ar)
                for i in range(4):
                    mm = T.transpose(bank[b][:, i * P:(i + 1) * P], A_[:, i * P:(i + 1) * P], const("ident"))
                mm = pe.done(mm)
                for par in range(2):
                    ga_ready = copy(act, GA[:, par, :, HEAD:P], quad(b)[:, :, par * HEAD:(par + 1) * HEAD],
                                    mm, prior)
                free_bank(b, ga_ready)
                pe.wait(Rr, Ar, Br, Kr)

                def products(lhs, rhs):
                    found = []
                    for par in range(2):
                        b = take_bank()
                        rows = slice(par * HEAD, (par + 1) * HEAD)
                        for i in range(4):
                            c = slice(i * P, (i + 1) * P)
                            mm = matmul(bank[b][:, c], lhs[rows, c], rhs[rows, c])
                        found.append((b, pe.done(mm)))
                    return found

                up, low = (1, 0) if d == 0 else (0, 1)
                x_ready, xt_ready, lt_ready = [None] * 2, [None] * 2, [None] * 2
                for par, (b, mm) in enumerate(products(A_, B)):
                    dve.wait(mm, x_init)
                    x_ready[par] = dve.done(V.copy_predicated(
                        X[:, par, :, :], four(masks[:, low, :]), quad(b)))
                    free_bank(b, x_ready[par])
                for par, (b, mm) in enumerate(products(B, A_)):
                    dve.wait(mm, x_init)
                    xt_ready[par] = dve.done(V.copy_predicated(
                        XT[:, par, :, :], four(masks[:, up, :]), quad(b)))
                    lt_ready[par] = copy(act, LT[:, par, :, :], quad(b), mm, prior, xt_ready[par])
                    free_bank(b, lt_ready[par])
                yield
                lak, lrb, lrk = [None] * 2, [None] * 2, [None] * 2
                for par, (b, mm) in enumerate(products(K, A_)):
                    lak[par] = tt(U[:, par, :, :], quad(b), four(rconst(f"strict{up}")), ALU.mult, mm, prior)
                    free_bank(b, lak[par])
                yield
                b = take_bank()
                for par in range(2):
                    pe.wait(lak[par], tokV_ready)
                    for i in range(4):
                        mm = matmul(bank[b][:, (4 * par + i) * HEAD:(4 * par + i + 1) * HEAD],
                                    U[:, par, i, :], tokV[:, i, par * HEAD:(par + 1) * HEAD])
                mm = pe.done(mm)
                lak_read = mm
                g_ready = copy(act, GA[:, :, :, 0:HEAD],
                               bank[b][:, :].rearrange("p (a t c) -> p a t c", a=2, t=4), mm, prior)
                free_bank(b, g_ready)
                for l in range(1, LEVELS):
                    u_ready = [None] * 2
                    for par in range(2):
                        b = take_bank()
                        pe.wait(lt_ready[par], x_ready[par], xt_ready[par])
                        for i in range(4):
                            mm = matmul(bank[b][:, i * P:(i + 1) * P], LT[:, par, i, :], X[:, par, i, :])
                        mm = pe.done(mm)
                        u_ready[par] = copy(act, U[:, par, :, :], quad(b), mm, lak_read)
                        free_bank(b, u_ready[par])
                    yield
                    if l == 1:
                        for par, (b, mm) in enumerate(products(B, R)):
                            lrb[par] = tt(Lrb[:, par, :, :], quad(b), four(rconst(f"incl{up}")), ALU.mult, mm, prior)
                            free_bank(b, lrb[par])
                    if l == 2:
                        for par, (b, mm) in enumerate(products(K, R)):
                            lrk[par] = tt(Lrk[:, par, :, :], quad(b), four(rconst(f"incl{up}")), ALU.mult, mm, prior)
                            free_bank(b, lrk[par])
                    if l == 3:
                        tokB_ready = transposed(tokB[:, :, :], Bh, Bhr, act, prior)
                    if l == 4:
                        tokK_ready = transposed(tokK[:, :, :], Kh, Khr, act, prior)
                    for par in range(2):
                        pe.wait(u_ready[par])
                        if l < LEVELS - 1:
                            b = take_bank()
                            for i in range(4):
                                mm = matmul(bank[b][:, i * P:(i + 1) * P], XT[:, par, i, :], U[:, par, i, :])
                            mm = pe.done(mm)
                            dve.wait(mm)
                            x_ready[par] = dve.done(V.copy_predicated(
                                X[:, par, :, :], four(masks[:, 2 * l + low, :]), quad(b)))
                            free_bank(b, x_ready[par])
                        b = take_bank()
                        for i in range(4):
                            mm = matmul(bank[b][:, i * P:(i + 1) * P], U[:, par, i, :], XT[:, par, i, :])
                        mm = pe.done(mm)
                        dve.wait(mm)
                        xt_ready[par] = dve.done(V.copy_predicated(
                            XT[:, par, :, :], four(masks[:, 2 * l + up, :]), quad(b)))
                        free_bank(b, xt_ready[par])
                    yield
                uw_ready = [None] * 2
                for par in range(2):
                    b = take_bank()
                    pe.wait(xt_ready[par], g_ready, ga_ready)
                    for i in range(4):
                        mm = matmul(bank[b][:, i * P:(i + 1) * P], XT[:, par, i, :], GA[:, par, i, :])
                    mm = pe.done(mm)
                    uw_ready[par] = copy(act, UW[:, par, :, :], quad(b), mm, prior)
                    free_bank(b, uw_ready[par])
                yield
                pe.wait(*uw_ready, tokB_ready, tokK_ready)
                b_eo = [take_bank(), take_bank()]
                for par in range(2):
                    hc = slice(par * HEAD, (par + 1) * HEAD)
                    for c in range(8):
                        i, rows, b = c // 2, slice((c % 2) * HEAD, (c % 2 + 1) * HEAD), b_eo[c % 2]
                        o = slice(i * HEAD, (i + 1) * HEAD)
                        o2 = slice((4 + i) * HEAD, (5 + i) * HEAD)
                        matmul(bank[b][hc, o], UW[rows, par, i, HEAD:P], tokB[rows, i, hc])
                        matmul(bank[b][hc, o2], tokB[rows, i, hc], UW[rows, par, i, 0:HEAD], True, False)
                        mm = matmul(bank[b][hc, o2], tokK[rows, i, hc], tokV[rows, i, hc], False, True)
                mm = pe.done(mm)
                by2 = lambda ap: ap.rearrange("p (i e) j -> p e i j", e=2)
                for e_ in range(2):
                    b = b_eo[e_]
                    mn = bank[b][:, :].rearrange("p (m c j) -> p m c j", m=2, c=4)
                    mt_ready = tt(by2(MT[:, :, :])[:, e_], by2(MT[:, :, :])[:, e_], mn[:, 0], ALU.add, mm, dg)
                    n_ready = copy(dve, by2(N_[:, :, :])[:, e_], mn[:, 1], mm)
                    free_bank(b, n_ready)
                b = take_bank()
                for par in range(2):
                    pe.wait(lrb[par])
                    for i in range(4):
                        mm = matmul(bank[b][par * HEAD:(par + 1) * HEAD, i * P:(i + 1) * P],
                                    UW[:, par, i, HEAD:P], Lrb[:, par, i, :])
                mm = pe.done(mm)
                z_ready = tt(R, R, bank[b][:, :], ALU.add, mm)
                free_bank(b, z_ready)
                opened = ("open", t) in shared
                if not opened:
                    pe.wait(*bank_free[7])
                    shared[("open", t)] = True
                for par in range(2):
                    hc = slice(par * HEAD, (par + 1) * HEAD)
                    pe.wait(lrk[par])
                    for i in range(4):
                        o = slice(i * P, (i + 1) * P)
                        matmul(bank[7][hc, o], UW[:, par, i, 0:HEAD], Lrb[:, par, i, :],
                               not opened and i == 0, False)
                        mm = matmul(bank[7][hc, o], tokV[:, i, hc], Lrk[:, par, i, :], False, False)
                order = list(range(8)) if d == 0 else list(range(8))[::-1]
                dve.wait(prior)
                s_ready = dve.done(V.memset(St[:, order[0], :], 0.0))
                for step in range(7):
                    yield
                    b = take_bank()
                    c, c_next = order[step], order[step + 1]
                    pe.wait(s_ready, mt_ready)
                    for par in range(2):
                        hc = slice(par * HEAD, (par + 1) * HEAD)
                        mm = matmul(bank[b][hc, 0:HEAD], MT[hc, c, :], St[hc, c, :])
                    mm = pe.done(mm)
                    s_ready = tt(St[:, c_next, :], bank[b][:, 0:HEAD], N_[:, c, :], ALU.add, mm, n_ready)
                    free_bank(b, s_ready)
                yield
                pe.wait(s_ready, z_ready)
                for par in range(2):
                    hc = slice(par * HEAD, (par + 1) * HEAD)
                    for c in range(8):
                        o = slice(c * CHUNK, (c + 1) * CHUNK)
                        mm = matmul(bank[7][hc, o], St[hc, c, :], R[hc, o], False,
                                    t in y_done and c == 7)
                y_done[t] = pe.done(mm)

            def tail_of(t, y_tokens):
                i2 = t % 2
                r_, v_ = rkv[:, i2, 0, :], rkv[:, i2, 2, :]
                ksum = ksums[:, i2, :]
                yt, tz = tail_sb[:, 0, :], tail_sb[:, 1, :]
                yr = copy(act, yt, bank[7][:, :], y_done[t], y_tokens.get("rwkv"), dve.last())
                bank_free[7] = [yr]
                yield
                b = take_bank()
                pe.wait(yr)
                mm = pe.done(matmul(bank[b][:, :], const("head_ones"), yt))
                yc = stt(yt, bank[b][:, :], -1.0 / HEAD, yt, ALU.mult, ALU.add, mm)
                free_bank(b, yc)
                sq = activate(tz, yt, ACT.Square, yc)
                yield
                b = take_bank()
                pe.wait(sq)
                mm = pe.done(matmul(bank[b][:, :], const("head_ones"), tz))
                inv = inverse_root(tz, tz, b, mm, 1.0 / HEAD, "gn_eps")
                yield
                yn = tt(yt, yt, tz, ALU.mult, inv)
                yn = ts(yt, yt, vcol("lnx_g", t), vcol("lnx_b", t), ALU.mult, ALU.add, yn)
                bo = stt(ksum, ksum, vcol("r_k", t), r_, ALU.mult, ALU.mult, shared[("ks", t)])
                yield
                b = take_bank()
                pe.wait(bo)
                mm = pe.done(matmul(bank[b][:, :], const("head_ones"), ksum))
                bo = tt(tz, bank[b][:, :], v_, ALU.mult, mm, yn)
                free_bank(b, bo)
                yn = tt(yt, yt, tz, ALU.add, bo)
                if t + 2 < 4:
                    rkv_loaded[t + 2] = load_rkv(t + 2, bo, pe.last(), pool.last(), act.last())
                tail_done[t] = bo
                yield
                b = take_bank()
                mm = pe.done(matmul(bank[b][:, :], up_w[:, 2, t * P:(t + 1) * P], gl))
                yg = tt(yt, yt, bank[b][:, :], ALU.mult, mm, yn)
                free_bank(b, yg)
                y_tokens["rwkv"] = store.load(y_spill[0, :, t, :], yt, yg)

            return rwkv_of, tail_of

        y_tokens_na = []

        def neighbourhood(ar):
            v = ar.sb("na_v", [P, 4, RW])
            qk = ar.sb("na_qk", [P, 2, S])
            bias = ar.sb("na_bias", [P, 14, GRID_W])
            score = ar.sb("na_score", [P, 4, S])
            pT = ar.sb("na_pT", [P, 4, S])
            stat = ar.sb("na_stat", [P, 4, 4])
            out_t = ar.sb("na_out", [P, S])
            v_ready = Loader(sp, sem("na_v_load")).load(v[:, :, :], p_spill[36:40].rearrange("t p c -> p t c"))
            qk_load = [Loader(sp, sem(f"na_qk_load{c}")) for c in range(2)]
            bias_load = [Loader(sp, sem(f"na_bias{a}")) for a in range(2)]
            store = Loader(sp, sem("yb_store"))
            bias_read, qk_read, stored, pT_read = None, None, None, None
            score_read = [None] * 4
            for t in range(4):
                ready = [qk_load[c].load(qk[:, c, :], p_spill[12 + 4 * c + t], qk_read) for c in range(2)]
                for par in range(2):
                    h = 2 * t + par
                    hc = slice(par * HEAD, (par + 1) * HEAD)
                    loaded = [bias_load[a].load(
                        bias[a * HEAD:(a + 1) * HEAD, :, :],
                        bias_na[h, 1 - a:15 - a, :, :].rearrange("m q k -> q m k"), bias_read) for a in range(2)]
                    pool.wait(*loaded, bias_read)
                    bias_ready = pool.done(G.tensor_tensor(
                        bias[:, :, :], bias[:, :, :],
                        const("na_mask").unsqueeze(1).to_broadcast([P, 14, GRID_W]), ALU.add))
                    yield
                    done_q = []
                    for qt in range(4):
                        pe.wait(*ready)
                        b = take_bank()
                        mm = pe.done(matmul(bank[b][:, :], qk[hc, 0, qt * P:(qt + 1) * P], qk[hc, 1, :]))
                        st = stat[:, qt, :]
                        rows = bias[:, 6 - 2 * qt:14 - 2 * qt, :].rearrange("p m k -> p (m k)")
                        dve.wait(mm, bias_ready, score_read[qt])
                        s1 = dve.done(V.tensor_tensor(score[:, qt, :], bank[b][:, :], rows, ALU.add))
                        free_bank(b, s1)
                        dve.wait(s1)
                        top = dve.done(V.tensor_reduce(st[:, 0:1], score[:, qt, :], AX_X, ALU.max, negate=True))
                        e = activate(score[:, qt, :], score[:, qt, :], ACT.Exp, top, bias=st[:, 0:1],
                                     accum_out=st[:, 1:2])
                        done_q.append(e)
                        if qt % 2:
                            yield
                    bias_read = s1
                    qk_read = pe.last()
                    for qt in range(4):
                        st = stat[:, qt, :]
                        dve.wait(done_q[qt])
                        r = dve.done(V.reciprocal(st[:, 2:3], st[:, 1:2]))
                        r = ts(score[:, qt, :], score[:, qt, :], st[:, 2:3], None, ALU.mult, None, r)
                        done_q[qt] = r
                    yield
                    p_ready = []
                    for k in range(4):
                        b = take_bank()
                        for qt in range(4):
                            pe.wait(done_q[qt])
                            mm = T.transpose(bank[b][:, qt * P:(qt + 1) * P],
                                             score[:, qt, k * P:(k + 1) * P], const("ident"))
                        mm = pe.done(mm)
                        p_ready.append(copy(act, pT[:, k, :], bank[b][:, :], mm, pT_read))
                        free_bank(b, p_ready[k])
                        if k == 1:
                            yield
                    score_read = [mm] * 4
                    yield
                    b_o = take_bank()
                    for k in range(4):
                        pe.wait(p_ready[k], v_ready)
                        mm = matmul(bank[b_o][hc, :], v[:, k, h * HEAD:(h + 1) * HEAD], pT[:, k, :], k == 0, k == 3)
                    pT_read = pe.done(mm)
                    o = copy(act, out_t[hc, :], bank[b_o][hc, :], pT_read, stored)
                    free_bank(b_o, o)
                stored = store.load(y_spill[1, :, t, :], out_t[:, :], o)
            y_tokens_na.append(stored)

        def combine(ya_stored, yb_stored):
            with ExitStack() as ph:
                ar = Arena(nc, ph)
                ends = phase_wait()
                y_sb = ar.sb("mix_y", [P, 2, 4, S])
                y2 = Acts(ar.sb("mix_y_hi", [P, 4, S], F32R), ar.sb("mix_y_lo", [P, 4, S], F32R), 4)
                z_act = Acts(ar.sb("mix_z_hi", [P, KT, S], F32R), ar.sb("mix_z_lo", [P, KT, S], F32R), KT)
                gate = ar.sb("mix_gate", [P, 4, S])
                x_loader = Loader(sp, sem("x_reload"))
                y_loader = [Loader(sp, sem(f"y_reload{i}")) for i in range(2)]
                g_loader = [Loader(sp, sem(f"gate_reload{i}")) for i in range(4)]
                y_loaded = [y_loader[0].load(y_sb[:, 0, :, :], y_spill[0], *ends, ya_stored)]
                gate_read, gate_loaded = {}, {}

                def load_gate(m):
                    gate_loaded[m] = g_loader[m % 4].load(gate[:, m % 4, :], p_spill[20 + m], gate_read.get(m - 4))

                for m in range(4):
                    load_gate(m)
                y_loaded.append(y_loader[1].load(y_sb[:, 1, :, :], y_spill[1], *yb_stored))
                z_part = [None] * KT
                for side, w_name in enumerate(("o_rwkv", "o_na")):
                    for k in range(4):
                        act.wait(y_loaded[side], pe.last())
                        dve.wait(y_loaded[side], pe.last())
                        split_act(y2, k, y_sb[:, side, k, :])
                    for half in range(2):
                        n = take(w_name, half)
                        for c in range(4):
                            j = 4 * half + c
                            m = KT * side + j
                            g = gate[:, m % 4, :]
                            b = take_bank()
                            mm = project(n, 4 * P, c, y2, range(4), b)
                            if side == 0:
                                z = tt(x[:, j, :], g, bank[b][:, :], ALU.mult, mm, gate_loaded[m])
                                z_part[j] = gate_read[m] = z
                                free_bank(b, z)
                            else:
                                z = tt(g, g, bank[b][:, :], ALU.mult, mm, gate_loaded[m])
                                free_bank(b, z)
                                z2 = tt(g, g, x[:, j, :], ALU.add, z, z_part[j])
                                hi, lo = split_act(z_act, j, g, z2)
                                gate_read[m] = lo
                            if m + 4 < 2 * KT:
                                load_gate(m + 4)
                x_back = x_loader.load(x[:, :, :], x_spill, dve.last())
                dve.wait(x_back)
                act.wait(x_back)
                norm_state["xg_last"] = None
                out_projection([("w_out2", 4, 2 * P)], z_act, {"w_out2": range(KT)}, next_norm("norm2_g"))
                norm_end()

        def experts():
            ends = phase_wait()
            with ExitStack() as ph:
                ar = Arena(nc, ph)
                r_col = ar.sb("e_rstd_col", [P, 4])
                rb = ar.sb("e_router_b", [P, 36])
                ec_at, n_ec = _places(_expert_consts())
                ec = ar.sb("e_constants", [P, n_ec])
                wide_raw = ar.sb("e_w_raw", [P, WIDE, UNIT])
                raws = [z[:, :] for z in ring["raw"]] + [wide_raw[:, i, :] for i in range(WIDE)]
                RAWS = len(raws)
                h_row = ar.sb("e_h_row", [P, ROWS_AHEAD, D])
                h_hi, h_lo = ar.sb("e_h_hi", [P, 2, KT, P], F32R), ar.sb("e_h_lo", [P, 2, KT, P], F32R)
                y_row = ar.sb("e_y_row", [P, 2, D])
                he = ar.sb("e_he", [P, 2, D_EXPERT])
                he_hi, he_lo = ar.sb("e_he_hi", [P, 2, 2, P], F32R), ar.sb("e_he_lo", [P, 2, 2, P], F32R)
                small = ar.sb("e_routing", [P, 1408])
                index_tok = ar.sb("e_tokens", [P, 4], U32)
                index = ar.sb("e_index", [P, 8 + BLOCKS + 3 * SPARE], U32)
                at = [0]

                def econst(name):
                    a, n = ec_at[name]
                    return ec[:, a:a + n]

                def piece(*shape):
                    n = int(np.prod(shape))
                    ap = small[:, at[0]:at[0] + n]
                    at[0] += n
                    return ap.rearrange("p (a b) -> p a b", a=shape[0]) if len(shape) > 1 else ap

                ld = Loader(sp, sem("e_loads"))
                ld.load(ec[:, :], econsts, *ends)
                rb_loaded = ld_done = ld.load(rb[:, :], router_b)
                order = []
                for e in range(N_EXPERTS):
                    order.append(e)
                    if e % 4 == 3 and e > 3:
                        order.append(N_EXPERTS + e // 4 - 1)
                units = []
                for k in range(BLOCKS + 1):
                    if k < BLOCKS:
                        units += [(order[k], 0), (order[k], 1)]
                    if k >= 1:
                        units += [(order[k - 1], 2)]
                static_loads = [Loader(sp, sem(f"e_raw_load{i}")) for i in range(RAWS)]
                spare_loads = [Loader(pool, sem(f"e_spare_load{i}")) for i in range(RAWS)]
                e_loaded, e_split, e_done = {}, {}, {}

                def load_expert(m, *after):
                    k, u = units[m]
                    free = e_split.get(m - RAWS, ())
                    if k < N_EXPERTS:
                        row = (3 * k + u) * P
                        e_loaded[m] = static_loads[m % RAWS].load(raws[m % RAWS], expert_rows[row:row + P, :],
                                                                  *free, *after)
                    else:
                        e_loaded[m] = spare_loads[m % RAWS].indirect(
                            raws[m % RAWS], None, expert_rows, w_index[:, k - N_EXPERTS, u:u + 1], *free,
                            bound=3 * P * N_EXPERTS - 1)

                n = take("router", 0)
                for m in range(RAWS):
                    load_expert(m, *unit_split[n], *unit_split[n - 1])
                table = index[:, 8:8 + BLOCKS]
                zeroed = dve.done(V.memset(table, 0))
                tab = Loader(sp, sem("table_zero"))
                cleared = tab.load(slot_table.rearrange("(p b) o -> p (b o)", p=P), table, zeroed)
                ids = index_tok[:, :]
                ids_ready = copy(dve, ids, econst("token"), ld_done)
                b = take_bank()
                mm = project(n, 2 * P, 0, xg, range(KT), b)
                z = scaled_by_rstd(square[:, 0, :], b, mm, square_read[0])
                b = take_bank()
                pe.wait(z)
                for t in range(4):
                    mm = T.transpose(bank[b][:, t * 36:(t + 1) * 36], square[0:36, 0, t * P:(t + 1) * P],
                                     const("ident")[0:36, 0:36])
                mm = pe.done(mm)
                logits = piece(4, 36)
                lg = tt(logits, bank[b][:, 0:4 * 36].rearrange("p (t c) -> p t c", t=4),
                        rb[:, :].unsqueeze(1).to_broadcast([P, 4, 36]), ALU.add, mm, rb_loaded)
                free_bank(b, lg)
                col_ready = rstd_by_token(r_col[:, :])
                gl, el = logits[:, :, 0:4], logits[:, :, 4:36]
                wide = lambda ap, n: ap.to_broadcast([P, 4, n])

                def first_of(dst, values, top, n, seg, ready, tmp_ap):
                    r = tt(dst, values, wide(top, n), ALU.is_equal, ready)
                    dve.wait(r)
                    flat = lambda ap: ap.rearrange("p a b -> p (a b)")
                    r = dve.done(V.tensor_tensor_scan(flat(tmp_ap), const(seg), flat(dst), 0.0, ALU.mult, ALU.add))
                    r = ts(tmp_ap, tmp_ap, 1.0, None, ALU.is_equal, None, r)
                    return tt(dst, dst, tmp_ap, ALU.mult, r)

                def row_of(t, cols):
                    return (y_row if t < 2 else h_row)[:, t % 2, cols]

                tile_read = [pe.last(), None]

                def rows_of_tile(j):
                    i = j % 2
                    g_ = activate(square[:, i, :], x[:, j, :], ACT.Identity, tile_read[i], square_read[i],
                                  scale=vcol("norm2_g", j))
                    b = take_bank()
                    pe.wait(g_)
                    for t in range(4):
                        mm = T.transpose(bank[b][:, t * P:(t + 1) * P], square[:, i, t * P:(t + 1) * P],
                                         const("ident"))
                    tile_read[i] = pe.done(mm)
                    for t in range(4):
                        done = activate(row_of(t, slice(j * P, (j + 1) * P)), bank[b][:, t * P:(t + 1) * P],
                                        ACT.Copy, tile_read[i], col_ready, scale=r_col[:, t:t + 1])
                    free_bank(b, done)
                    return done

                g_top = piece(4, 1)
                dve.wait(lg)
                r = dve.done(V.tensor_reduce(g_top, gl, AX_X, ALU.max))
                g_one, g_tmp = piece(4, 4), piece(4, 4)
                one_r = first_of(g_one, gl, g_top, 4, "seg4", r, g_tmp)
                r = tt(g_tmp, gl, wide(g_top, 4), ALU.subtract, one_r)
                r = activate(g_tmp, g_tmp, ACT.Exp, r)
                for j in range(4):
                    rows_of_tile(j)
                p_group = piece(4, 1)
                dve.wait(r)
                r = dve.done(V.tensor_reduce(p_group, g_tmp, AX_X, ALU.add))
                dve.wait(r)
                pg_r = dve.done(V.reciprocal(p_group, p_group))
                e8, e_tmp = piece(4, 8), piece(4, 8)
                r = None
                for g in range(N_GROUPS):
                    dst = e8 if g == 0 else e_tmp
                    r = tt(dst, el[:, :, 8 * g:8 * g + 8], wide(g_one[:, :, g:g + 1], 8), ALU.mult, r)
                    if g:
                        r = tt(e8, e8, e_tmp, ALU.add, r)
                v1, v2, one1, one2 = piece(4, 1), piece(4, 1), piece(4, 8), piece(4, 8)
                dve.wait(r)
                r = dve.done(V.tensor_reduce(v1, e8, AX_X, ALU.max))
                r = first_of(one1, e8, v1, 8, "seg8", r, e_tmp)
                r = stt(e8, one1, -3e38, e8, ALU.mult, ALU.add, r)
                dve.wait(r)
                r = dve.done(V.tensor_reduce(v2, e8, AX_X, ALU.max))
                r = first_of(one2, e8, v2, 8, "seg8", r, e_tmp)
                w1, w2 = piece(4, 1), piece(4, 1)
                r = tt(w2, v2, v1, ALU.subtract, r)
                r = activate(w2, w2, ACT.Exp, r)
                r = ts(w1, w2, 1.0, None, ALU.add, None, r)
                dve.wait(r)
                r = dve.done(V.reciprocal(w1, w1))
                r = tt(w1, w1, p_group, ALU.mult, r, pg_r)
                r = tt(w2, w2, w1, ALU.mult, r)
                weights_ready = r
                for j in range(4, KT):
                    rows_ready = rows_of_tile(j)
                h_store = Loader(sp, sem("h_rows_store"))
                for t in range(4):
                    h_stored = h_store.load(h_rows[t * P:(t + 1) * P, :], row_of(t, slice(0, D)), rows_ready)

                choice = [piece(4, 32), piece(4, 32)]
                both = piece(4, 32)
                for c, one in enumerate((one1, one2)):
                    for g in range(N_GROUPS):
                        r = tt(choice[c][:, :, 8 * g:8 * g + 8], one, wide(g_one[:, :, g:g + 1], 8), ALU.mult,
                               weights_ready)
                both_ready = tt(both, choice[0], choice[1], ALU.add, r)
                b = take_bank()
                pe.wait(both_ready, ld_done)
                for t in range(4):
                    o = bank[b][:, t * 32:(t + 1) * 32]
                    for u in range(t):
                        matmul(o, const("ones"), both[:, u, :], u == 0, False)
                    matmul(o, econst("before"), both[:, t, :], t == 0, True)
                for t in range(4):
                    mm = matmul(bank[b][:, P:P + 32], const("ones"), both[:, t, :], t == 0, t == 3)
                mm = pe.done(mm)
                rank, quot, beyond, over = piece(4, 32), piece(4, 32), piece(4, 32), piece(4, 32)
                count, blocks, ended, begun = piece(32), piece(32), piece(32), piece(32)
                c1 = copy(dve, count, bank[b][:, P:P + 32], mm)
                c2 = copy(dve, rank, bank[b][:, 0:P].rearrange("p (t e) -> p t e", t=4), mm)
                free_bank(b, c2)
                r = ts(blocks, count, float(P + 1), None, ALU.is_ge, None, c1)
                q = ts(quot, rank, float(P), None, ALU.is_ge, None, c2)
                q = copy(dve, beyond, quot, q)
                for m in range(2, 4):
                    r = stt(blocks, count, float(m * P + 1), blocks, ALU.is_ge, ALU.add, r)
                    q = stt(quot, rank, float(m * P), quot, ALU.is_ge, ALU.add, q)
                dve.wait(r)
                r = dve.done(V.tensor_tensor_scan(ended, econst("one32"), blocks, 0.0, ALU.mult, ALU.add))
                r = tt(begun, ended, blocks, ALU.subtract, r)
                spare_r = tt(begun, begun, econst("above"), ALU.add, r)
                q = stt(rank, quot, -float(P), rank, ALU.mult, ALU.add, q)
                q = tt(quot, quot, begun.unsqueeze(1).to_broadcast([P, 4, 32]), ALU.add, q, spare_r)
                q = tt(quot, quot, beyond, ALU.mult, q)
                q = tt(quot, quot, econst("expert").unsqueeze(1).to_broadcast([P, 4, 32]), ALU.add, q)
                q = stt(rank, rank, float(BLOCKS), quot, ALU.mult, ALU.add, q)
                slot = index[:, 0:8]
                slot_f = piece(2, 4)
                for c in range(2):
                    o = tt(over, choice[c], rank, ALU.mult, q)
                    dve.wait(o)
                    o = dve.done(V.tensor_reduce(slot_f[:, c, :], over, AX_X, ALU.add))
                    q = o
                slot_ready = copy(dve, slot, slot_f.rearrange("p c t -> p (c t)"), q)
                scatter = Loader(pool, sem("table_scatter"))
                pool.wait(cleared, slot_ready, ids_ready)
                for c in range(2):
                    for t in range(4):
                        scattered = scatter.indirect(slot_table, slot[:, 4 * c + t:4 * c + t + 1], ids[:, t:t + 1], None)
                table_ready = tab.load(table, slot_table.rearrange("(p b) o -> p (b o)", p=P), scattered)

                owner = piece(SPARE)
                sq3 = square[:, 0, 0:SPARE * 32].rearrange("p (b e) -> p b e", b=SPARE)
                o = tt(sq3, econst("block").unsqueeze(2).to_broadcast([P, SPARE, 32]),
                       ended.unsqueeze(1).to_broadcast([P, SPARE, 32]), ALU.is_ge, *tile_read, dve.last())
                dve.wait(o)
                o = dve.done(V.tensor_reduce(owner, sq3, AX_X, ALU.add))
                o = ts(owner, owner, 3.0 * P, None, ALU.mult, None, o)
                w_index = index[:, 8 + BLOCKS:8 + BLOCKS + 3 * SPARE].rearrange("p (b u) -> p b u", u=3)
                for u in range(3):
                    w_index_ready = tt(w_index[:, :, u], owner,
                                       econst("row")[:, u:u + 1].to_broadcast([P, SPARE]), ALU.add, o)

                row_loads = [Loader(pool, sem(f"e_row_load{i}")) for i in range(ROWS_AHEAD)]
                y_stores = [Loader(sp, sem(f"e_y_store{i}")) for i in range(2)]
                base = taken[0]
                for q in (pool, act, dve):
                    q.wait(h_stored)
                pool.wait(table_ready, w_index_ready)

                def split_expert(m):
                    r, hi, lo = raws[m % RAWS], ring["hi"][(base + m) % SLOTS], ring["lo"][(base + m) % SLOTS]
                    free = e_done.get(m - SLOTS, unit_done.get(base + m - SLOTS))
                    act.wait(e_loaded[m], free)
                    rounded = act.done(A.activation(hi[:, :], r, ACT.Copy))
                    dve.wait(rounded, free)
                    rest = dve.done(V.tensor_tensor(lo[:, :], r, hi[:, :].bitcast(F32), ALU.subtract))
                    e_split[m] = (rounded, rest)

                row_loaded, row_read = {}, {}

                def load_rows(k):
                    row_loaded[k] = row_loads[k % ROWS_AHEAD].indirect(
                        h_row[:, k % ROWS_AHEAD, :], None, h_rows, table[:, order[k]:order[k] + 1],
                        row_read.get(k - ROWS_AHEAD))

                for k in range(ROWS_AHEAD):
                    load_rows(k)
                next_load, next_split, use = RAWS, 0, 0

                def use_unit():
                    nonlocal next_load, next_split, use
                    while next_split < min(use + SLOTS, len(units)) and (
                            next_split < SLOTS or next_split - SLOTS in e_done):
                        split_expert(next_split)
                        next_split += 1
                        if next_load < len(units):
                            load_expert(next_load)
                            next_load += 1
                    m = use
                    use += 1
                    pe.wait(*e_split[m])
                    s = (base + m) % SLOTS
                    return m, ring["hi"][s], ring["lo"][s]

                hb_read, he_read, y_stored = {}, {}, {}
                he_done, h_ready, he_ready = {}, {}, {}

                def turn_rows(k):
                    i = k % 2
                    pe.wait(row_loaded[k])
                    parts = []
                    for half in range(2):
                        b = take_bank()
                        for c in range(4):
                            kt = 4 * half + c
                            mm = T.transpose(bank[b][:, c * P:(c + 1) * P], h_row[:, k % ROWS_AHEAD, kt * P:(kt + 1) * P],
                                             const("ident"))
                        mm = pe.done(mm)
                        src = bank[b][:, :].rearrange("p (k c) -> p k c", k=4)
                        dst = slice(4 * half, 4 * half + 4)
                        act.wait(mm, hb_read.get(k - 2))
                        a1 = act.done(A.activation(h_hi[:, i, dst, :], src, ACT.Copy))
                        d1 = tt(h_lo[:, i, dst, :], src, h_hi[:, i, dst, :].bitcast(F32), ALU.subtract, a1,
                                hb_read.get(k - 2))
                        free_bank(b, d1)
                        parts.append((a1, d1))
                    row_read[k] = mm
                    if k + ROWS_AHEAD < BLOCKS:
                        load_rows(k + ROWS_AHEAD)
                    h_ready[k] = parts

                def gate_up(k):
                    i, parts = k % 2, h_ready[k]
                    b = take_bank()
                    for half in range(2):
                        m, hi, lo = use_unit()
                        pe.wait(*parts[half])
                        w = [z[:, :].rearrange("p (k c) -> p k c", k=4) for z in (hi, lo)]
                        for c in range(4):
                            kt = 4 * half + c
                            first, last = kt == 0, kt == KT - 1
                            matmul(bank[b][:, :], h_hi[:, i, kt, :], w[0][:, c, :], first, False)
                            matmul(bank[b][:, :], h_hi[:, i, kt, :], w[1][:, c, :], False, False)
                            mm = matmul(bank[b][:, :], h_lo[:, i, kt, :], w[0][:, c, :], False, last)
                        e_done[m] = pe.done(mm)
                    hb_read[k] = e_done[m]
                    sil = activate(he[:, i, :], bank[b][:, 0:D_EXPERT], ACT.Silu, e_done[m], he_read.get(k - 2))
                    r = tt(he[:, i, :], he[:, i, :], bank[b][:, D_EXPERT:], ALU.mult, sil)
                    free_bank(b, r)
                    he_done[k] = r

                def turn_he(k):
                    i = k % 2
                    b = take_bank()
                    pe.wait(he_done[k])
                    for c in range(2):
                        mm = T.transpose(bank[b][:, c * P:(c + 1) * P], he[:, i, c * P:(c + 1) * P], const("ident"))
                    he_read[k] = pe.done(mm)
                    src = bank[b][:, 0:2 * P].rearrange("p (k c) -> p k c", k=2)
                    a1 = activate(he_hi[:, i, :, :], src, ACT.Copy, he_read[k])
                    d1 = tt(he_lo[:, i, :, :], src, he_hi[:, i, :, :].bitcast(F32), ALU.subtract, a1)
                    free_bank(b, d1)
                    he_ready[k] = (a1, d1)

                def down(k):
                    i = k % 2
                    m, hi, lo = use_unit()
                    pe.wait(*he_ready[k])
                    w = [z[:, :].rearrange("p (k c) -> p k c", k=2) for z in (hi, lo)]
                    copied = []
                    for half in range(2):
                        b = take_bank()
                        cols = slice(half * S, (half + 1) * S)
                        for c in range(2):
                            matmul(bank[b][:, :], he_hi[:, i, c, :], w[0][:, c, cols], c == 0, False)
                            matmul(bank[b][:, :], he_hi[:, i, c, :], w[1][:, c, cols], False, False)
                            mm = matmul(bank[b][:, :], he_lo[:, i, c, :], w[0][:, c, cols], False, c == 1)
                        mm = pe.done(mm)
                        q_ = copy((act, dve)[half], y_row[:, i, cols], bank[b][:, :], mm, y_stored.get(k - 2))
                        free_bank(b, q_)
                        copied.append(q_)
                    e_done[m] = mm
                    y_stored[k] = y_stores[i].load(
                        y_rows.rearrange("(p b) d -> p b d", b=BLOCKS)[:, order[k], :], y_row[:, i, :], *copied)

                turn_rows(0)
                for k in range(BLOCKS + 1):
                    if k < BLOCKS:
                        gate_up(k)
                    if k + 1 < BLOCKS:
                        turn_rows(k + 1)
                    if k >= 1:
                        down(k - 1)
                    if k < BLOCKS:
                        turn_he(k)

                pool.wait(y_stored[BLOCKS - 1], y_stored[BLOCKS - 2], act.last(), dve.last())
                gathered = [Loader(pool, sem(f"e_gather{t}")) for t in range(4)]
                got = []
                for t in range(4):
                    for c in range(2):
                        token = gathered[t].indirect(raws[t][:, c * D:(c + 1) * D], None, y_rows,
                                                     slot[:, 4 * c + t:4 * c + t + 1])
                    got.append(token)
                out_load = [Loader(sp, sem(f"out_store{i}")) for i in range(2)]
                stored = [y_stored[BLOCKS - 2], y_stored[BLOCKS - 1]] if BLOCKS % 2 == 0 else \
                    [y_stored[BLOCKS - 1], y_stored[BLOCKS - 2]]
                for t in range(4):
                    i = t % 2
                    for half in range(2):
                        b = take_bank()
                        for c in range(4):
                            mm = T.transpose(bank[b][:, c * P:(c + 1) * P], x[:, 4 * half + c, t * P:(t + 1) * P],
                                             const("ident"))
                        mm = pe.done(mm)
                        cols = slice(half * S, (half + 1) * S)
                        r = stt(y_row[:, i, cols], raws[t][:, cols], w1[:, t, :], bank[b][:, :], ALU.mult,
                                ALU.add, mm, got[t], stored[i], weights_ready)
                        free_bank(b, r)
                        r = stt(y_row[:, i, cols], raws[t][:, D + half * S:D + (half + 1) * S], w2[:, t, :],
                                y_row[:, i, cols], ALU.mult, ALU.add, r)
                    stored[i] = out_load[i].load(out[t * P:(t + 1) * P, :], y_row[:, i, :], r)
                sp.wait(*stored)


        mixer()
        cross_attention(0)
        conv_ffn(0, "c_norm")
        conformer()
        cross_attention(1)
        conv_ffn(1, None)
        final_norm()
        p_stored = second_projections()
        ring["stack"].close()
        ya_stored, yb_stored = mixers(p_stored)
        ends = phase_wait()
        open_ring("_2", len(plan))
        xg.hi, xg.lo = ring["xg"]
        for n in range(mixers_at, mixers_at + RAW):
            load_unit(n, *ends)
        for q in (act, dve):
            q.wait(*ends, pool.last())
        combine(ya_stored, yb_stored)
        experts()
        ring["stack"].close()


def _unit_arrays(inp):
    def pack(w, cols):
        k, n = w.shape
        return w.reshape(k // P, P, n // cols, cols).transpose(2, 1, 0, 3).reshape(n // cols, P, -1)

    def pairs(a, b):
        k, n = a.shape
        return np.concatenate([a.reshape(k, n // P, P), b.reshape(k, n // P, P)], axis=2).reshape(k, 2 * n)

    w = {}
    w_in = inp["ab_w_in"][0]
    w["ab_in"] = pack(pairs(w_in[:, 0:D], w_in[:, D:2 * D]), 2 * P)
    w["pool_in"] = pack(w_in[:, 2 * D:], 2 * P)
    w["ab_out_a"] = pack(inp["ab_w_out"][0][0:D], 2 * P)
    w["ab_out_b"] = pack(inp["ab_w_out"][0][D:], 4 * P)
    w["pw1"] = pack(pairs(inp["c_w_pw1"][0][:, 0:D], inp["c_w_pw1"][0][:, D:]), 2 * P)
    w["pw2"] = pack(inp["c_w_pw2"][0], 2 * P)
    for l in range(DEPTH):
        for m in "kvqo":
            w[f"w{m}{l}"] = pack(inp[f"xa_w{m}"][l], 2 * P)
        up = inp["f_w_up"][l]
        w[f"up{l}"] = pack(pairs(up[:, 0:D_FF], up[:, D_FF:]), 2 * P)
        w[f"down{l}"] = np.concatenate([pack(inp["f_w_down"][l][p * D:(p + 1) * D], 2 * P) for p in range(3)])
    w2 = inp["w_in_2"][0]
    r_, k_, v_ = (w2[:, i * RW:(i + 1) * RW] for i in range(3))
    lora = w2[:, 3 * RW:3 * RW + 384]
    zero = np.zeros((D, P), np.float32)
    w["lora"] = pack(np.concatenate([lora, zero], axis=1), 2 * P)
    w["rkvg"] = pack(np.concatenate([np.concatenate([m[:, t * P:(t + 1) * P] for m in (r_, k_, v_)] + [zero], axis=1)
                                     for t in range(4)], axis=1), 2 * P)
    base = 3 * RW + 384
    q2, k2, v2 = (w2[:, base + i * RW:base + (i + 1) * RW] for i in range(3))
    w["na_v"] = pack(v2, 2 * P)
    w["na_qk"] = pack(pairs(q2, k2), 2 * P)
    gates = w2[:, base + 3 * RW:]
    w["gate_a"], w["gate_b"] = pack(gates[:, 0:D], 2 * P), pack(gates[:, D:], 2 * P)
    w["o_rwkv"], w["o_na"] = pack(inp["w_o_rwkv_2"][0], 4 * P), pack(inp["w_o_na_2"][0], 4 * P)
    w["w_out2"] = pack(inp["w_out_2"][0], 2 * P)
    router = np.concatenate([inp["w_router_group_2"][0], inp["w_router_expert_2"][0],
                             np.zeros((D, 2 * P - 36), np.float32)], axis=1)
    w["router"] = pack(router, 2 * P)
    return np.stack([w[name][i] for name, i in _plan()])


def _expert_rows(inp):
    gate_up = np.concatenate([inp["w_gate_e_2"][0], inp["w_up_e_2"][0]], axis=2)
    gate_up = gate_up.reshape(N_EXPERTS, 2, 4, P, S).transpose(0, 1, 3, 2, 4).reshape(N_EXPERTS, 2, P, UNIT)
    down = inp["w_down_e_2"][0].reshape(N_EXPERTS, 1, 2, P, D).transpose(0, 1, 3, 2, 4).reshape(N_EXPERTS, 1, P, UNIT)
    return np.concatenate([gate_up, down], axis=1).reshape(-1, UNIT)


def _channel_major(a):
    t, c = a.shape
    return np.ascontiguousarray(a.T.reshape(c // P, P, t).transpose(1, 0, 2))


def kernel(**inputs):
    import concourse.bacc as bacc
    from concourse.bass_utils import run_bass_kernel_spmd

    inp = {k: np.asarray(v) for k, v in inputs.items()}
    cols = []
    for _, name, layer in _vector_names():
        a = inp[name] if layer is None else inp[name][layer]
        cols.append(a.reshape(-1, P).T)
    for name, layer in (("a_conv_w", 0), ("c_dw_w", 0), ("f_dw_w", 0), ("f_dw_w", 1)):
        a = inp[name][layer]
        taps, width = a.shape
        cols.append(a.reshape(taps, width // P, P).transpose(2, 1, 0).reshape(P, -1))
    for name in ("q_gain_2", "k_gain_2"):
        cols.append(np.tile(inp[name][0], 2).reshape(P, 1))
    rpb = np.pad(inp["rpb_2"][0], ((0, 0), (0, 0), (48, 48)))
    bias = np.stack([rpb[:, :, 63 - q:127 - q] for q in range(GRID_W)], axis=2)
    lora = np.stack([np.concatenate([inp["w_up_f_2"][0], inp["w_up_b_2"][0]]),
                     np.concatenate([inp["a_up_f_2"][0], inp["a_up_b_2"][0]]), inp["g_up_2"][0]], axis=1)
    arrays = {
        "stream": _unit_arrays(inp),
        "vectors": np.concatenate(cols, axis=1),
        "consts": np.concatenate(list(_consts().values()), axis=1),
        "rconsts": np.concatenate(list(_rwkv_consts().values()), axis=1),
        "x_in": _channel_major(inp["x"][0]),
        "mem_in": _channel_major(inp["mem"][0]),
        "gates_w": np.stack([inp["a_gate_x_w"][0], inp["a_gate_a_w"][0]], axis=1).transpose(2, 0, 1, 3),
        "group_w": inp["b_group_w"][0].transpose(1, 0, 2),
        "lora_w": lora,
        "router_b": np.broadcast_to(np.concatenate([inp["b_router_group_2"][0], inp["b_router_expert_2"][0]]),
                                    (P, 36)),
        "bias_na": bias,
        "level_masks": _level_masks(),
        "expert_rows": _expert_rows(inp),
        "econsts": np.concatenate(list(_expert_consts().values()), axis=1),
    }
    arrays = {k: np.ascontiguousarray(v) for k, v in arrays.items()}
    nc = bacc.Bacc("TRN2", target_bir_lowering=False, num_devices=1)
    args = [nc.dram_tensor(k, v.shape, mybir.dt.from_np(v.dtype), kind="ExternalInput").ap()
            for k, v in arrays.items()]
    out = nc.dram_tensor("out", (S, D), F32, kind="ExternalOutput").ap()
    spill = nc.dram_tensor("x_spill", (P, KT, S), F32, kind="Internal").ap()
    y_spill = nc.dram_tensor("y_spill", (2, P, 4, S), F32, kind="Internal").ap()
    p_spill = nc.dram_tensor("p_spill", (40, P, S), F32, kind="Internal").ap()
    h_rows = nc.dram_tensor("h_rows", (S, D), F32, kind="Internal").ap()
    y_rows = nc.dram_tensor("y_rows", (P * BLOCKS, D), F32, kind="Internal").ap()
    slot_table = nc.dram_tensor("slot_table", (P * BLOCKS, 1), U32, kind="Internal").ap()
    build(nc, *args, out, spill, y_spill, p_spill, h_rows, y_rows, slot_table)
    r = run_bass_kernel_spmd(nc, [arrays], core_ids=[0])
    return np.asarray(r.results[0]["out"])[None]
```
